# Optimizing a Trainium2 kernel written in Bass

```python
import math
import jax, jax.numpy as jnp
from jax import lax
import numpy as np

D_MODEL = 1024
BATCH = 1
SEQ = 512
DEPTH = 1

GRID_W = 64
CTX_LEN = 256
HEAD_DIM = 64
NA_HEADS = 8
NA_WIDTH = NA_HEADS * HEAD_DIM
NA_WIN_H = 8
NA_WIN_W = 16
HY_WIDTH = D_MODEL // 2
HY_ORDER = 2
HY_SHORT = 3
HY_EMB = 33
HY_BANDS = (HY_EMB - 1) // 2
HY_FFN = 64
HY_FAST_DECAY = 0.3
HY_SLOW_DECAY = 1.5
HY_TARGET = 1e-2
HY_FILTER_SCALE = 0.008
HY_PROJ = (HY_ORDER + 1) * HY_WIDTH
FFN_HIDDEN = -(-(8 * D_MODEL) // (3 * 256)) * 256
N_MOD = 6
ROPE_THETA = 10000.0
RMS_EPS = 1e-6
NEG_INF = -1e30
IN_SPLITS = (NA_WIDTH, 2 * NA_WIDTH, 3 * NA_WIDTH, 3 * NA_WIDTH + HY_WIDTH,
             3 * NA_WIDTH + 2 * HY_WIDTH, 3 * NA_WIDTH + HY_PROJ, 3 * NA_WIDTH + HY_PROJ + D_MODEL)
IN_WIDTH = 3 * NA_WIDTH + HY_PROJ + 2 * D_MODEL


def rmsnorm(x, g):
    xf = x.astype(jnp.float32)
    y = xf * lax.rsqrt(jnp.mean(xf * xf, axis=-1, keepdims=True) + RMS_EPS)
    return (y * g.astype(jnp.float32)).astype(x.dtype)

def modulate(h, shift, scale):
    return h * (1 + scale) + shift

def to_heads(a):
    B, L, _ = a.shape
    return a.reshape(B, L, NA_HEADS, HEAD_DIM)

def axial_rope(x, rows, cols):
    nf = HEAD_DIM // 4
    inv = ROPE_THETA ** (-jnp.arange(nf, dtype=jnp.float32) / nf)

    def rot(xp, pos):
        ang = pos.astype(jnp.float32)[:, None] * inv
        cos = jnp.cos(ang)[None, :, None, :]
        sin = jnp.sin(ang)[None, :, None, :]
        x1 = xp[..., :nf].astype(jnp.float32)
        x2 = xp[..., nf:].astype(jnp.float32)
        return jnp.concatenate([x1 * cos - x2 * sin, x2 * cos + x1 * sin], axis=-1)

    half = HEAD_DIM // 2
    return jnp.concatenate([rot(x[..., :half], rows), rot(x[..., half:], cols)], axis=-1).astype(x.dtype)

def neighbourhood_attention(q, k, v, k_ctx, v_ctx, rpb):
    B, L, H, Dh = q.shape
    R = L // GRID_W
    wh = min(NA_WIN_H, R)
    scale = Dh ** -0.5
    t = jnp.arange(L)
    rows, cols = t // GRID_W, t % GRID_W
    q_rot = axial_rope(q, rows, cols)
    k_rot = axial_rope(k, rows, cols)

    def grid(a):
        return a.reshape(B, R, GRID_W, H, Dh)

    r = jnp.arange(R)
    row_idx = jnp.clip(r - wh // 2, 0, R - wh)[:, None] + jnp.arange(wh)[None, :]
    k_band = grid(k_rot)[:, row_idx]
    v_band = grid(v)[:, row_idx]
    cq = jnp.arange(GRID_W)
    start_c = jnp.clip(cq - NA_WIN_W // 2, 0, GRID_W - NA_WIN_W)
    col_ok = (cq[None, :] >= start_c[:, None]) & (cq[None, :] < start_c[:, None] + NA_WIN_W)
    roff = row_idx - r[:, None] + (NA_WIN_H - 1)
    coff = jnp.clip(cq[None, :] - cq[:, None], -(NA_WIN_W - 1), NA_WIN_W - 1) + (NA_WIN_W - 1)
    bias = rpb.astype(jnp.float32)[:, roff[:, None, :, None], coff[None, :, None, :]]
    s_nb = jnp.einsum('brqhd,brikhd->bhrqik', grid(q_rot), k_band,
                      preferred_element_type=jnp.float32) * scale + bias[None]
    s_nb = jnp.where(col_ok[:, None, :], s_nb, NEG_INF)
    s_ctx = jnp.einsum('brqhd,bchd->bhrqc', grid(q), k_ctx, preferred_element_type=jnp.float32) * scale
    s = jnp.concatenate([s_nb.reshape(B, H, R, GRID_W, wh * GRID_W), s_ctx], axis=-1)
    p = jax.nn.softmax(s, axis=-1).astype(v.dtype)
    p_nb = p[..., :wh * GRID_W].reshape(B, H, R, GRID_W, wh, GRID_W)
    p_ctx = p[..., wh * GRID_W:]
    o = (jnp.einsum('bhrqik,brikhd->brqhd', p_nb, v_band)
         + jnp.einsum('bhrqc,bchd->brqhd', p_ctx, v_ctx))
    return o.reshape(B, L, H * Dh)

def context_attention(q, k, v):
    B, Lc, H, Dh = q.shape
    s = jnp.einsum('bqhd,bkhd->bhqk', q, k, preferred_element_type=jnp.float32) * (Dh ** -0.5)
    p = jax.nn.softmax(s, axis=-1).astype(v.dtype)
    return jnp.einsum('bhqk,bkhd->bqhd', p, v).reshape(B, Lc, H * Dh)

def short_conv(u, w, b):
    up = jnp.pad(u, ((0, 0), (1, 1), (0, 0)))
    return up[:, :-2] * w[0] + up[:, 1:-1] * w[1] + up[:, 2:] * w[2] + b

def hyena_filters(L, w1, b1, w2, b2, freq, w3):
    f32 = jnp.float32
    t = jnp.linspace(0.0, 1.0, L, dtype=f32)[:, None]
    w = 2.0 * math.pi * jnp.arange(L, dtype=f32)[:, None] / L
    bands = jnp.linspace(1e-4, HY_BANDS - 1, HY_BANDS, dtype=f32)
    z = jnp.concatenate([t, jnp.cos(bands * w), jnp.sin(-bands * w)], axis=-1)
    fr = freq.astype(f32)
    hid = jnp.sin(fr * (z @ w1.astype(f32) + b1.astype(f32)))
    hid = jnp.sin(fr * (hid @ w2.astype(f32) + b2.astype(f32)))
    h = (hid @ w3.astype(f32)).reshape(L, 2, HY_ORDER, HY_WIDTH)
    min_decay = math.log(HY_TARGET) / HY_SLOW_DECAY
    max_decay = math.log(HY_TARGET) / HY_FAST_DECAY
    deltas = jnp.abs(jnp.linspace(min_decay, max_decay, HY_WIDTH, dtype=f32))
    decay = jnp.exp(-t * deltas)
    return h * decay[:, None, None, :]

def long_conv_bidir(u, h_fwd, h_bwd, bias):
    B, L, C = u.shape
    k2 = jnp.concatenate([h_fwd, jnp.zeros((1, C), jnp.float32), h_bwd[:0:-1]], axis=0)
    U = jnp.fft.rfft(u.astype(jnp.float32), n=2 * L, axis=1)
    K = jnp.fft.rfft(k2, n=2 * L, axis=0)
    y = jnp.fft.irfft(U * K[None], n=2 * L, axis=1)[:, :L]
    return (y + u.astype(jnp.float32) * bias.astype(jnp.float32)).astype(u.dtype)

def hyena_mixer(hv, hx1, hx2, conv_w, conv_b, w1, b1, w2, b2, freq, w3, bias):
    u = short_conv(jnp.concatenate([hv, hx1, hx2], axis=-1), conv_w, conv_b)
    parts = jnp.split(u, HY_ORDER + 1, axis=-1)
    z, gates = parts[0], parts[1:]
    filt = hyena_filters(z.shape[1], w1, b1, w2, b2, freq, w3)
    for n in range(HY_ORDER):
        z = gates[n] * long_conv_bidir(z, filt[:, 0, n], filt[:, 1, n], bias[n])
    return z

def gated_merge(g_na, g_hy, y_na, y_hy, w_na_o, w_hy_o, w_out):
    m = jax.nn.sigmoid(g_na) * (y_na @ w_na_o) + jax.nn.sigmoid(g_hy) * (y_hy @ w_hy_o)
    return m @ w_out

def swiglu(h, w1, w3, w2):
    return (jax.nn.silu(h @ w1) * (h @ w3)) @ w2

def first_inputs(seed: int = 0) -> dict:
    key = jax.random.key(seed)
    ks = jax.random.split(key, 32)
    f32 = jnp.float32

    def nrm(k, shape, scale):
        return jax.random.normal(k, shape, f32) * scale

    return {
        'x': nrm(ks[0], (BATCH, SEQ, D_MODEL), 1.0),
        'c': nrm(ks[1], (BATCH, D_MODEL), 1.0),
        'ctx': nrm(ks[2], (BATCH, CTX_LEN, D_MODEL), 1.0),
        'c_ctx': nrm(ks[3], (D_MODEL,), 1.0),
        'w_ada': nrm(ks[4], (DEPTH, D_MODEL, N_MOD * D_MODEL), D_MODEL ** -0.5),
        'b_ada': nrm(ks[5], (DEPTH, N_MOD * D_MODEL), 0.02),
        'norm1_g': 1.0 + nrm(ks[6], (DEPTH, D_MODEL), 0.02),
        'norm2_g': 1.0 + nrm(ks[7], (DEPTH, D_MODEL), 0.02),
        'w_in': nrm(ks[8], (DEPTH, D_MODEL, IN_WIDTH), D_MODEL ** -0.5),
        'na_rpb': nrm(ks[9], (DEPTH, NA_HEADS, 2 * NA_WIN_H - 1, 2 * NA_WIN_W - 1), 0.1),
        'hy_conv_w': nrm(ks[10], (DEPTH, HY_SHORT, HY_PROJ), HY_SHORT ** -0.5),
        'hy_conv_b': nrm(ks[11], (DEPTH, HY_PROJ), 0.02),
        'hy_ffn_w1': nrm(ks[12], (DEPTH, HY_EMB, HY_FFN), HY_EMB ** -0.5),
        'hy_ffn_b1': nrm(ks[13], (DEPTH, HY_FFN), 0.1),
        'hy_ffn_w2': nrm(ks[14], (DEPTH, HY_FFN, HY_FFN), HY_FFN ** -0.5),
        'hy_ffn_b2': nrm(ks[15], (DEPTH, HY_FFN), 0.1),
        'hy_sin_freq': 1.0 + nrm(ks[16], (DEPTH, HY_FFN), 0.05),
        'hy_ffn_w3': nrm(ks[17], (DEPTH, HY_FFN, 2 * HY_ORDER * HY_WIDTH), HY_FILTER_SCALE),
        'hy_bias': nrm(ks[18], (DEPTH, HY_ORDER, HY_WIDTH), 0.2),
        'w_na_o': nrm(ks[19], (DEPTH, NA_WIDTH, D_MODEL), NA_WIDTH ** -0.5),
        'w_hy_o': nrm(ks[20], (DEPTH, HY_WIDTH, D_MODEL), HY_WIDTH ** -0.5),
        'w_out': nrm(ks[21], (DEPTH, D_MODEL, D_MODEL), D_MODEL ** -0.5),
        'ffn_w1': nrm(ks[22], (DEPTH, D_MODEL, FFN_HIDDEN), D_MODEL ** -0.5),
        'ffn_w3': nrm(ks[23], (DEPTH, D_MODEL, FFN_HIDDEN), D_MODEL ** -0.5),
        'ffn_w2': nrm(ks[24], (DEPTH, FFN_HIDDEN, D_MODEL), FFN_HIDDEN ** -0.5),
        'final_g': 1.0 + nrm(ks[25], (D_MODEL,), 0.02),
    }

def first_block(x, c, ctx, c_ctx, w_ada, b_ada, norm1_g, norm2_g, w_in, na_rpb, hy_conv_w, hy_conv_b,
              hy_ffn_w1, hy_ffn_b1, hy_ffn_w2, hy_ffn_b2, hy_sin_freq, hy_ffn_w3, hy_bias,
              w_na_o, w_hy_o, w_out, ffn_w1, ffn_w3, ffn_w2, final_g):
    xc = ctx
    for i in range(DEPTH):
        last = i == DEPTH - 1
        mod = jax.nn.silu(c) @ w_ada[i] + b_ada[i]
        mod_c = jax.nn.silu(c_ctx) @ w_ada[i] + b_ada[i]
        sh1, sc1, g1, sh2, sc2, g2 = jnp.split(mod[:, None, :], N_MOD, axis=-1)
        csh1, csc1, cg1, csh2, csc2, cg2 = jnp.split(mod_c, N_MOD, axis=-1)
        hy_params = (hy_conv_w[i], hy_conv_b[i], hy_ffn_w1[i], hy_ffn_b1[i], hy_ffn_w2[i], hy_ffn_b2[i],
                     hy_sin_freq[i], hy_ffn_w3[i], hy_bias[i])

        hc = modulate(rmsnorm(xc, norm1_g[i]), csh1, csc1)
        if last:
            k_c, v_c = jnp.split(hc @ w_in[i][:, NA_WIDTH:3 * NA_WIDTH], 2, axis=-1)
        else:
            q_c, k_c, v_c, hv_c, hx1_c, hx2_c, gna_c, ghy_c = jnp.split(hc @ w_in[i], IN_SPLITS, axis=-1)
            y_na_c = context_attention(to_heads(q_c), to_heads(k_c), to_heads(v_c))
            y_hy_c = hyena_mixer(hv_c, hx1_c, hx2_c, *hy_params)
            xc_next = xc + cg1 * gated_merge(gna_c, ghy_c, y_na_c, y_hy_c, w_na_o[i], w_hy_o[i], w_out[i])
            hc2 = modulate(rmsnorm(xc_next, norm2_g[i]), csh2, csc2)
            xc_next = xc_next + cg2 * swiglu(hc2, ffn_w1[i], ffn_w3[i], ffn_w2[i])

        h = modulate(rmsnorm(x, norm1_g[i]), sh1, sc1)
        q, k, v, hv, hx1, hx2, gna, ghy = jnp.split(h @ w_in[i], IN_SPLITS, axis=-1)
        y_na = neighbourhood_attention(to_heads(q), to_heads(k), to_heads(v),
                                       to_heads(k_c), to_heads(v_c), na_rpb[i])
        y_hy = hyena_mixer(hv, hx1, hx2, *hy_params)
        x = x + g1 * gated_merge(gna, ghy, y_na, y_hy, w_na_o[i], w_hy_o[i], w_out[i])
        h2 = modulate(rmsnorm(x, norm2_g[i]), sh2, sc2)
        x = x + g2 * swiglu(h2, ffn_w1[i], ffn_w3[i], ffn_w2[i])
        if not last:
            xc = xc_next
    return rmsnorm(x, final_g)


MEM_LEN = 256
EPS = 1e-6
MLA_HEADS = 8
Q_LORA = 384
KV_LORA = 256
D_NOPE = 64
D_ROPE = 32
D_QK = D_NOPE + D_ROPE
D_V = 64
MLA_WIDTH = MLA_HEADS * D_V
Q_BLOCK = 128
SSM_GROUPS = 32
SSM_GROUP_CH = 16
SSM_WIDTH = SSM_GROUPS * SSM_GROUP_CH
SSM_STATE = 64
DT_MIN = 1e-3
DT_MAX = 1e-1
X_HEADS = 4
X_HEAD_DIM = 128
X_WIDTH = X_HEADS * X_HEAD_DIM
N_BRANCH = 3
D_FF = 2816
CONV_WIDTH = 3
IN_WIDTH_2 = Q_LORA + KV_LORA + D_ROPE + SSM_WIDTH + X_WIDTH + N_BRANCH * D_MODEL


def rmsnorm_2(x, g):
    xf = x.astype(jnp.float32)
    y = xf * lax.rsqrt(jnp.mean(xf * xf, axis=-1, keepdims=True) + EPS)
    return (y * g.astype(jnp.float32)).astype(x.dtype)

def rope_tables(positions):
    inv_freq = ROPE_THETA ** (-jnp.arange(0, D_ROPE, 2, dtype=jnp.float32) / D_ROPE)
    ang = positions.astype(jnp.float32)[..., None] * inv_freq
    return jnp.cos(ang), jnp.sin(ang)

def apply_rope(x, cos, sin):
    xf = x.astype(jnp.float32)
    x1, x2 = jnp.split(xf, 2, axis=-1)
    return jnp.concatenate([x1 * cos - x2 * sin, x1 * sin + x2 * cos], axis=-1).astype(x.dtype)

def split_combined(proj):
    sizes = (Q_LORA, KV_LORA, D_ROPE, SSM_WIDTH, X_WIDTH)
    idx = [int(v) for v in np.cumsum(sizes)]
    return jnp.split(proj, idx, axis=-1)

def causal_block_attention(q, k, v):
    b, l, h, dq = q.shape
    nb = l // Q_BLOCK
    scale = dq ** -0.5
    qb = jnp.moveaxis(q.reshape(b, nb, Q_BLOCK, h, dq), 1, 0)
    kpos = jnp.arange(l)

    def one_block(args):
        i, qi = args
        s = jnp.einsum('bqhd,bkhd->bhqk', qi, k, preferred_element_type=jnp.float32) * scale
        qpos = i * Q_BLOCK + jnp.arange(Q_BLOCK)
        s = jnp.where(kpos[None, :] <= qpos[:, None], s, -jnp.inf)
        p = jax.nn.softmax(s, axis=-1)
        return jnp.einsum('bhqk,bkhd->bqhd', p.astype(v.dtype), v)

    out = lax.map(one_block, (jnp.arange(nb), qb))
    return jnp.moveaxis(out, 0, 1).reshape(b, l, h * v.shape[-1])

def mla_branch(c_q, c_kv, k_r, cos, sin, q_a_norm_g, w_q_b, kv_a_norm_g, w_kv_b, q_norm_g, k_norm_g):
    b, l, _ = c_q.shape
    q = (rmsnorm_2(c_q, q_a_norm_g) @ w_q_b).reshape(b, l, MLA_HEADS, D_QK)
    kv = (rmsnorm_2(c_kv, kv_a_norm_g) @ w_kv_b).reshape(b, l, MLA_HEADS, D_NOPE + D_V)
    k_nope, v = kv[..., :D_NOPE], kv[..., D_NOPE:]
    k_rope = jnp.broadcast_to(k_r[:, :, None, :], (b, l, MLA_HEADS, D_ROPE))
    k = jnp.concatenate([k_nope, k_rope], axis=-1)
    q = rmsnorm_2(q, q_norm_g)
    k = rmsnorm_2(k, k_norm_g)
    c4, s4 = cos[:, :, None, :], sin[:, :, None, :]
    q = jnp.concatenate([q[..., :D_NOPE], apply_rope(q[..., D_NOPE:], c4, s4)], axis=-1)
    k = jnp.concatenate([k[..., :D_NOPE], apply_rope(k[..., D_NOPE:], c4, s4)], axis=-1)
    return causal_block_attention(q, k, v)

def _ssm_combine(left, right):
    a1r, a1i, b1r, b1i = left
    a2r, a2i, b2r, b2i = right
    return (a2r * a1r - a2i * a1i,
            a2r * a1i + a2i * a1r,
            a2r * b1r - a2i * b1i + b2r,
            a2r * b1i + a2i * b1r + b2i)

def s5_branch(u, lam_re, lam_im, log_dt, b_re, b_im, c_re, c_im, d_skip, w_glu, b_glu):
    f32 = jnp.float32
    bsz, l, _ = u.shape
    uf = u.astype(f32).reshape(bsz, l, SSM_GROUPS, SSM_GROUP_CH)
    dt = jnp.exp(log_dt.astype(f32))[:, None]
    lr, li = lam_re.astype(f32), lam_im.astype(f32)
    mag = jnp.exp(lr * dt)
    a_re, a_im = mag * jnp.cos(li * dt), mag * jnp.sin(li * dt)
    den = lr * lr + li * li
    e_re, e_im = a_re - 1.0, a_im
    f_re = ((e_re * lr + e_im * li) / den)[..., None]
    f_im = ((e_im * lr - e_re * li) / den)[..., None]
    br, bi = b_re.astype(f32), b_im.astype(f32)
    bb_re = f_re * br - f_im * bi
    bb_im = f_re * bi + f_im * br
    bu_re = jnp.einsum('blgc,gnc->blgn', uf, bb_re)
    bu_im = jnp.einsum('blgc,gnc->blgn', uf, bb_im)
    a_re_t = jnp.broadcast_to(a_re, bu_re.shape)
    a_im_t = jnp.broadcast_to(a_im, bu_im.shape)
    _, _, s_re, s_im = lax.associative_scan(_ssm_combine, (a_re_t, a_im_t, bu_re, bu_im), axis=1)
    y = (jnp.einsum('blgn,gcn->blgc', s_re, c_re.astype(f32))
         - jnp.einsum('blgn,gcn->blgc', s_im, c_im.astype(f32))
         + d_skip.astype(f32) * uf)
    y = jax.nn.gelu(y.reshape(bsz, l, SSM_WIDTH)).astype(u.dtype)
    return y * jax.nn.sigmoid(y @ w_glu + b_glu)

def cross_branch(x_q, mem, mem_norm_g, w_mem_kv, xq_norm_g, xk_norm_g):
    b, l, _ = x_q.shape
    kv = rmsnorm_2(mem, mem_norm_g) @ w_mem_kv
    k = kv[..., :X_WIDTH].reshape(b, MEM_LEN, X_HEADS, X_HEAD_DIM)
    v = kv[..., X_WIDTH:].reshape(b, MEM_LEN, X_HEADS, X_HEAD_DIM)
    q = rmsnorm_2(x_q.reshape(b, l, X_HEADS, X_HEAD_DIM), xq_norm_g)
    k = rmsnorm_2(k, xk_norm_g)
    s = jnp.einsum('blhd,bmhd->bhlm', q, k, preferred_element_type=jnp.float32) * (X_HEAD_DIM ** -0.5)
    p = jax.nn.softmax(s, axis=-1)
    return jnp.einsum('bhlm,bmhd->blhd', p.astype(v.dtype), v).reshape(b, l, X_WIDTH)

def causal_dwconv(x, w, bias):
    c = x.shape[-1]
    y = lax.conv_general_dilated(x, w[:, None, :].astype(x.dtype), window_strides=(1,),
                                 padding=((CONV_WIDTH - 1, 0),),
                                 dimension_numbers=('NWC', 'WIO', 'NWC'),
                                 feature_group_count=c)
    return y + bias

def second_inputs(seed: int = 0) -> dict:
    key = jax.random.key(seed)
    ks = iter(jax.random.split(key, 48))
    f32 = jnp.float32
    L = DEPTH

    def nrm(shape, fan_in):
        return jax.random.normal(next(ks), shape, f32) * (fan_in ** -0.5)

    def gain(shape):
        return 1.0 + 0.02 * jax.random.normal(next(ks), shape, f32)

    def small(shape):
        return 0.01 * jax.random.normal(next(ks), shape, f32)

    x = jax.random.normal(next(ks), (BATCH, SEQ, D_MODEL), f32)
    mem = jax.random.normal(next(ks), (BATCH, MEM_LEN, D_MODEL), f32)
    offset = jax.random.randint(next(ks), (BATCH, 1), 0, 1024, dtype=jnp.int32)
    positions = offset + jnp.arange(SEQ, dtype=jnp.int32)[None, :]
    n_idx = jnp.arange(SSM_STATE, dtype=f32)
    lam_re = -0.5 + small((L, SSM_GROUPS, SSM_STATE))
    lam_im = math.pi * n_idx + small((L, SSM_GROUPS, SSM_STATE))
    log_dt = jax.random.uniform(next(ks), (L, SSM_GROUPS), f32, math.log(DT_MIN), math.log(DT_MAX))
    return {
        "x": x,
        "mem": mem,
        "positions": positions,
        "norm_mix_g": gain((L, D_MODEL)),
        "w_in": nrm((L, D_MODEL, IN_WIDTH_2), D_MODEL),
        "q_a_norm_g": gain((L, Q_LORA)),
        "w_q_b": nrm((L, Q_LORA, MLA_HEADS * D_QK), Q_LORA),
        "kv_a_norm_g": gain((L, KV_LORA)),
        "w_kv_b": nrm((L, KV_LORA, MLA_HEADS * (D_NOPE + D_V)), KV_LORA),
        "q_norm_g": gain((L, D_QK)),
        "k_norm_g": gain((L, D_QK)),
        "w_o_mla": nrm((L, MLA_WIDTH, D_MODEL), MLA_WIDTH),
        "ssm_lambda_re": lam_re,
        "ssm_lambda_im": lam_im,
        "ssm_log_dt": log_dt,
        "ssm_b_re": nrm((L, SSM_GROUPS, SSM_STATE, SSM_GROUP_CH), 2 * SSM_GROUP_CH),
        "ssm_b_im": nrm((L, SSM_GROUPS, SSM_STATE, SSM_GROUP_CH), 2 * SSM_GROUP_CH),
        "ssm_c_re": nrm((L, SSM_GROUPS, SSM_GROUP_CH, SSM_STATE), SSM_STATE),
        "ssm_c_im": nrm((L, SSM_GROUPS, SSM_GROUP_CH, SSM_STATE), SSM_STATE),
        "ssm_d": jax.random.normal(next(ks), (L, SSM_GROUPS, SSM_GROUP_CH), f32),
        "w_glu": nrm((L, SSM_WIDTH, SSM_WIDTH), SSM_WIDTH),
        "b_glu": small((L, SSM_WIDTH)),
        "w_o_ssm": nrm((L, SSM_WIDTH, D_MODEL), SSM_WIDTH),
        "mem_norm_g": gain((L, D_MODEL)),
        "w_mem_kv": nrm((L, D_MODEL, 2 * X_WIDTH), D_MODEL),
        "xq_norm_g": gain((L, X_HEAD_DIM)),
        "xk_norm_g": gain((L, X_HEAD_DIM)),
        "w_o_cross": nrm((L, X_WIDTH, D_MODEL), X_WIDTH),
        "b_gate": small((L, N_BRANCH * D_MODEL)),
        "w_out": nrm((L, D_MODEL, D_MODEL), D_MODEL),
        "norm_ffn_g": gain((L, D_MODEL)),
        "w_up": nrm((L, D_MODEL, 2 * D_FF), D_MODEL),
        "conv_w": nrm((L, CONV_WIDTH, 2 * D_FF), CONV_WIDTH),
        "conv_b": small((L, 2 * D_FF)),
        "w_down": nrm((L, D_FF, D_MODEL), D_FF),
    }

def second_block(x, mem, positions, norm_mix_g, w_in, q_a_norm_g, w_q_b, kv_a_norm_g, w_kv_b,
              q_norm_g, k_norm_g, w_o_mla, ssm_lambda_re, ssm_lambda_im, ssm_log_dt,
              ssm_b_re, ssm_b_im, ssm_c_re, ssm_c_im, ssm_d, w_glu, b_glu, w_o_ssm,
              mem_norm_g, w_mem_kv, xq_norm_g, xk_norm_g, w_o_cross, b_gate, w_out,
              norm_ffn_g, w_up, conv_w, conv_b, w_down):
    bsz, l, _ = x.shape
    cos, sin = rope_tables(positions)
    for i in range(DEPTH):
        h = rmsnorm_2(x, norm_mix_g[i])
        c_q, c_kv, k_r, u_ssm, x_q, gate_logits = split_combined(h @ w_in[i])
        y_a = mla_branch(c_q, c_kv, k_r, cos, sin, q_a_norm_g[i], w_q_b[i], kv_a_norm_g[i],
                         w_kv_b[i], q_norm_g[i], k_norm_g[i]) @ w_o_mla[i]
        y_b = s5_branch(u_ssm, ssm_lambda_re[i], ssm_lambda_im[i], ssm_log_dt[i], ssm_b_re[i],
                        ssm_b_im[i], ssm_c_re[i], ssm_c_im[i], ssm_d[i], w_glu[i], b_glu[i]) @ w_o_ssm[i]
        y_c = cross_branch(x_q, mem, mem_norm_g[i], w_mem_kv[i], xq_norm_g[i], xk_norm_g[i]) @ w_o_cross[i]
        gates = jax.nn.sigmoid(gate_logits + b_gate[i]).reshape(bsz, l, N_BRANCH, D_MODEL)
        merged = gates[:, :, 0] * y_a + gates[:, :, 1] * y_b + gates[:, :, 2] * y_c
        x = x + merged @ w_out[i]
        h2 = rmsnorm_2(x, norm_ffn_g[i])
        up = causal_dwconv(h2 @ w_up[i], conv_w[i], conv_b[i])
        g_ff, v_ff = up[..., :D_FF], up[..., D_FF:]
        x = x + (jax.nn.silu(g_ff) * v_ff) @ w_down[i]
    return x


def setup_inputs(seed=0):
    out = dict(first_inputs(seed))
    for name, value in second_inputs(seed + 1).items():
        if name != "x":
            out[name + "_2"] = value
    return out


def reference(
    x, c, ctx, c_ctx, w_ada, b_ada, norm1_g, norm2_g, w_in, na_rpb, hy_conv_w, hy_conv_b,
    hy_ffn_w1, hy_ffn_b1, hy_ffn_w2, hy_ffn_b2, hy_sin_freq, hy_ffn_w3, hy_bias, w_na_o, w_hy_o,
    w_out, ffn_w1, ffn_w3, ffn_w2, final_g, mem_2, positions_2, norm_mix_g_2, w_in_2,
    q_a_norm_g_2, w_q_b_2, kv_a_norm_g_2, w_kv_b_2, q_norm_g_2, k_norm_g_2, w_o_mla_2,
    ssm_lambda_re_2, ssm_lambda_im_2, ssm_log_dt_2, ssm_b_re_2, ssm_b_im_2, ssm_c_re_2,
    ssm_c_im_2, ssm_d_2, w_glu_2, b_glu_2, w_o_ssm_2, mem_norm_g_2, w_mem_kv_2, xq_norm_g_2,
    xk_norm_g_2, w_o_cross_2, b_gate_2, w_out_2, norm_ffn_g_2, w_up_2, conv_w_2, conv_b_2,
    w_down_2,
):
    x = first_block(
        x, c, ctx, c_ctx, w_ada, b_ada, norm1_g, norm2_g, w_in, na_rpb, hy_conv_w, hy_conv_b,
        hy_ffn_w1, hy_ffn_b1, hy_ffn_w2, hy_ffn_b2, hy_sin_freq, hy_ffn_w3, hy_bias, w_na_o,
        w_hy_o, w_out, ffn_w1, ffn_w3, ffn_w2, final_g,
    )
    return second_block(
        x, mem_2, positions_2, norm_mix_g_2, w_in_2, q_a_norm_g_2, w_q_b_2, kv_a_norm_g_2,
        w_kv_b_2, q_norm_g_2, k_norm_g_2, w_o_mla_2, ssm_lambda_re_2, ssm_lambda_im_2,
        ssm_log_dt_2, ssm_b_re_2, ssm_b_im_2, ssm_c_re_2, ssm_c_im_2, ssm_d_2, w_glu_2, b_glu_2,
        w_o_ssm_2, mem_norm_g_2, w_mem_kv_2, xq_norm_g_2, xk_norm_g_2, w_o_cross_2, b_gate_2,
        w_out_2, norm_ffn_g_2, w_up_2, conv_w_2, conv_b_2, w_down_2,
    )


_drawn_inputs = setup_inputs


def setup_inputs(seed=0):
    import zlib

    import numpy as np

    out = dict(_drawn_inputs(seed))
    spreads = {}
    factors = {'norm1_g': 4.94,
     'norm2_g': 3.535,
     'na_rpb': 8.0,
     'norm_mix_g_2': 8.0,
     'q_a_norm_g_2': 8.0,
     'kv_a_norm_g_2': 8.0,
     'q_norm_g_2': 8.0,
     'k_norm_g_2': 8.0,
     'ssm_lambda_re_2': 64.0,
     'ssm_log_dt_2': 112.456,
     'ssm_b_re_2': 191.888,
     'ssm_b_im_2': 189.216,
     'ssm_c_re_2': 182.176,
     'ssm_c_im_2': 182.192,
     'b_glu_2': 64.0,
     'mem_norm_g_2': 8.0,
     'xq_norm_g_2': 8.0,
     'xk_norm_g_2': 8.0,
     'b_gate_2': 33.223,
     'norm_ffn_g_2': 3.737,
     'conv_b_2': 7.865,
     'ssm_lambda_im_2': 35.776}
    for name, (base, spread) in spreads.items():
        noise = np.random.default_rng([zlib.crc32(name.encode()), seed]).standard_normal(out[name].shape)
        drawn = base * np.exp(spread * noise) if base else spread * noise
        out[name] = __import__('jax').numpy.asarray(drawn.astype(out[name].dtype))
    for name, factor in factors.items():
        out[name] = (out[name] * factor).astype(out[name].dtype)
    return out
```

```python
import math
from contextlib import ExitStack

import numpy as np

import concourse.bass as bass
from concourse import mybir

F32 = mybir.dt.float32
F32R = mybir.dt.float32r
I32 = mybir.dt.int32
ALU = mybir.AluOpType
ACT = mybir.ActivationFunctionType
AX = mybir.AxisListType

P = 128
T = 512
TT = T // P
D = 1024
KD = D // P
CTX = 256
CT = CTX // P
HEADS = 8
HD = 64
GRID_W = 64
GRID_R = T // GRID_W
WIN_H, WIN_W = 8, 16
NEG = -1e30
HYW = 512
HT = HYW // P
EMB = 33
FW = 64
FF = 2816
FT = FF // P
QL, KVL = 384, 256
DQK, DNOPE, DROPE, DV = 96, 64, 32, 64
XH = 4
NSTATE = 64
ST = 16
RING = 4
SLOT = 1024
EPS = 1e-6
TAPS = 14

VECTORS = [
    ("c", 8), ("c_ctx", 8), ("b_ada", 48), ("norm1", 8), ("norm2", 8), ("final", 8), ("norm_mix", 8),
    ("mem_norm", 8), ("norm_ffn", 8), ("hy_conv_w", 36), ("hy_conv_b", 12), ("hy_bias", 8),
    ("hy_b1", 1), ("hy_b2", 1), ("hy_freq", 1), ("conv_w", 132), ("conv_b", 44), ("b_gate", 24),
    ("b_glu", 4), ("q_a", 3), ("kv_a", 2), ("q_norm", 1), ("k_norm", 1), ("xq", 1), ("xk", 1),
    ("lam_re", 16), ("lam_im", 16), ("log_dt", 16), ("ssm_d", 4), ("inv_freq", 1), ("rope_sign", 1),
    ("zero", 8), ("half_pi", 1),
]
VECTOR_AT = {}
NV = 0
for _name, _n in VECTORS:
    VECTOR_AT[_name] = (NV, _n)
    NV += _n

ADA_SLOTS = 48
STAGES = [
    ("q", 4), ("k", 4), ("v", 4), ("hyena_in", 12), ("merge1", 24), ("out1", 8), ("up1", 44),
    ("down1", 22), ("mem_k", 4), ("mem_v", 4), ("in2", 14), ("q_b", 4), ("kv_b", 2), ("glu", 2),
    ("merge2", 36), ("out2", 8), ("up2", 44), ("down2", 22),
]
FIRST = {}
NS = 0
for _name, _n in STAGES:
    FIRST[_name] = NS
    NS += _n

BASE = 16512
TILE_BYTES = 2048
X_AT, RAW_AT, RHIGH_AT, RLOW_AT, HHIGH_AT, HLOW_AT, W = 0, 8, 16, 24, 32, 40, 48
SMALL_AT = 100

MASK_SWAP = [(i + 16) % 32 for i in range(32)]


class Chain:

    def __init__(self, engine, semaphore):
        self.engine, self.semaphore, self.count = engine, semaphore, 0

    def __call__(self, instruction):
        instruction.then_inc(self.semaphore, 1)
        self.count = self.count + 1
        self.engine.wait_ge(self.semaphore, self.count)


def build(nc, a, out, STOP=99, dumps=None):
    ctx = ExitStack()
    with ctx:
        def at(name, tile, tiles, dtype=F32, width=512):
            return nc.alloc_sbuf_tensor_at(name, [P, tiles, width], dtype, offset=BASE + tile * TILE_BYTES)

        def sem(name):
            return ctx.enter_context(nc.semaphore(name))

        small_bytes = [0]

        def small(name, columns, dtype=F32):
            t = nc.alloc_sbuf_tensor_at(name, [P, columns], dtype, offset=BASE + SMALL_AT * TILE_BYTES + small_bytes[0])
            small_bytes[0] += (columns * 4 + 31) // 32 * 32
            return t

        bank = ctx.enter_context(nc.psum_tensor("bank", [P, 8, 512], F32))

        x = at("x", X_AT, 8)
        raw = at("raw", RAW_AT, RING, width=SLOT)
        ring_high = at("ring_high", RHIGH_AT, RING, F32R, SLOT)
        ring_low = at("ring_low", RLOW_AT, RING, F32R, SLOT)
        h_high = at("h_high", HHIGH_AT, 8, F32R)
        h_low = at("h_low", HLOW_AT, 8, F32R)

        vec = small("vec", NV)
        ones = small("ones", P)
        ident = small("ident", P)
        silu_c = small("silu_c", 16)
        mod = small("mod", 48)
        mod_c = small("mod_c", 16)
        gain1 = small("gain1", 8)
        gain1_c = small("gain1_c", 8)
        gain2 = small("gain2", 8)
        att_max = small("att_max", 4)
        att_neg = small("att_neg", 2)
        att_sums = small("att_sums", 4)
        att_total = small("att_total", 2)
        s5 = small("s5", 16 * 24)

        def v_(name, i=0, n=1, p0=0, p1=P):
            return vec[p0:p1, VECTOR_AT[name][0] + i:VECTOR_AT[name][0] + i + n]

        y_high = at("y_high", W + 28, 12, F32R)
        y_low = at("y_low", W + 40, 12, F32R)

        q_scaled = at("q_scaled", W, 4)
        q_rot = at("q_rot", W + 4, 4)
        k_rot = at("k_rot", W + 8, 4)
        v_tok = at("v_tok", W + 12, 4)
        kc = at("kc", W + 16, 4, width=CTX)
        vc = at("vc", W + 18, 2)
        trig1 = at("trig1", W + 20, 2)
        bias1 = at("bias1", W + 22, 2, width=TAPS * GRID_W)
        hc_high = at("hc_high", W + 32, 8, F32R, CTX)
        hc_low = at("hc_low", W + 36, 8, F32R, CTX)
        ctx_in = at("ctx_in", W, 8, width=CTX)
        att1 = dict(s=at("att1_s", W + 32, 2), p=at("att1_p", W + 34, 2, width=768),
                    pt=at("att1_pt", W + 37, 2, width=768))
        rope_t = at("rope_t", W + 26, 2)
        k_plain = at("k_plain", W + 44, 4)
        o_tok1 = at("o_tok1", W + 44, 4)

        w3f = at("w3f", W + 0, 4)
        zt = at("zt", W + 4, 1)
        hid = at("hid", W + 5, 2)
        arg = at("arg", W + 7, 2)
        w12f = at("w12f", W + 9, 1)
        decay = at("decay", W + 44, 4)
        filt = at("filt", W + 32, 8)
        hyu = at("hyu", W + 0, 12)
        dft = at("dft", W + 12, 8)
        spec = [at("spec1", W + 20, 8), at("spec2", X_AT, 8)]
        z_tok = at("z_tok", W + 32, 4)
        y_re = at("y_re", W + 36, 4)
        y_im = at("y_im", W + 48, 4)
        hyt = at("hyt", W + 44, 2)
        hyz = at("hyz", W + 20, 4)

        merged = at("merged", W + 8, 8)
        m_high = at("m_high", W + 0, 8, F32R)
        m_low = at("m_low", W + 16, 8, F32R)
        sig = at("sig", W + 24, 2)
        mprod = at("mprod", W + 26, 2)

        hid_high = at("hid_high", W + 0, 22, F32R)
        hid_low = at("hid_low", W + 22, 22, F32R)
        ff_a = at("ff_a", W + 44, 2)
        ff_v = at("ff_v", W + 46, 2)
        ff_s = at("ff_s", W + 48, 2)
        ff_p = at("ff_p", W + 50, 2)

        mem_in = at("mem_in", W + 12, 8, width=CTX)
        hm_high = at("hm_high", W + 0, 8, F32R, CTX)
        hm_low = at("hm_low", W + 4, 8, F32R, CTX)
        kx = at("kx", W + 8, 4, width=CTX)
        vx = at("vx", W + 10, 2)
        cq = at("cq", W + 12, 3)
        ckv = at("ckv", W + 15, 2)
        kr = at("kr", W + 17, 1)
        xq = at("xq", W + 18, 4)
        u_ssm = at("u_ssm", W + 22, 4)
        cmask = at("cmask", W + 26, 1)
        cq_high = at("cq_high", W + 28, 3, F32R)
        cq_low = at("cq_low", W + 31, 3, F32R)
        ckv_high = at("ckv_high", W + 40, 2, F32R)
        ckv_low = at("ckv_low", W + 42, 2, F32R)
        att2 = dict(s=at("att2_s", W + 0, 2), p=at("att2_p", W + 2, 2, width=768),
                    pt=at("att2_pt", W + 5, 2, width=768))
        o_tok2 = at("o_tok2", W + 44, 4)
        qh = at("qh", W + 0, 8)
        kh = at("kh", W + 12, 4)
        kh2 = at("kh2", W + 18, 4)
        k_head = [kh[:, i] for i in range(4)] + [kh2[:, i] for i in range(4)]
        v_mla = at("v_mla", W + 8, 4)
        rope2 = at("rope2", W + 34, 2)
        rope_w = at("rope_w", W + 28, 4)
        pos_i = at("pos_i", W + 27, 1, I32)
        att3 = dict(s=at("att3_s", W + 40, 2), p=at("att3_p", W + 42, 2, width=768),
                    pt=at("att3_pt", W + 45, 2, width=768))
        o_tok3 = at("o_tok3", W + 32, 4)
        tab_re = at("tab_re", W + 0, 8)
        tab_im = at("tab_im", W + 8, 8)
        bmat = at("bmat", W + 16, 4)
        s5r = at("s5r", W + 20, 2)
        s5t = at("s5t", W + 26, 2)
        s5s = at("s5s", W + 32, 2)
        cmat = at("cmat", W + 34, 4, width=2 * P)
        gy = at("gy", W + 44, 4)
        gy_high = at("gy_high", W + 4, 4, F32R)
        gy_low = at("gy_low", W + 8, 4, F32R)
        gsig = at("gsig", W + 12, 2)
        gprod = at("gprod", W + 14, 2)

        raw_loaded = [sem(f"raw_loaded{i}") for i in range(RING)]
        ada_used = sem("ada_used")
        high_ready = sem("high_ready")
        low_ready = sem("low_ready")
        slot_used = sem("slot_used")
        dve_step = sem("dve_step")
        act_step = sem("act_step")
        first_loaded = sem("first_loaded")
        x_loaded = sem("x_loaded")
        ctx_loaded = sem("ctx_loaded")
        silu_ready = sem("silu_ready")
        mod_ready = sem("mod_ready")
        norm_squared, norm_summed, norm_inverse, norm_root, norm_scaled, norm_rounded, norm_done = (
            sem("norm_" + s) for s in ("squared", "summed", "inverse", "root", "scaled", "rounded", "done"))
        att_scored, att_biased, att_exp, att_turned, att_copied, att_copied2, att_summed, att_written = (
            sem("att_" + s) for s in ("scored", "biased", "exp", "turned", "copied", "copied2", "summed", "written"))
        y_turned, y_rounded, y_split = sem("y_turned"), sem("y_rounded"), sem("y_split")
        in_copied = sem("in_copied")
        out_added = sem("out_added")
        bias_loaded = [sem("bias_loaded0"), sem("bias_loaded1")]
        trig_loaded = sem("trig_loaded")
        qkv_copied, rope_done, qkv_copied2 = sem("qkv_copied"), sem("rope_done"), sem("qkv_copied2")

        def norm(name, tiles, width, size, gains, shifts=None, outs=None, split=None, scratch=W + 40, ready=None):
            rows = tiles[0].shape[0]
            return dict(name=name, tiles=tiles, width=width, size=size, gains=gains, shifts=shifts, outs=outs,
                        split=split, rows=rows, ready=ready,
                        sq=at(f"{name}_sq", scratch, 2), var=at(f"{name}_var", scratch + 2, 1),
                        inv=at(f"{name}_inv", scratch + 3, 1), root=at(f"{name}_root", scratch + 4, 1),
                        t=at(f"{name}_t", scratch + 5, 2))

        def cols(t, n, rows=P):
            return [t[0:rows, i:i + 1] for i in range(n)]

        def vcols(name, n, rows=P):
            return [v_(name, i, 1, 0, rows) for i in range(n)]

        NORMS = [
            norm("n_x1", [x[:, k] for k in range(8)], T, D, cols(gain1, 8), cols(mod, 8),
                 split=([h_high[:, k] for k in range(8)], [h_low[:, k] for k in range(8)])),
            norm("n_ctx", [ctx_in[:, k] for k in range(8)], CTX, D, cols(gain1_c, 8), cols(mod_c, 8),
                 split=([hc_high[:, k] for k in range(8)], [hc_low[:, k] for k in range(8)])),
            norm("n_x2", [x[:, k] for k in range(8)], T, D, cols(gain2, 8), [mod[:, 24 + i:25 + i] for i in range(8)],
                 ready=(out_added, 4),
                 split=([h_high[:, k] for k in range(8)], [h_low[:, k] for k in range(8)])),
            norm("n_final", [x[:, k] for k in range(8)], T, D, vcols("final", 8), outs=[x[:, k] for k in range(8)],
                 scratch=W + 44, ready=(out_added, 4 + 16 - 8)),
            norm("n_mem", [mem_in[:, k] for k in range(8)], CTX, D, vcols("mem_norm", 8), scratch=W + 44,
                 split=([hm_high[:, k] for k in range(8)], [hm_low[:, k] for k in range(8)])),
            norm("n_mix", [x[:, k] for k in range(8)], T, D, vcols("norm_mix", 8), scratch=W + 44, ready=(norm_done, 24),
                 split=([h_high[:, k] for k in range(8)], [h_low[:, k] for k in range(8)])),
        ]
        NORMS += [norm(f"n_kx{i}", [kx[:, i]], CTX, P, vcols("xk", 1), outs=[kx[:, i]], scratch=W + 28,
                       ready=(in_copied, i)) for i in range(4)]
        NORMS += [norm(f"n_xq{i}", [xq[:, i]], T, P, vcols("xq", 1), outs=[xq[:, i]], scratch=W + 28,
                       ready=(in_copied, 12 + i)) for i in range(4)]
        NORMS += [
            norm("n_cq", [cq[:, k] for k in range(3)], T, QL, vcols("q_a", 3), scratch=W + 0, ready=(in_copied, 6),
                 split=([cq_high[:, k] for k in range(3)], [cq_low[:, k] for k in range(3)])),
            norm("n_ckv", [ckv[:, k] for k in range(2)], T, KVL, vcols("kv_a", 2), scratch=W + 0, ready=(in_copied, 9),
                 split=([ckv_high[:, k] for k in range(2)], [ckv_low[:, k] for k in range(2)])),
        ]
        NORMS += [norm(f"n_q{i}", [qh[0:DQK, i]], T, DQK, vcols("q_norm", 1, DQK), outs=[qh[0:DQK, i]], scratch=W + 40)
                  for i in range(8)]
        NORMS += [norm(f"n_k{i}", [k_head[i][0:DQK]], T, DQK, vcols("k_norm", 1, DQK), outs=[k_head[i][0:DQK]],
                       scratch=W + 40) for i in range(8)]
        NORMS += [norm("n_ffn", [x[:, k] for k in range(8)], T, D, vcols("norm_ffn", 8), ready=(out_added, 4 + 16),
                       split=([h_high[:, k] for k in range(8)], [h_low[:, k] for k in range(8)]))]
        NORM = {}
        squares = outputs = rounds = 0
        for i, n in enumerate(NORMS):
            n.update(index=i, squares=squares, outputs=outputs, rounds=rounds)
            squares += len(n["tiles"])
            outputs += len(n["tiles"])
            rounds += len(n["tiles"]) if n["split"] else 0
            n["done"] = outputs
            NORM[n["name"]] = n

        def norm_scalar(act, n):
            w, r = n["width"], n["rows"]
            for k, t in enumerate(n["tiles"]):
                i = n["squares"] + k
                if n["ready"]:
                    act.wait_ge(n["ready"][0], n["ready"][1] + k + 1)
                if i >= 2:
                    act.wait_ge(norm_summed, i - 1)
                nc.scalar.activation(n["sq"][0:r, i % 2, 0:w], t, ACT.Square).then_inc(norm_squared, 1)
            act.wait_ge(norm_inverse, n["index"] + 1)
            nc.scalar.activation(n["root"][0:r, 0, 0:w], n["inv"][0:r, 0, 0:w], ACT.Sqrt).then_inc(norm_root, 1)
            if n["split"]:
                for k in range(len(n["tiles"])):
                    act.wait_ge(norm_scaled, n["rounds"] + k + 1)
                    shift = n["shifts"][k] if n["shifts"] else v_("zero")
                    nc.scalar.activation(n["split"][0][k], n["t"][0:r, k % 2, 0:w], ACT.Identity,
                                         bias=shift).then_inc(norm_rounded, 1)

        def norm_tensor(pe, n):
            w, r = n["width"], n["rows"]
            if n["index"] >= 1:
                pe.wait_ge(norm_inverse, n["index"])
            for k in range(len(n["tiles"])):
                i = n["squares"] + k
                pe.wait_ge(norm_squared, i + 1)
                nc.tensor.matmul(bank[0:r, 7, 0:w], ones[0:r, 0:r], n["sq"][0:r, i % 2, 0:w],
                                 start=(k == 0), stop=(k == len(n["tiles"]) - 1)).then_inc(norm_summed, 1)

        def norm_vector(dve, link, n):
            w, r = n["width"], n["rows"]
            m = len(n["tiles"])
            dve.wait_ge(norm_summed, n["squares"] + m)
            link(nc.vector.tensor_scalar(n["var"][0:r, 0, 0:w], bank[0:r, 7, 0:w], 1.0 / n["size"], EPS, ALU.mult, ALU.add))
            nc.vector.reciprocal(n["inv"][0:r, 0, 0:w], n["var"][0:r, 0, 0:w]).then_inc(norm_inverse, 1)
            dve.wait_ge(norm_root, n["index"] + 1)
            root = n["root"][0:r, 0, 0:w]
            if not n["split"]:
                for k in range(m):
                    nc.vector.scalar_tensor_tensor(out=n["outs"][k], in0=n["tiles"][k], scalar=n["gains"][k], in1=root,
                                                   op0=ALU.mult, op1=ALU.mult).then_inc(norm_done, 1)
                dve.wait_ge(norm_done, n["done"])
                return
            for k in range(m + 1):
                if k < m:
                    if k >= 2:
                        dve.wait_ge(norm_done, n["outputs"] + k - 1)
                    nc.vector.scalar_tensor_tensor(out=n["t"][0:r, k % 2, 0:w], in0=n["tiles"][k], scalar=n["gains"][k],
                                                   in1=root, op0=ALU.mult, op1=ALU.mult).then_inc(norm_scaled, 1)
                if k >= 1:
                    j = k - 1
                    dve.wait_ge(norm_rounded, n["rounds"] + j + 1)
                    shift = n["shifts"][j] if n["shifts"] else v_("zero")
                    nc.vector.scalar_tensor_tensor(out=n["split"][1][j], in0=n["t"][0:r, j % 2, 0:w], scalar=shift,
                                                   in1=n["split"][0][j], op0=ALU.add, op1=ALU.subtract).then_inc(norm_done, 1)
            dve.wait_ge(norm_done, n["done"])

        ATT = []

        def half_rows(t, i, h):
            return t[64 * (h % 2):64 * (h % 2) + 64, i]

        for h in range(HEADS):
            for t in range(TT):
                qs = slice(t * P, t * P + P)
                ATT.append(dict(
                    at=att1, q=half_rows(q_rot, h // 2, h)[:, qs], k=half_rows(k_rot, h // 2, h),
                    table=bias1[:, h % 2, (6 - 2 * t) * GRID_W:(6 - 2 * t + 8) * GRID_W], width=T, scale=1.0,
                    q2=half_rows(q_scaled, h // 2, h)[:, qs], k2=half_rows(kc, h // 2, h), width2=CTX,
                    values=[v_tok[:, i, h * HD:(h + 1) * HD] for i in range(TT)]
                    + [vc[:, i, h * HD:(h + 1) * HD] for i in range(CT)],
                    out=o_tok1[:, t, h * HD:(h + 1) * HD], head=h, first=(t == 0)))
        ATT1 = len(ATT)
        for h in range(XH):
            for t in range(TT):
                ATT.append(dict(
                    at=att2, q=xq[:, h, t * P:t * P + P], k=kx[:, h], table=cmask[:, 0, 0:CTX], width=CTX,
                    scale=float(P) ** -0.5, q2=None,
                    values=[vx[:, i, h * P:(h + 1) * P] for i in range(CT)], out=o_tok2[:, t, h * P:(h + 1) * P]))
        ATT2 = len(ATT)
        for h in range(HEADS):
            for t in range(TT):
                w = (t + 1) * P
                ATT.append(dict(
                    at=att3, q=qh[0:DQK, h, t * P:t * P + P], k=k_head[h][0:DQK, 0:w], table=cmask[:, 0, T - w:T], width=w,
                    scale=float(DQK) ** -0.5, q2=None,
                    values=[v_mla[:, i, h * DV:(h + 1) * DV] for i in range(t + 1)], out=o_tok3[:, t, h * DV:(h + 1) * DV]))
        ATT3 = len(ATT)
        seconds = 0
        for s in ATT:
            keys = len(s["values"])
            s["near"] = min(keys, (keys + 1) // 2)
            s["seconds"] = seconds
            seconds += keys > s["near"]
            s["seconds_done"] = seconds

        def att_tensor(pe, lo, hi):
            def scores(n):
                s = ATT[n]
                if n >= 2:
                    pe.wait_ge(att_biased, n - 1)
                    pe.wait_ge(att_exp, n - 1)
                mm = nc.tensor.matmul(bank[:, n % 2, 0:s["width"]], s["q"], s["k"], start=True, stop=True)
                if s["q2"] is not None:
                    mm = nc.tensor.matmul(bank[:, 2 + n % 2, 0:CTX], s["q2"], s["k2"], start=True, stop=True)
                mm.then_inc(att_scored, 1)

            def weigh(n):
                s = ATT[n]
                keys, near = len(s["values"]), s["near"]
                pe.wait_ge(att_exp, n + 1)
                if n >= 1:
                    pe.wait_ge(att_copied, n)
                if s["seconds"] >= 1:
                    pe.wait_ge(att_copied2, s["seconds"])
                for i in range(keys):
                    b, c = (4, i) if i < near else (5, i - near)
                    mm = nc.tensor.transpose(bank[:, b, c * P:(c + 1) * P], s["at"]["p"][:, n % 2, i * P:(i + 1) * P], ident[:, :])
                mm.then_inc(att_turned, 1)
                pe.wait_ge(att_copied, n + 1)
                if keys > near:
                    pe.wait_ge(att_copied2, s["seconds_done"])
                if n >= 2:
                    pe.wait_ge(att_written, n - 1)
                dv = s["values"][0].shape[1]
                for i in range(keys):
                    mm = nc.tensor.matmul(bank[:, 6 + n % 2, 0:dv], s["at"]["pt"][:, n % 2, i * P:(i + 1) * P], s["values"][i],
                                          start=(i == 0), stop=(i == keys - 1))
                mm.then_inc(att_summed, 1)

            scores(lo)
            for n in range(lo, hi):
                if n + 1 < hi:
                    scores(n + 1)
                weigh(n)

        def att_scalar(act, lo, hi, between=None):
            def exps(n):
                s = ATT[n]
                act.wait_ge(att_biased, n + 1)
                if n >= 2:
                    act.wait_ge(att_turned, n - 1)
                    act.wait_ge(att_written, n - 1)
                j = n % 2
                neg = att_neg[:, j:j + 1]
                e = nc.scalar.activation(s["at"]["p"][:, j, 0:s["width"]], s["at"]["s"][:, j, 0:s["width"]], ACT.Exp,
                                         bias=neg, accum_out=att_sums[:, 2 * j:2 * j + 1])
                if s["q2"] is not None:
                    e = nc.scalar.activation(s["at"]["p"][:, j, T:T + CTX], bank[:, 2 + j, 0:CTX], ACT.Exp,
                                             bias=neg, accum_out=att_sums[:, 2 * j + 1:2 * j + 2])
                e.then_inc(att_exp, 1)

            exps(lo)
            for n in range(lo, hi):
                if n + 1 < hi:
                    exps(n + 1)
                s = ATT[n]
                keys, near = len(s["values"]), s["near"]
                if keys > near:
                    act.wait_ge(att_turned, n + 1)
                    if n >= 2:
                        act.wait_ge(att_summed, n - 1)
                    nc.scalar.activation(s["at"]["pt"][:, n % 2, near * P:keys * P], bank[:, 5, 0:(keys - near) * P],
                                         ACT.Copy).then_inc(att_copied2, 1)
                if between:
                    between(n)

        def att_vector(dve, link, lo, hi):
            def biased(n):
                s = ATT[n]
                j = n % 2
                dve.wait_ge(att_scored, n + 1)
                if n >= 2:
                    dve.wait_ge(att_exp, n - 1)
                if n < ATT1 and s["first"]:
                    dve.wait_ge(bias_loaded[s["head"] % 2], 16 * (s["head"] // 2 + 1))
                w = s["width"]
                start = NEG
                if s["q2"] is not None:
                    link(nc.vector.reduce_max(att_max[:, j:j + 1], bank[:, 2 + j, 0:CTX], AX.X))
                    start = att_max[:, j:j + 1]
                link(nc.vector.tensor_tensor_reduce(s["at"]["s"][:, j, 0:w], bank[:, j, 0:w], s["table"], s["scale"], start,
                                                    ALU.add, ALU.max, att_max[:, 2 + j:3 + j]))
                nc.vector.tensor_scalar(att_neg[:, j:j + 1], att_max[:, 2 + j:3 + j], -1.0, None,
                                        ALU.mult).then_inc(att_biased, 1)

            def written(n):
                s = ATT[n]
                j = n % 2
                dv = s["values"][0].shape[1]
                dve.wait_ge(att_exp, n + 1)
                total = att_sums[:, 2 * j:2 * j + 1]
                if s["q2"] is not None:
                    link(nc.vector.tensor_tensor(att_total[:, j:j + 1], total, att_sums[:, 2 * j + 1:2 * j + 2], ALU.add))
                    total = att_total[:, j:j + 1]
                link(nc.vector.reciprocal(att_total[:, j:j + 1], total))
                dve.wait_ge(att_summed, n + 1)
                nc.vector.tensor_scalar(s["out"], bank[:, 6 + j, 0:dv], att_total[:, j:j + 1], None,
                                        ALU.mult).then_inc(att_written, 1)

            biased(lo)
            for n in range(lo, hi):
                if n + 1 < hi:
                    biased(n + 1)
                s = ATT[n]
                dve.wait_ge(att_turned, n + 1)
                if n >= 2:
                    dve.wait_ge(att_summed, n - 1)
                near = s["near"]
                nc.vector.tensor_copy(s["at"]["pt"][:, n % 2, 0:near * P], bank[:, 4, 0:near * P]).then_inc(att_copied, 1)
                if n > lo:
                    written(n - 1)
            written(hi - 1)

        def turn_tensor(pe, o_tok, steps, before):
            pe.wait_ge(att_written, steps)
            for c in range(4):
                for t in range(TT):
                    mm = nc.tensor.transpose(bank[:, c, t * P:(t + 1) * P], o_tok[:, t, c * P:(c + 1) * P], ident[:, :])
                mm.then_inc(y_turned, 1)

        def turn_scalar(act, branch, before):
            for c in range(4):
                act.wait_ge(y_turned, before + c + 1)
                nc.scalar.activation(y_high[:, 4 * branch + c], bank[:, c], ACT.Copy).then_inc(y_rounded, 1)

        def turn_vector(dve, branch, before):
            for c in range(4):
                dve.wait_ge(y_rounded, before + c + 1)
                nc.vector.tensor_tensor(y_low[:, 4 * branch + c], bank[:, c], y_high[:, 4 * branch + c],
                                        ALU.subtract).then_inc(y_split, 1)
            dve.wait_ge(y_split, before + 4)

        def product(o, w_high, w_low, a_high, a_low, start, stop):
            nc.tensor.matmul(o, w_high, a_high, start=start, stop=False)
            nc.tensor.matmul(o, w_high, a_low, start=False, stop=False)
            return nc.tensor.matmul(o, w_low, a_high, start=False, stop=stop)

        def block_of(position, k, n=P):
            return ring_high[:, position, k * P:k * P + n], ring_low[:, position, k * P:k * P + n]

        def tile_product(o, position, first, acts, stop_all=True):
            for k, (ah, al) in enumerate(acts):
                wh, wl = block_of(position, first + k)
                mm = product(o, wh, wl, ah, al, k == 0, k == len(acts) - 1)
            return mm

        def split_high(act, n, it=0):
            if isinstance(it, int) and n >= NS:
                return
            act.wait_ge(raw_loaded[n % RING], 16 * (ADA_SLOTS // RING + n // RING + 1) + it * 16)
            if n >= RING:
                act.wait_ge(slot_used, it * 4 + (n - RING + 1))
            nc.scalar.activation(ring_high[:, n % RING], raw[:, n % RING], ACT.Copy).then_inc(high_ready, 1)

        H = [(h_high[:, k], h_low[:, k]) for k in range(8)]

        HC = [(hc_high[:, k], hc_low[:, k]) for k in range(8)]
        HM = [(hm_high[:, k], hm_low[:, k]) for k in range(8)]
        M_ = [(m_high[:, k], m_low[:, k]) for k in range(8)]
        CQ = [(cq_high[:, k], cq_low[:, k]) for k in range(3)]
        CKV = [(ckv_high[:, k], ckv_low[:, k]) for k in range(2)]
        GY = [(gy_high[:, k], gy_low[:, k]) for k in range(4)]

        filt_loaded, hid_made, arg_ready, hid_ready = (sem(s) for s in ("filt_loaded", "hid_made", "arg_ready", "hid_ready"))
        filt_made, filt_summed, k_made, k_copied, dft_loaded = (
            sem(s) for s in ("filt_made", "filt_summed", "k_made", "k_copied", "dft_loaded"))
        conv_centre, conv_done = sem("conv_centre"), sem("conv_done")
        z_turned, z_copied, u_made, y_made, z_back, z_done = (
            sem(s) for s in ("z_turned", "z_copied", "u_made", "y_made", "z_back", "z_done"))
        merge_sig, merge_added, merge_rounded, merge_low = (
            sem("merge_" + s) for s in ("sig", "added", "rounded", "low"))
        up_gate, up_prod, up_rounded, up_low, up_centre, up_conv = (
            sem("up_" + s) for s in ("gate", "prod", "rounded", "low", "centre", "conv"))
        mem_loaded, mask_loaded, mla_roped, pos_loaded, rope_arg, rope_sin = (
            sem(s) for s in ("mem_loaded", "mask_loaded", "mla_roped", "pos_loaded", "rope_arg", "rope_sin"))
        s5_arg, s5_sin, s5_in, s5_rotated, s5_states, s5_out, s5_y, s5_gelu, s5_b = (
            sem("s5_" + s) for s in ("arg", "sin", "in", "rotated", "states", "out", "y", "gelu", "b"))
        s5_c = [sem(f"s5_c{i}") for i in range(4)]
        s5_c_ready = sem("s5_c_ready")
        glu_rounded, glu_low, glu_sig, glu_prod = (sem("glu_" + s) for s in ("rounded", "low", "sig", "prod"))
        stored = sem("stored")

        IN_MEM, IN_IN2, IN_QB, IN_K, IN_V = 6, 20, 28, 36, 40
        IN_KR = 48

        block = ctx.enter_context(nc.Block())

        @block.sync
        def _(sp):
            def load(position, index):
                sp.dma_start(raw[:, position], a["stream"][bass.ds(index, 1)].rearrange("a p n -> (a p) n")) \
                  .then_inc(raw_loaded[position], 16)

            for j in range(RING):
                load(j, j)
            with sp.Fori(1, ADA_SLOTS // RING) as i:
                for j in range(RING):
                    sp.wait_ge(ada_used, i * RING + (j - RING + 1))
                    load(j, i * RING + j)
            for j in range(RING):
                sp.wait_ge(ada_used, ADA_SLOTS - RING + j + 1)
                load(j, ADA_SLOTS + j)
            with sp.Fori(1, NS // RING) as i:
                for j in range(RING):
                    sp.wait_ge(low_ready, i * RING + (j - RING + 1))
                    load(j, i * RING + (ADA_SLOTS + j))
            for n in range(NS // RING * RING, NS):
                sp.wait_ge(low_ready, n - RING + 1)
                load(n % RING, ADA_SLOTS + n)

        @block.gpsimd
        def _(pool):
            def split_low(position, n):
                pool.wait_ge(high_ready, n)
                nc.gpsimd.tensor_tensor(ring_low[:, position], raw[:, position], ring_high[:, position],
                                        ALU.subtract).then_inc(low_ready, 1)

            with pool.Fori(0, NS // RING) as i:
                for j in range(RING):
                    split_low(j, i * RING + (j + 1))
            for n in range(NS // RING * RING, NS):
                split_low(n % RING, n + 1)

        @block.scalar
        def _(act):
            copy = nc.scalar.activation
            link = Chain(act, act_step)
            act.dma_start(vec[:, :], a["vectors"]).then_inc(first_loaded, 16)
            act.dma_start(ones[:, :], a["ones"]).then_inc(first_loaded, 16)
            act.dma_start(ident[:, :], a["identity"]).then_inc(first_loaded, 16)
            act.dma_start(x[:, :, :], a["x"]).then_inc(x_loaded, 16)
            act.dma_start(ctx_in[:, :, :], a["ctx"]).then_inc(ctx_loaded, 16)
            act.dma_start(trig1[:, :, :], a["trig1"]).then_inc(trig_loaded, 16)
            for h in range(2):
                act.dma_start(bias1[:, h], a["bias"][h]).then_inc(bias_loaded[h], 16)

            act.wait_ge(first_loaded, 48)
            copy(silu_c[:, :].rearrange("p (k v) -> p v k", v=2), vec[:, 0:16].rearrange("p (v k) -> p v k", v=2),
                 ACT.Silu).then_inc(silu_ready, 1)
            act.wait_ge(x_loaded, 16)
            norm_scalar(act, NORM["n_x1"])
            act.wait_ge(ctx_loaded, 16)
            norm_scalar(act, NORM["n_ctx"])
            split_high(act, 0)
            split_high(act, 1)
            if STOP <= 1:
                return

            act.wait_ge(norm_done, NORM["n_ctx"]["done"])
            for j in range(4):
                n = FIRST["q"] + j
                split_high(act, n + 2)
                act.wait_ge(slot_used, n + 1)
                copy(q_scaled[:, j], bank[:, j], ACT.Copy, scale=HD ** -0.5).then_inc(qkv_copied, 1)
            for j in range(4):
                n = FIRST["k"] + j
                split_high(act, n + 2)
                act.wait_ge(slot_used, n + 1)
                copy(k_plain[:, j], bank[:, j], ACT.Copy).then_inc(qkv_copied, 1)
                copy(kc[:, j], bank[:, 4 + j, 0:CTX], ACT.Copy).then_inc(qkv_copied, 1)
            for j in range(4):
                split_high(act, FIRST["v"] + j + 2)
            act.wait_ge(slot_used, FIRST["v"] + 4)
            for t in range(TT):
                copy(v_tok[:, t], bank[:, t], ACT.Copy).then_inc(qkv_copied, 1)
            for t in range(CT):
                copy(vc[:, t], bank[:, 4 + t], ACT.Copy).then_inc(qkv_copied, 1)

            def next_bias(n):
                h = n // TT + 1
                if n % TT == 1 and 2 <= h < HEADS:
                    act.wait_ge(att_biased, TT * (h - 1))
                    act.dma_start(bias1[:, h % 2], a["bias"][h]).then_inc(bias_loaded[h % 2], 16)

            att_scalar(act, 0, ATT1, next_bias)
            turn_scalar(act, 0, 0)
            if STOP <= 2:
                return

            act.wait_ge(y_turned, 4)
            for dst, src in ((w3f[0:FW, :, :], "hy_w3"), (zt[0:EMB, 0], "hy_z"), (w12f[0:FW, 0, 0:2 * FW], "hy_w12"),
                             (decay[:, :, :], "decay"), (dft[:, :, :], "dft1")):
                act.dma_start(dst, a[src]).then_inc(filt_loaded, 16)
            for i in range(2):
                act.wait_ge(arg_ready, i + 1)
                copy(hid[0:FW, i], arg[0:FW, 0], ACT.Sin).then_inc(hid_ready, 1)
            for n in range(2):
                for f in range(4):
                    act.wait_ge(k_made, 4 * n + f + 1)
                    b = 4 + 2 * (f % 2)
                    link(copy(spec[n][:, f], bank[:, b], ACT.Copy, scale=1.0 / T))
                    copy(spec[n][:, 4 + f], bank[:, b + 1], ACT.Copy, scale=1.0 / T).then_inc(k_copied, 1)
            act.dma_start(dft[:, :, :], a["dft2"]).then_inc(dft_loaded, 16)

            with act.Fori(0, 3) as part:
                for j in range(4):
                    n = FIRST["hyena_in"] + j
                    split_high(act, n + 2, part)
                    act.wait_ge(slot_used, part * 4 + (n + 1))
                    wc, bc = VECTOR_AT["hy_conv_w"][0] + 12 + j, VECTOR_AT["hy_conv_b"][0] + j
                    copy(hyu[:, bass.ds(part * 4 + j, 1)].rearrange("p a n -> p (a n)"), bank[:, j], ACT.Identity,
                         scale=vec[:, bass.ds(part * 4 + wc, 1)], bias=vec[:, bass.ds(part * 4 + bc, 1)]).then_inc(conv_centre, 1)
            for n in range(2):
                for t in range(TT):
                    act.wait_ge(z_turned, 4 * n + t + 1)
                    copy(z_tok[:, t], bank[:, t], ACT.Copy).then_inc(z_copied, 1)
            act.wait_ge(y_made, 8)
            act.dma_start(x[:, :, :], a["x"]).then_inc(x_loaded, 16)
            for c in range(4):
                act.wait_ge(z_done, 4 + c + 1)
                copy(y_high[:, 4 + c], hyz[:, c], ACT.Copy).then_inc(y_rounded, 1)
            if STOP <= 3:
                return

            def merge_scalar(stage, branches, tiles, bias):
                with act.Fori(0, branches) as b:
                    for p in range(4):
                        q = 4 * (p % 2)
                        for i in range(2):
                            n = FIRST[stage] + 3 * p + i
                            g = 2 * p + i
                            split_high(act, n + 2, b * 3)
                            act.wait_ge(slot_used, b * 12 + (n + 1))
                            act.wait_ge(merge_added, b * 8 + (tiles + g + 3))
                            shift = vec[:, bass.ds(b * 8 + (bias + g), 1)] if bias is not None else v_("zero")
                            copy(sig[:, i], bank[:, q + i], ACT.Sigmoid, bias=shift).then_inc(merge_sig, 1)
                        split_high(act, FIRST[stage] + 3 * p + 4, b * 3)
                        for i in range(2):
                            g = 2 * p + i
                            act.wait_ge(merge_added, b * 8 + (tiles + g + 5))
                            copy(m_high[:, g], merged[:, g], ACT.Copy).then_inc(merge_rounded, 1)

            def splits(stage):
                with act.Fori(0, 2) as i:
                    for j in range(4):
                        split_high(act, FIRST[stage] + j + 2, i)

            def down_splits(stage):
                for half in range(2):
                    n = FIRST[stage] + 11 * half
                    split_high(act, n + 2)
                    with act.Fori(0, 2) as i:
                        for j in range(4):
                            split_high(act, n + 1 + j + 2, i)
                    split_high(act, n + 11)
                    split_high(act, n + 12)

            merge_scalar("merge1", 2, 0, None)
            splits("out1")
            norm_scalar(act, NORM["n_x2"])

            with act.Fori(0, 11) as i:
                for q in range(2):
                    n = FIRST["up1"] + 2 * q
                    split_high(act, n + 2, i)
                    act.wait_ge(slot_used, i * 4 + (n + 1))
                    act.wait_ge(up_prod, i * 2 + (q + 1))
                    copy(ff_s[:, q], bank[:, 2 * q], ACT.Silu).then_inc(up_gate, 1)
                    split_high(act, n + 3, i)
                    act.wait_ge(up_prod, i * 2 + (q + 3))
                    copy(hid_high[:, bass.ds(i * 2 + q, 1)].rearrange("p a n -> p (a n)"), ff_p[:, q], ACT.Copy) \
                        .then_inc(up_rounded, 1)
            down_splits("down1")
            if STOP <= 4:
                return

            act.wait_ge(slot_used, FIRST["down1"] + 22)
            act.dma_start(mem_in[:, :, :], a["mem"]).then_inc(mem_loaded, 16)
            act.dma_start(cmask[:, 0], a["cmask"]).then_inc(mask_loaded, 16)
            act.dma_start(pos_i[64:96, 0], a["positions"].partition_broadcast(DROPE)).then_inc(pos_loaded, 16)
            norm_scalar(act, NORM["n_final"])
            act.wait_ge(mem_loaded, 16)
            norm_scalar(act, NORM["n_mem"])
            norm_scalar(act, NORM["n_mix"])
            for j in range(4):
                n = FIRST["mem_k"] + j
                split_high(act, n + 2)
                act.wait_ge(slot_used, n + 1)
                copy(kx[:, j], bank[:, j, 0:CTX], ACT.Copy).then_inc(in_copied, 1)
            for j in range(4):
                split_high(act, FIRST["mem_v"] + j + 2)
            act.wait_ge(slot_used, FIRST["mem_v"] + 4)
            for t in range(CT):
                copy(vx[:, t], bank[:, 4 + t], ACT.Copy).then_inc(in_copied, 1)
            dests = [cq[:, i] for i in range(3)] + [ckv[:, i] for i in range(2)] + [kr[64:96, 0]] \
                + [xq[:, i] for i in range(4)] + [u_ssm[:, i] for i in range(4)]
            act.wait_ge(norm_done, NORM["n_mem"]["done"])
            for j, dst in enumerate(dests):
                n = FIRST["in2"] + j
                split_high(act, n + 2)
                act.wait_ge(slot_used, n + 1)
                src = bank[64:96, j % 4] if j == 5 else bank[:, j % 4]
                copy(dst, src, ACT.Copy).then_inc(in_copied, 1)
            for i in range(4):
                norm_scalar(act, NORM[f"n_kx{i}"])
            for i in range(4):
                norm_scalar(act, NORM[f"n_xq{i}"])
            att_scalar(act, ATT1, ATT2)
            turn_scalar(act, 2, 4)
            if STOP <= 5:
                return

            norm_scalar(act, NORM["n_cq"])
            norm_scalar(act, NORM["n_ckv"])
            for j in range(4):
                n = FIRST["q_b"] + j
                split_high(act, n + 2)
                act.wait_ge(slot_used, n + 1)
                for i in range(2):
                    copy(qh[0:DQK, 2 * j + i], bank[0:DQK, (2 * j + i) % 4], ACT.Copy).then_inc(in_copied, 1)
            n = FIRST["kv_b"]
            split_high(act, n + 2)
            act.wait_ge(slot_used, n + 1)
            for h in range(HEADS):
                copy(k_head[h][0:DNOPE], bank[64 * (h % 2):64 * (h % 2) + 64, h // 2], ACT.Copy).then_inc(in_copied, 1)
            split_high(act, n + 3)
            act.wait_ge(slot_used, n + 2)
            for t in range(TT):
                copy(v_mla[:, t], bank[:, 4 + t], ACT.Copy).then_inc(in_copied, 1)
            for h in range(HEADS):
                copy(k_head[h][64:96], kr[64:96, 0], ACT.Copy).then_inc(in_copied, 1)
            act.wait_ge(in_copied, IN_KR)
            for i in range(8):
                norm_scalar(act, NORM[f"n_q{i}"])
            for i in range(8):
                norm_scalar(act, NORM[f"n_k{i}"])
            for i in range(2):
                act.wait_ge(rope_arg, i + 1)
                copy(rope2[64:96, 1 - i], rope_w[64:96, 3], ACT.Sin).then_inc(rope_sin, 1)
            att_scalar(act, ATT2, ATT3)
            turn_scalar(act, 0, 8)
            if STOP <= 6:
                return

            act.wait_ge(y_split, 16)
            act.wait_ge(y_turned, 12)
            act.dma_start(bmat[:, :, :], a["ssm_b"][0]).then_inc(s5_b, 16)
            for s in range(4):
                act.dma_start(cmat[:, s], a["ssm_c"][s]).then_inc(s5_c[s], 16)
            for i in range(2):
                act.wait_ge(s5_arg, i + 1)
                copy(s5[:, 16 * (6 + i):16 * (7 + i)], s5[:, 16 * 5:16 * 6], ACT.Sin).then_inc(s5_sin, 1)
            for s in range(ST):
                if s == 7:
                    act.wait_ge(s5_in, 8)
                    act.dma_start(bmat[:, :, :], a["ssm_b"][1]).then_inc(s5_b, 16)
                act.wait_ge(s5_out, s + 1)
                if s + 4 < ST:
                    act.dma_start(cmat[:, s % 4], a["ssm_c"][s + 4]).then_inc(s5_c[s % 4], 16)
                if s % 4 == 3:
                    i = s // 4
                    act.wait_ge(s5_y, i + 1)
                    copy(gy[:, i], gy[:, i], ACT.Gelu_apprx_tanh).then_inc(s5_gelu, 1)
            act.wait_ge(s5_gelu, 4)
            for c in range(4):
                copy(gy_high[:, c], gy[:, c], ACT.Copy).then_inc(glu_rounded, 1)
            for c in range(4):
                n = FIRST["glu"] + c // 2
                if c % 2 == 0:
                    split_high(act, n + 2)
                    act.wait_ge(slot_used, n + 1)
                if c >= 2:
                    act.wait_ge(glu_prod, c - 1)
                copy(gsig[:, c % 2], bank[:, c], ACT.Sigmoid, bias=v_("b_glu", c)).then_inc(glu_sig, 1)
                act.wait_ge(glu_prod, c + 1)
                copy(y_high[:, 4 + c], gprod[:, c % 2], ACT.Copy).then_inc(y_rounded, 1)
            if STOP <= 7:
                return

            merge_scalar("merge2", 3, 16, VECTOR_AT["b_gate"][0])
            splits("out2")
            norm_scalar(act, NORM["n_ffn"])

            with act.Fori(0, 11) as i:
                for q in range(2):
                    n = FIRST["up2"] + 2 * q
                    for g, dst in ((0, ff_a), (1, ff_v)):
                        split_high(act, n + 2 + g, i)
                        act.wait_ge(slot_used, i * 4 + (n + 1 + g))
                        if g == 0:
                            act.wait_ge(up_prod, i * 2 + (22 + q + 1))
                        wc, bc = VECTOR_AT["conv_w"][0] + 88 + 22 * g + q, VECTOR_AT["conv_b"][0] + 22 * g + q
                        copy(dst[:, q], bank[:, 2 * q + g], ACT.Identity, scale=vec[:, bass.ds(i * 2 + wc, 1)],
                             bias=vec[:, bass.ds(i * 2 + bc, 1)]).then_inc(up_centre, 1)
                    act.wait_ge(up_conv, i * 4 + (4 + 2 * q + 1))
                    copy(ff_s[:, q], ff_a[:, q], ACT.Silu).then_inc(up_gate, 1)
                    act.wait_ge(up_prod, i * 2 + (22 + q + 3))
                    copy(hid_high[:, bass.ds(i * 2 + q, 1)].rearrange("p a n -> p (a n)"), ff_p[:, q], ACT.Copy) \
                        .then_inc(up_rounded, 1)
            down_splits("down2")
            for k in range(8):
                act.wait_ge(out_added, 4 + 24 + k + 1)
                act.dma_start(out[k], x[:, k]).then_inc(stored, 16)
            act.wait_ge(stored, 16 * 8)

        @block.tensor
        def _(pe):
            mm = nc.tensor.matmul
            pe.wait_ge(first_loaded, 48)
            norm_tensor(pe, NORM["n_x1"])
            pe.wait_ge(silu_ready, 1)
            with pe.Fori(0, ADA_SLOTS // RING) as i:
                for j in range(RING):
                    pe.wait_ge(raw_loaded[j], i * 16 + 16)
                    for k in range(8):
                        last = mm(bank[:, 0, bass.ds(i * 8 + 2 * j, 2)], raw[:, j, k * P:(k + 1) * P],
                                  silu_c[:, 2 * k:2 * k + 2], start=(k == 0), stop=(k == 7))
                    last.then_inc(ada_used, 1)
            norm_tensor(pe, NORM["n_ctx"])
            if STOP <= 1:
                return

            def ready(n):
                pe.wait_ge(low_ready, n + 1)

            pe.wait_ge(norm_done, NORM["n_x1"]["done"])
            for j in range(4):
                n = FIRST["q"] + j
                ready(n)
                tile_product(bank[:, j], n % RING, 0, H).then_inc(slot_used, 1)
            pe.wait_ge(norm_done, NORM["n_ctx"]["done"])
            for j in range(4):
                n = FIRST["k"] + j
                ready(n)
                pe.wait_ge(qkv_copied, j + 1)
                tile_product(bank[:, j], n % RING, 0, H)
                tile_product(bank[:, 4 + j, 0:CTX], n % RING, 0, HC).then_inc(slot_used, 1)
            pe.wait_ge(qkv_copied, 12)

            def token_major(stage, groups):
                for i in range(4):
                    n = FIRST[stage] + i
                    ready(n)
                    for kk in range(2):
                        k = 2 * i + kk
                        wh, wl = (r[:, n % RING, kk * 512:kk * 512 + 512] for r in (ring_high, ring_low))
                        for b, (ah, al), t in groups:
                            s = slice(t * P, (t + 1) * P)
                            last = product(bank[:, b], ah[:, k, s], al[:, k, s], wh, wl, k == 0, k == 7)
                    last.then_inc(slot_used, 1)

            token_major("v", [(t, (h_high, h_low), t) for t in range(TT)] + [(4 + t, (hc_high, hc_low), t) for t in range(CT)])
            pe.wait_ge(qkv_copied, 18)
            pe.wait_ge(rope_done, 8)
            att_tensor(pe, 0, ATT1)
            turn_tensor(pe, o_tok1, ATT1, 0)
            if STOP <= 2:
                return

            pe.wait_ge(filt_loaded, 16 * 5)
            pe.wait_ge(y_split, 4)
            mm(bank[0:FW, 0], w12f[0:EMB, 0, 0:FW], zt[0:EMB, 0], start=True, stop=True).then_inc(hid_made, 1)
            pe.wait_ge(hid_ready, 1)
            mm(bank[0:FW, 0], w12f[0:FW, 0, FW:2 * FW], hid[0:FW, 0], start=True, stop=True).then_inc(hid_made, 1)
            pe.wait_ge(hid_ready, 2)
            for n in range(2):
                for t in range(TT):
                    if 4 * n + t >= 2:
                        pe.wait_ge(filt_summed, 4 * n + t - 1)
                    for d in range(2):
                        last = mm(bank[:, 2 * (t % 2) + d], hid[0:FW, 1, t * P:(t + 1) * P], w3f[0:FW, 2 * d + n],
                                  start=True, stop=True)
                    last.then_inc(filt_made, 1)
                pe.wait_ge(filt_summed, 4 * n + 4)
                for f in range(4):
                    if 4 * n + f >= 2:
                        pe.wait_ge(k_copied, 4 * n + f - 1)
                    for d in range(2):
                        for t in range(TT):
                            last = mm(bank[:, 4 + 2 * (f % 2) + d], dft[:, 4 * d + t, f * P:(f + 1) * P], filt[:, 4 * d + t],
                                      start=(t == 0), stop=(t == 3))
                    last.then_inc(k_made, 1)

            with pe.Fori(0, 3) as part:
                for j in range(4):
                    n = FIRST["hyena_in"] + j
                    pe.wait_ge(low_ready, part * 4 + (n + 1))
                    pe.wait_ge(conv_done, part * 4 + (j + 1))
                    tile_product(bank[:, j], n % RING, 0, H).then_inc(slot_used, 1)
            pe.wait_ge(conv_done, 4 + 12)
            pe.wait_ge(k_copied, 8)
            for n in range(2):
                for t in range(TT):
                    for c in range(4):
                        last = nc.tensor.transpose(bank[:, t, c * P:(c + 1) * P], hyu[:, c, t * P:(t + 1) * P], ident[:, :])
                    last.then_inc(z_turned, 1)
                pe.wait_ge(z_copied, 4 * n + 4)
                pe.wait_ge(dft_loaded, 16)
                for f in range(4):
                    if 4 * n + f >= 2:
                        pe.wait_ge(y_made, 4 * n + f - 1)
                    for d in range(2):
                        for t in range(TT):
                            last = mm(bank[:, 4 + 2 * (f % 2) + d], dft[:, 4 * d + t, f * P:(f + 1) * P], z_tok[:, t],
                                      start=(t == 0), stop=(t == 3))
                    last.then_inc(u_made, 1)
                pe.wait_ge(y_made, 4 * n + 4)
                for c in range(4):
                    for f in range(4):
                        mm(bank[:, c], y_re[:, f, c * P:(c + 1) * P], dft[:, f], start=(f == 0), stop=False)
                        last = mm(bank[:, c], y_im[:, f, c * P:(c + 1) * P], dft[:, 4 + f], start=False, stop=(f == 3))
                    last.then_inc(z_back, 1)
                pe.wait_ge(z_done, 4 * n + 4)
            if STOP <= 3:
                return

            def merge_tensor(stage, branches, tiles):
                with pe.Fori(0, branches) as b:
                    for p in range(4):
                        q = 4 * (p % 2)
                        for i in range(2):
                            n = FIRST[stage] + 3 * p + i
                            pe.wait_ge(low_ready, b * 12 + (n + 1))
                            pe.wait_ge(merge_added, b * 8 + (tiles + 2 * p + i + 1))
                            tile_product(bank[:, q + i], n % RING, 0, H).then_inc(slot_used, 1)
                        n = FIRST[stage] + 3 * p + 2
                        pe.wait_ge(low_ready, b * 12 + (n + 1))
                        ys = [(y_high[:, bass.ds(b * 4 + k, 1)].rearrange("p a n -> p (a n)"),
                               y_low[:, bass.ds(b * 4 + k, 1)].rearrange("p a n -> p (a n)")) for k in range(4)]
                        for i in range(2):
                            last = tile_product(bank[:, q + 2 + i], n % RING, 4 * i, ys)
                        last.then_inc(slot_used, 1)

            def out_tensor(stage, tiles):
                with pe.Fori(0, 2) as i:
                    for j in range(4):
                        n = FIRST[stage] + j
                        pe.wait_ge(low_ready, i * 4 + (n + 1))
                        pe.wait_ge(out_added, i * 4 + (tiles + j + 1))
                        tile_product(bank[:, j], n % RING, 0, M_).then_inc(slot_used, 1)

            def up_tensor(stage, freed, before, each):
                with pe.Fori(0, 11) as i:
                    for q in range(2):
                        for g in range(2):
                            n = FIRST[stage] + 2 * q + g
                            pe.wait_ge(low_ready, i * 4 + (n + 1))
                            if g == 0:
                                pe.wait_ge(freed, i * (2 * each) + (before + each * (q + 1)))
                            tile_product(bank[:, 2 * q + g], n % RING, 0, H).then_inc(slot_used, 1)

            def down_tensor(stage):
                for half in range(2):
                    def one(n, hidden, wait, start, stop):
                        pe.wait_ge(low_ready, wait)
                        for kk in range(2):
                            ah, al = hidden(kk)
                            for m in range(4):
                                wh, wl = block_of(n % RING, 4 * kk + m)
                                last = product(bank[:, 4 * half + m], wh, wl, ah, al, start and kk == 0, stop and kk == 1)
                        last.then_inc(slot_used, 1)

                    base = FIRST[stage] + 11 * half
                    one(base, lambda kk: (hid_high[:, kk], hid_low[:, kk]), base + 1, True, False)
                    with pe.Fori(0, 2) as i:
                        for j in range(4):
                            def tiles(kk, j=j):
                                k = bass.ds(i * 8 + (2 * (1 + j) + kk), 1)
                                return tuple(t[:, k].rearrange("p a n -> p (a n)") for t in (hid_high, hid_low))
                            one(base + 1 + j, tiles, i * 4 + (base + 1 + j + 1), False, False)
                    for m in (9, 10):
                        one(base + m, lambda kk, m=m: (hid_high[:, 2 * m + kk], hid_low[:, 2 * m + kk]), base + m + 1,
                            False, m == 10)

            pe.wait_ge(y_split, 8)
            merge_tensor("merge1", 2, 0)
            pe.wait_ge(merge_low, 16)
            out_tensor("out1", 0)
            norm_tensor(pe, NORM["n_x2"])
            pe.wait_ge(norm_done, NORM["n_x2"]["done"])
            up_tensor("up1", up_prod, 0, 1)
            pe.wait_ge(up_low, 22)
            down_tensor("down1")
            if STOP <= 4:
                return
            pe.wait_ge(out_added, 4 + 16)
            norm_tensor(pe, NORM["n_final"])
            norm_tensor(pe, NORM["n_mem"])
            norm_tensor(pe, NORM["n_mix"])
            pe.wait_ge(norm_done, NORM["n_mix"]["done"])
            for j in range(4):
                n = FIRST["mem_k"] + j
                ready(n)
                tile_product(bank[:, j, 0:CTX], n % RING, 0, HM).then_inc(slot_used, 1)
            token_major("mem_v", [(4 + t, (hm_high, hm_low), t) for t in range(CT)])
            for j in range(14):
                n = FIRST["in2"] + j
                ready(n)
                pe.wait_ge(in_copied, j + 1 if j < 4 else IN_MEM + j - 3)
                tile_product(bank[:, j % 4], n % RING, 0, H).then_inc(slot_used, 1)
            for i in range(4):
                norm_tensor(pe, NORM[f"n_kx{i}"])
            for i in range(4):
                norm_tensor(pe, NORM[f"n_xq{i}"])
            pe.wait_ge(norm_done, NORM["n_xq3"]["done"])
            pe.wait_ge(in_copied, IN_IN2)
            att_tensor(pe, ATT1, ATT2)
            turn_tensor(pe, o_tok2, ATT2, 8)
            if STOP <= 5:
                return

            norm_tensor(pe, NORM["n_cq"])
            norm_tensor(pe, NORM["n_ckv"])
            pe.wait_ge(y_split, 12)
            pe.wait_ge(norm_done, NORM["n_ckv"]["done"])
            for j in range(4):
                n = FIRST["q_b"] + j
                ready(n)
                for i in range(2):
                    h = 2 * j + i
                    if h >= 4:
                        pe.wait_ge(in_copied, IN_IN2 + h - 3)
                    for k, (ah, al) in enumerate(CQ):
                        wh, wl = block_of(n % RING, 3 * i + k, DQK)
                        last = product(bank[0:DQK, h % 4], wh, wl, ah, al, k == 0, k == 2)
                last.then_inc(slot_used, 1)
            n = FIRST["kv_b"]
            ready(n)
            pe.wait_ge(in_copied, IN_QB)
            for m in range(4):
                last = tile_product(bank[:, m], n % RING, 2 * m, CKV)
            last.then_inc(slot_used, 1)
            ready(n + 1)
            for t in range(TT):
                for k in range(2):
                    s = slice(t * P, (t + 1) * P)
                    wh, wl = (r[:, (n + 1) % RING, k * 512:k * 512 + 512] for r in (ring_high, ring_low))
                    last = product(bank[:, 4 + t], ckv_high[:, k, s], ckv_low[:, k, s], wh, wl, k == 0, k == 1)
            last.then_inc(slot_used, 1)
            pe.wait_ge(in_copied, IN_V)
            for i in range(8):
                norm_tensor(pe, NORM[f"n_q{i}"])
            for i in range(8):
                norm_tensor(pe, NORM[f"n_k{i}"])
            pe.wait_ge(mla_roped, 2)
            pe.wait_ge(in_copied, IN_KR)
            att_tensor(pe, ATT2, ATT3)
            turn_tensor(pe, o_tok3, ATT3, 12)
            if STOP <= 6:
                return

            pe.wait_ge(y_split, 16)

            def s5_output(s):
                pe.wait_ge(s5_states, s + 1)
                i = s // 4
                if s % 4 == 0 and i >= 2:
                    pe.wait_ge(s5_y, i - 1)
                for r in range(2):
                    last = mm(bank[:, 4 + i % 2], cmat[:, s % 4, r * P:(r + 1) * P], s5s[:, r],
                              start=(s % 4 == 0 and r == 0), stop=(s % 4 == 3 and r == 1))
                last.then_inc(s5_out, 1)

            for s in range(ST):
                if s % 8 == 0:
                    pe.wait_ge(s5_b, 16 * (s // 8 + 1))
                if s >= 2:
                    pe.wait_ge(s5_rotated, s - 1)
                for r in range(2):
                    last = mm(bank[:, 2 * (s % 2) + r], bmat[:, 2 * r + s % 8 // 4, (s % 4) * P:(s % 4 + 1) * P],
                              u_ssm[:, s // 4], start=True, stop=True)
                last.then_inc(s5_in, 1)
                if s >= 1:
                    s5_output(s - 1)
            s5_output(ST - 1)
            pe.wait_ge(glu_low, 4)
            pe.wait_ge(s5_rotated, ST)
            for j in range(2):
                n = FIRST["glu"] + j
                ready(n)
                for i in range(2):
                    last = tile_product(bank[:, 2 * j + i], n % RING, 4 * i, GY)
                last.then_inc(slot_used, 1)
            pe.wait_ge(y_split, 20)
            if STOP <= 7:
                return
            merge_tensor("merge2", 3, 16)
            pe.wait_ge(merge_low, 16 + 24)
            out_tensor("out2", 16)
            norm_tensor(pe, NORM["n_ffn"])
            pe.wait_ge(norm_done, NORM["n_ffn"]["done"])
            up_tensor("up2", up_conv, 0, 2)
            pe.wait_ge(up_low, 44)
            down_tensor("down2")

        @block.vector
        def _(dve):
            link = Chain(dve, dve_step)
            tt, ts, stt = nc.vector.tensor_tensor, nc.vector.tensor_scalar, nc.vector.scalar_tensor_tensor
            MAGIC = 12582912.0
            TAU = (6.28125, 0.0019350051879882812, 3.019915981956753e-07)

            def reduce_angle(value, whole, last):
                link(ts(whole, value, 1.0 / (2 * math.pi), MAGIC, ALU.mult, ALU.add))
                link(ts(whole, whole, -MAGIC, None, ALU.add))
                for part in TAU:
                    link(stt(out=value, in0=whole, scalar=-part, in1=value, op0=ALU.mult, op1=ALU.add))
                return ts(last, value, 3.1415925, -3.1415925, ALU.min, ALU.max)

            dve.sem_inc(conv_done, 4)
            dve.sem_inc(merge_added, 4)
            dve.sem_inc(out_added, 4)
            dve.sem_inc(up_prod, 2)
            dve.sem_inc(up_conv, 4)

            dve.wait_ge(first_loaded, 48)
            dve.wait_ge(ada_used, ADA_SLOTS)
            mods = bank[:, 0, 0:2 * ADA_SLOTS].rearrange("p (m v) -> p v m", v=2)
            link(tt(mod[:, :], mods[:, 0], v_("b_ada", 0, 48), ALU.add))
            link(tt(mod_c[:, :], mods[:, 1, 0:16], v_("b_ada", 0, 16), ALU.add))
            link(stt(out=gain1[:, :], in0=mod[:, 8:16], scalar=1.0, in1=v_("norm1", 0, 8), op0=ALU.add, op1=ALU.mult))
            link(stt(out=gain1_c[:, :], in0=mod_c[:, 8:16], scalar=1.0, in1=v_("norm1", 0, 8), op0=ALU.add, op1=ALU.mult))
            stt(out=gain2[:, :], in0=mod[:, 32:40], scalar=1.0, in1=v_("norm2", 0, 8), op0=ALU.add, op1=ALU.mult) \
                .then_inc(mod_ready, 1)
            dve.wait_ge(mod_ready, 1)
            norm_vector(dve, link, NORM["n_x1"])
            norm_vector(dve, link, NORM["n_ctx"])
            if STOP <= 1:
                return

            dve.wait_ge(trig_loaded, 16)
            for src, dst, count in [(q_scaled, q_rot, lambda j: j + 1), (k_plain, k_rot, lambda j: 4 + 2 * j + 1)]:
                for j in range(4):
                    dve.wait_ge(qkv_copied, count(j))
                    link(nc.vector.stream_shuffle(rope_t[:, 0], src[:, j], mask=MASK_SWAP))
                    link(tt(rope_t[:, 0], rope_t[:, 0], trig1[:, 1], ALU.mult))
                    link(tt(rope_t[:, 1], src[:, j], trig1[:, 0], ALU.mult))
                    tt(dst[:, j], rope_t[:, 0], rope_t[:, 1], ALU.add).then_inc(rope_done, 1)
                    dve.wait_ge(rope_done, j + 1 if src is q_scaled else 5 + j)
            att_vector(dve, link, 0, ATT1)
            turn_vector(dve, 0, 0)
            if STOP <= 2:
                return

            dve.wait_ge(filt_loaded, 16 * 5)
            for i in range(2):
                dve.wait_ge(hid_made, i + 1)
                if i:
                    dve.wait_ge(hid_ready, 1)
                link(ts(arg[0:FW, 0], bank[0:FW, 0], v_(f"hy_b{i + 1}", 0, 1, 0, FW), v_("hy_freq", 0, 1, 0, FW), ALU.add, ALU.mult))
                reduce_angle(arg[0:FW, 0], arg[0:FW, 1], arg[0:FW, 0]).then_inc(arg_ready, 1)
            dve.wait_ge(hid_ready, 2)
            for n in range(2):
                for t in range(TT):
                    dve.wait_ge(filt_made, 4 * n + t + 1)
                    if n and t == 0:
                        dve.wait_ge(k_made, 4)
                    b = 2 * (t % 2)
                    link(tt(arg[:, 0], bank[:, b], decay[:, t], ALU.mult))
                    link(tt(arg[:, 1], bank[:, b + 1], decay[:, t], ALU.mult))
                    if t == 0:
                        link(nc.vector.memset(arg[0:1, 1], 0.0))
                    link(tt(filt[:, t], arg[:, 0], arg[:, 1], ALU.add))
                    tt(filt[:, 4 + t], arg[:, 0], arg[:, 1], ALU.subtract).then_inc(filt_summed, 1)
                    dve.wait_ge(filt_summed, 4 * n + t + 1)

            with dve.Fori(0, 3) as part:
                start = link.count
                link.count = start + part * 4
                for j in range(4):
                    dve.wait_ge(conv_centre, part * 4 + (j + 1))
                    tile = bass.ds(part * 4 + j, 1)
                    later = hyu[:, tile, 1:T].rearrange("p a n -> p (a n)")
                    sooner = hyu[:, tile, 0:T - 1].rearrange("p a n -> p (a n)")
                    w0, w2 = (VECTOR_AT["hy_conv_w"][0] + tap * 12 + j for tap in (0, 2))
                    link(stt(out=later, in0=bank[:, j, 0:T - 1], scalar=vec[:, bass.ds(part * 4 + w0, 1)], in1=later,
                             op0=ALU.mult, op1=ALU.add))
                    stt(out=sooner, in0=bank[:, j, 1:T], scalar=vec[:, bass.ds(part * 4 + w2, 1)], in1=sooner,
                        op0=ALU.mult, op1=ALU.add).then_inc(conv_done, 1)
            link.count = start + 12
            dve.wait_ge(conv_done, 4 + 12)
            dve.wait_ge(k_copied, 8)
            for n in range(2):
                for f in range(4):
                    dve.wait_ge(u_made, 4 * n + f + 1)
                    b = 4 + 2 * (f % 2)
                    kre, kim = spec[n][:, f], spec[n][:, 4 + f]
                    link(tt(y_re[:, f], bank[:, b], kre, ALU.mult))
                    link(tt(hyt[:, 0], bank[:, b + 1], kim, ALU.mult))
                    link(tt(y_re[:, f], y_re[:, f], hyt[:, 0], ALU.subtract))
                    link(tt(y_im[:, f], bank[:, b], kim, ALU.mult))
                    link(tt(hyt[:, 1], bank[:, b + 1], kre, ALU.mult))
                    tt(y_im[:, f], y_im[:, f], hyt[:, 1], ALU.add).then_inc(y_made, 1)
                    dve.wait_ge(y_made, 4 * n + f + 1)
                for c in range(4):
                    dve.wait_ge(z_back, 4 * n + c + 1)
                    link(stt(out=hyz[:, c], in0=hyu[:, c], scalar=v_("hy_bias", 4 * n + c), in1=bank[:, c],
                             op0=ALU.mult, op1=ALU.add))
                    dst = hyu[:, c] if n == 0 else hyz[:, c]
                    tt(dst, hyz[:, c], hyu[:, 4 + 4 * n + c], ALU.mult).then_inc(z_done, 1)
                    dve.wait_ge(z_done, 4 * n + c + 1)
            for c in range(4):
                dve.wait_ge(y_rounded, 4 + c + 1)
                tt(y_low[:, 4 + c], hyz[:, c], y_high[:, 4 + c], ALU.subtract).then_inc(y_split, 1)
            dve.wait_ge(y_split, 8)
            if STOP <= 3:
                return

            def merge_vector(stage, branches, tiles):
                link(nc.vector.memset(merged[:, :, :].rearrange("p a n -> p (a n)"), 0.0))
                start = link.count
                with dve.Fori(0, branches) as b:
                    link.count = start + b * 8
                    for p in range(4):
                        q = 4 * (p % 2)
                        dve.wait_ge(slot_used, b * 12 + (FIRST[stage] + 3 * p + 3))
                        for i in range(2):
                            g = 2 * p + i
                            dve.wait_ge(merge_sig, b * 8 + (tiles + g + 1))
                            link(tt(mprod[:, i], sig[:, i], bank[:, q + 2 + i], ALU.mult))
                            tt(merged[:, g], merged[:, g], mprod[:, i], ALU.add).then_inc(merge_added, 1)
                        for i in range(2):
                            g = 2 * p + i
                            dve.wait_ge(merge_rounded, b * 8 + (tiles + g + 1))
                            tt(m_low[:, g], merged[:, g], m_high[:, g], ALU.subtract).then_inc(merge_low, 1)
                link.count = start + branches * 8
                dve.wait_ge(merge_low, tiles + branches * 8)

            def add_to_x(k, b, gate):
                xk = x[:, k] if isinstance(k, int) else x[:, bass.ds(k, 1)].rearrange("p a n -> p (a n)")
                if gate is None:
                    return tt(xk, xk, bank[:, b], ALU.add)
                g = mod[:, gate + k:gate + k + 1] if isinstance(k, int) else mod[:, bass.ds(k + gate, 1)]
                return stt(out=xk, in0=bank[:, b], scalar=g, in1=xk, op0=ALU.mult, op1=ALU.add)

            def out_vector(stage, gate):
                with dve.Fori(0, 2) as i:
                    for j in range(4):
                        dve.wait_ge(slot_used, i * 4 + (FIRST[stage] + j + 1))
                        add_to_x(i * 4 + j, j, gate).then_inc(out_added, 1)

            def down_vector(stage, gate):
                for half in range(2):
                    dve.wait_ge(slot_used, FIRST[stage] + 11 * (half + 1))
                    for m in range(4):
                        add_to_x(4 * half + m, 4 * half + m, gate).then_inc(out_added, 1)

            merge_vector("merge1", 2, 0)
            dve.wait_ge(x_loaded, 32)
            out_vector("out1", 16)
            norm_vector(dve, link, NORM["n_x2"])
            with dve.Fori(0, 11) as i:
                for q in range(2):
                    hidden = bass.ds(i * 2 + q, 1)
                    dve.wait_ge(up_gate, i * 2 + (q + 1))
                    dve.wait_ge(slot_used, i * 4 + (FIRST["up1"] + 2 * q + 2))
                    tt(ff_p[:, q], ff_s[:, q], bank[:, 2 * q + 1], ALU.mult).then_inc(up_prod, 1)
                    dve.wait_ge(up_rounded, i * 2 + (q + 1))
                    tt(hid_low[:, hidden].rearrange("p a n -> p (a n)"), ff_p[:, q],
                       hid_high[:, hidden].rearrange("p a n -> p (a n)"), ALU.subtract).then_inc(up_low, 1)
                    dve.wait_ge(up_low, i * 2 + (q + 1))
            down_vector("down1", 40)
            if STOP <= 4:
                return

            norm_vector(dve, link, NORM["n_final"])
            norm_vector(dve, link, NORM["n_mem"])
            norm_vector(dve, link, NORM["n_mix"])
            for i in range(4):
                norm_vector(dve, link, NORM[f"n_kx{i}"])
            for i in range(4):
                norm_vector(dve, link, NORM[f"n_xq{i}"])
            dve.wait_ge(mask_loaded, 16)
            att_vector(dve, link, ATT1, ATT2)
            turn_vector(dve, 2, 8)
            if STOP <= 5:
                return

            norm_vector(dve, link, NORM["n_cq"])
            norm_vector(dve, link, NORM["n_ckv"])
            for i in range(8):
                norm_vector(dve, link, NORM[f"n_q{i}"])
            for i in range(8):
                norm_vector(dve, link, NORM[f"n_k{i}"])
            dve.wait_ge(pos_loaded, 16)
            rw = [rope_w[64:96, i] for i in range(4)]
            link(nc.vector.tensor_copy(rw[0], pos_i[64:96, 0]))
            link(ts(rw[0], rw[0], v_("inv_freq", 0, 1, 64, 96), None, ALU.mult))
            reduce_angle(rw[0], rw[1], rw[3]).then_inc(rope_arg, 1)
            dve.wait_ge(rope_sin, 1)
            link(ts(rope2[64:96, 1], rope2[64:96, 1], v_("rope_sign", 0, 1, 64, 96), None, ALU.mult))
            link(ts(rw[0], rw[3], math.pi / 2, None, ALU.add))
            reduce_angle(rw[0], rw[1], rw[3]).then_inc(rope_arg, 1)
            dve.wait_ge(rope_sin, 2)
            for which, heads in enumerate(([qh[64:96, h] for h in range(8)], [k_head[h][64:96] for h in range(8)])):
                if which:
                    dve.wait_ge(mla_roped, 1)
                for h in range(8):
                    link(nc.vector.stream_shuffle(rw[0], heads[h], mask=MASK_SWAP))
                    link(tt(rw[0], rw[0], rope2[64:96, 1], ALU.mult))
                    link(tt(rw[1], heads[h], rope2[64:96, 0], ALU.mult))
                    if h < 7:
                        link(tt(heads[h], rw[0], rw[1], ALU.add))
                    else:
                        tt(heads[h], rw[0], rw[1], ALU.add).then_inc(mla_roped, 1)
            dve.wait_ge(mla_roped, 2)
            att_vector(dve, link, ATT2, ATT3)
            turn_vector(dve, 0, 12)
            if STOP <= 6:
                return

            def s5v(i, n=16):
                return s5[:, 16 * i:16 * i + n]

            LOG2E, LN2_HIGH, LN2_LOW = 1.4426950408889634, 0.693359375, -2.12194440e-4

            def exact_exp(dst, src, whole, rest, poly):
                bias = MAGIC + 127.0
                link(ts(rest, src, 88.0, -87.0, ALU.min, ALU.max))
                link(ts(whole, rest, LOG2E, bias, ALU.mult, ALU.add))
                link(ts(poly, whole, -bias, None, ALU.add))
                link(stt(out=rest, in0=poly, scalar=-LN2_HIGH, in1=rest, op0=ALU.mult, op1=ALU.add))
                link(stt(out=rest, in0=poly, scalar=-LN2_LOW, in1=rest, op0=ALU.mult, op1=ALU.add))
                link(ts(whole.bitcast(I32), whole.bitcast(I32), 23, None, ALU.logical_shift_left))
                link(ts(poly, rest, 1.0 / math.factorial(7), None, ALU.mult))
                for d in range(6, 0, -1):
                    link(stt(out=poly, in0=poly, scalar=1.0 / math.factorial(d), in1=rest, op0=ALU.add, op1=ALU.mult))
                link(stt(out=dst, in0=poly, scalar=1.0, in1=whole, op0=ALU.add, op1=ALU.mult))

            DT, TH, WH, RE, PO, AN, SI, CO, MAG, ARE, AIM, DEN, FRE, FIM, PR, PI_, NPR, NPI, NFI = range(19)
            exact_exp(s5v(DT), v_("log_dt", 0, 16), s5v(WH), s5v(RE), s5v(PO))
            link(tt(s5v(TH), v_("lam_im", 0, 16), s5v(DT), ALU.mult))
            reduce_angle(s5v(TH), s5v(WH), s5v(AN)).then_inc(s5_arg, 1)
            dve.wait_ge(s5_sin, 1)
            link(ts(s5v(TH), s5v(AN), math.pi / 2, None, ALU.add))
            reduce_angle(s5v(TH), s5v(WH), s5v(AN)).then_inc(s5_arg, 1)
            link(tt(s5v(ARE), v_("lam_re", 0, 16), s5v(DT), ALU.mult))
            exact_exp(s5v(MAG), s5v(ARE), s5v(WH), s5v(RE), s5v(PO))
            dve.wait_ge(s5_sin, 2)
            lr, li = v_("lam_re", 0, 16), v_("lam_im", 0, 16)
            link(tt(s5v(ARE), s5v(MAG), s5v(CO), ALU.mult))
            link(ts(s5v(ARE), s5v(ARE), -1.0, None, ALU.add))
            link(tt(s5v(AIM), s5v(MAG), s5v(SI), ALU.mult))
            link(tt(s5v(DEN), lr, lr, ALU.mult))
            link(tt(s5v(WH), li, li, ALU.mult))
            link(tt(s5v(DEN), s5v(DEN), s5v(WH), ALU.add))
            link(nc.vector.reciprocal(s5v(DEN), s5v(DEN)))
            link(tt(s5v(FRE), s5v(ARE), lr, ALU.mult))
            link(tt(s5v(WH), s5v(AIM), li, ALU.mult))
            link(tt(s5v(FRE), s5v(FRE), s5v(WH), ALU.add))
            link(tt(s5v(FRE), s5v(FRE), s5v(DEN), ALU.mult))
            link(tt(s5v(FIM), s5v(AIM), lr, ALU.mult))
            link(tt(s5v(WH), s5v(ARE), li, ALU.mult))
            link(tt(s5v(FIM), s5v(FIM), s5v(WH), ALU.subtract))
            link(tt(s5v(FIM), s5v(FIM), s5v(DEN), ALU.mult))
            link(ts(s5v(NFI), s5v(FIM), -1.0, None, ALU.mult))

            def tables(group):
                s = slice(4 * (group % 2), 4 * (group % 2) + 4)
                pr, pi, npr, npi = (s5[:, 16 * i + 4 * group:16 * i + 4 * group + 4] for i in (PR, PI_, NPR, NPI))
                link(nc.vector.tensor_copy(pr, s5[:, 16 * CO + 4 * group:16 * CO + 4 * group + 4]))
                link(nc.vector.tensor_copy(pi, s5[:, 16 * SI + 4 * group:16 * SI + 4 * group + 4]))
                link(nc.vector.memset(tab_re[:, s, 0:1], 1.0))
                link(nc.vector.memset(tab_im[:, s, 0:1], 0.0))
                m = 1
                while m < T:
                    old_re, old_im = tab_re[:, s, 0:m], tab_im[:, s, 0:m]
                    new_re, new_im = tab_re[:, s, m:2 * m], tab_im[:, s, m:2 * m]
                    tmp = s5t[:, :, :].rearrange("p a n -> p (a n)")[:, 0:4 * m].rearrange("p (a n) -> p a n", a=4)
                    br, bi = (v.rearrange("p (a n) -> p a n", n=1).to_broadcast([P, 4, m]) for v in (pr, pi))
                    link(tt(new_re, old_re, br, ALU.mult))
                    link(tt(tmp, old_im, bi, ALU.mult))
                    link(tt(new_re, new_re, tmp, ALU.subtract))
                    link(tt(new_im, old_re, bi, ALU.mult))
                    link(tt(tmp, old_im, br, ALU.mult))
                    link(tt(new_im, new_im, tmp, ALU.add))
                    m *= 2
                    if m < T:
                        link(tt(npr, pr, pr, ALU.mult))
                        link(tt(npi, pi, pi, ALU.mult))
                        link(tt(npr, npr, npi, ALU.subtract))
                        link(tt(npi, pr, pi, ALU.mult))
                        link(ts(pi, npi, 2.0, None, ALU.mult))
                        link(nc.vector.tensor_copy(pr, npr))

            for s in range(ST):
                if s % 8 == 0:
                    tables(s // 4)
                    tables(s // 4 + 1)
                e_re, e_im = tab_re[:, s % 8], tab_im[:, s % 8]
                b = 2 * (s % 2)
                dve.wait_ge(s5_in, s + 1)
                link(tt(s5r[:, 0], bank[:, b], e_re, ALU.mult))
                link(tt(s5t[:, 0], bank[:, b + 1], e_im, ALU.mult))
                link(tt(s5r[:, 0], s5r[:, 0], s5t[:, 0], ALU.add))
                link(tt(s5r[:, 1], bank[:, b + 1], e_re, ALU.mult))
                link(tt(s5t[:, 0], bank[:, b], e_im, ALU.mult))
                tt(s5r[:, 1], s5r[:, 1], s5t[:, 0], ALU.subtract).then_inc(s5_rotated, 1)
                dve.wait_ge(s5_rotated, s + 1)
                decay_b = s5[:, 16 * MAG + s:16 * MAG + s + 1].to_broadcast([P, T])
                for r in range(2):
                    link(nc.vector.tensor_tensor_scan(s5t[:, r], decay_b, s5r[:, r], 0.0, ALU.mult, ALU.add))
                dve.wait_ge(s5_c[s % 4], 16 * (s // 4 + 1))
                c_re, c_im = cmat[:, s % 4, 0:P], cmat[:, s % 4, P:2 * P]
                f_re, f_im, nf_im = (s5[:, 16 * i + s:16 * i + s + 1] for i in (FRE, FIM, NFI))
                link(ts(s5r[:, 0, 0:P], c_im, f_im, None, ALU.mult))
                link(ts(s5r[:, 0, P:2 * P], c_im, f_re, None, ALU.mult))
                link(stt(out=c_im, in0=c_re, scalar=nf_im, in1=s5r[:, 0, P:2 * P], op0=ALU.mult, op1=ALU.subtract))
                link(stt(out=c_re, in0=c_re, scalar=f_re, in1=s5r[:, 0, 0:P], op0=ALU.mult, op1=ALU.subtract))
                if s:
                    dve.wait_ge(s5_out, s)
                link(tt(s5s[:, 0], s5t[:, 0], e_re, ALU.mult))
                link(tt(s5r[:, 0], s5t[:, 1], e_im, ALU.mult))
                link(tt(s5s[:, 0], s5s[:, 0], s5r[:, 0], ALU.subtract))
                link(tt(s5s[:, 1], s5t[:, 0], e_im, ALU.mult))
                link(tt(s5r[:, 0], s5t[:, 1], e_re, ALU.mult))
                tt(s5s[:, 1], s5s[:, 1], s5r[:, 0], ALU.add).then_inc(s5_states, 1)
                dve.wait_ge(s5_states, s + 1)
                if s % 4 == 3:
                    i = s // 4
                    dve.wait_ge(s5_out, s + 1)
                    stt(out=gy[:, i], in0=u_ssm[:, i], scalar=v_("ssm_d", i), in1=bank[:, 4 + i % 2],
                        op0=ALU.mult, op1=ALU.add).then_inc(s5_y, 1)
            for c in range(4):
                dve.wait_ge(glu_rounded, c + 1)
                tt(gy_low[:, c], gy[:, c], gy_high[:, c], ALU.subtract).then_inc(glu_low, 1)
            for c in range(4):
                dve.wait_ge(glu_sig, c + 1)
                tt(gprod[:, c % 2], gsig[:, c % 2], gy[:, c], ALU.mult).then_inc(glu_prod, 1)
                dve.wait_ge(y_rounded, 16 + c + 1)
                tt(y_low[:, 4 + c], gprod[:, c % 2], y_high[:, 4 + c], ALU.subtract).then_inc(y_split, 1)
            dve.wait_ge(y_split, 20)
            if STOP <= 7:
                return

            merge_vector("merge2", 3, 16)
            out_vector("out2", None)
            norm_vector(dve, link, NORM["n_ffn"])
            start = link.count
            with dve.Fori(0, 11) as i:
                link.count = start + i * 4
                for q in range(2):
                    hidden = bass.ds(i * 2 + q, 1)
                    for g, dst in ((0, ff_a), (1, ff_v)):
                        dve.wait_ge(up_centre, i * 4 + (2 * q + g + 1))
                        w0, w1 = (VECTOR_AT["conv_w"][0] + 44 * tap + 22 * g + q for tap in (0, 1))
                        link(stt(out=dst[:, q, 1:T], in0=bank[:, 2 * q + g, 0:T - 1], scalar=vec[:, bass.ds(i * 2 + w1, 1)],
                                 in1=dst[:, q, 1:T], op0=ALU.mult, op1=ALU.add))
                        stt(out=dst[:, q, 2:T], in0=bank[:, 2 * q + g, 0:T - 2], scalar=vec[:, bass.ds(i * 2 + w0, 1)],
                            in1=dst[:, q, 2:T], op0=ALU.mult, op1=ALU.add).then_inc(up_conv, 1)
                    dve.wait_ge(up_conv, i * 4 + (4 + 2 * q + 2))
                    dve.wait_ge(up_gate, i * 2 + (22 + q + 1))
                    tt(ff_p[:, q], ff_s[:, q], ff_v[:, q], ALU.mult).then_inc(up_prod, 1)
                    dve.wait_ge(up_rounded, i * 2 + (22 + q + 1))
                    tt(hid_low[:, hidden].rearrange("p a n -> p (a n)"), ff_p[:, q],
                       hid_high[:, hidden].rearrange("p a n -> p (a n)"), ALU.subtract).then_inc(up_low, 1)
            link.count = start + 44
            down_vector("down2", None)
    return locals()


INS = ["x", "ctx", "mem", "stream", "vectors", "ones", "identity", "trig1", "bias", "hy_w3", "hy_z", "hy_w12", "decay",
       "dft1", "dft2", "cmask", "positions", "ssm_b", "ssm_c"]


def constants():
    out = {"ones": np.ones((P, P), np.float32), "identity": np.eye(P, dtype=np.float32)}
    t = np.arange(T)
    nf = HD // 4
    inv = 10000.0 ** (-np.arange(nf, dtype=np.float32) / nf)
    trig = np.zeros((P, 2, T), np.float32)
    for p in range(P):
        d = p % HD
        pos = (t // GRID_W if d < HD // 2 else t % GRID_W).astype(np.float32)
        ang = (pos * np.float32(inv[d % nf])).astype(np.float32).astype(np.float64)
        trig[p, 0] = np.cos(ang)
        trig[p, 1] = np.sin(ang) * (-1 if d % 32 < nf else 1)
    out["trig1"] = trig
    f32 = np.float32
    tl = np.linspace(0.0, 1.0, T, dtype=f32)
    w = (2.0 * math.pi * np.arange(T, dtype=f32) / T).astype(f32)
    bands = np.linspace(1e-4, (EMB - 1) // 2 - 1, (EMB - 1) // 2, dtype=f32)
    arg = (bands[:, None] * w[None, :]).astype(f32)
    out["hy_z"] = np.concatenate([tl[None], np.cos(arg), np.sin(-arg)], 0).astype(f32)
    deltas = np.abs(np.linspace(math.log(1e-2) / 1.5, math.log(1e-2) / 0.3, HYW, dtype=f32))
    out["decay"] = np.exp(-tl[:, None] * deltas[None, :]).astype(f32).reshape(TT, P, HYW).transpose(1, 0, 2).copy()
    n = np.arange(T, dtype=np.float64)
    for name, shift in (("dft1", 0.0), ("dft2", 0.5)):
        ang = 2 * math.pi * np.outer(n + shift, n + 0.5) / (2 * T)
        both = np.stack([np.cos(ang), np.sin(ang)]).astype(f32)
        out[name] = both.reshape(2, TT, P, T).transpose(2, 0, 1, 3).reshape(P, 8, T).copy()
    mask = np.zeros((P, T), f32)
    mask[:, T - P:] = np.where(np.arange(P)[None, :] <= np.arange(P)[:, None], 0.0, NEG)
    out["cmask"] = mask
    return out


def k_tiles(w, columns=P):
    k, n = w.shape
    return w.reshape(k // P, P, n).transpose(1, 0, 2)


def slots_by_tile(w):
    k, n = w.shape
    return w.reshape(k // P, P, n // P, P).transpose(2, 1, 0, 3).reshape(n // P, P, -1)


def slots_of(w, k_each, n_all):
    k, n = w.shape
    return w.reshape(k // P // k_each, k_each, P, n).transpose(0, 2, 1, 3).reshape(-1, P, k_each * n)


def slots_down(w):
    return np.concatenate([slots_of(np.ascontiguousarray(w[:, h * 512:h * 512 + 512]), 2, 512) for h in range(2)])


def slots_pairs(w1, w2):
    s1, s2 = slots_by_tile(w1), slots_by_tile(w2)
    return np.stack([s1, s2], 1).reshape(-1, P, SLOT)


def slots_merge(gates, outs):
    parts = []
    for g, o in zip(gates, outs):
        gs = slots_by_tile(g)
        os_ = slots_by_tile(o).reshape(4, 2, P, 512).transpose(0, 2, 1, 3).reshape(4, P, SLOT)
        for p in range(4):
            parts += [gs[2 * p:2 * p + 1], gs[2 * p + 1:2 * p + 2], os_[p:p + 1]]
    return np.concatenate(parts)


def padded(blocks, n=SLOT):
    out = np.zeros((1, P, n), blocks.dtype)
    out[0, :, :blocks.shape[1]] = blocks
    return out


def feature_columns(v):
    v = np.asarray(v).reshape(-1)
    if v.size % P:
        out = np.zeros((P, 1), np.float32)
        out[:v.size, 0] = v
        return out
    return v.reshape(-1, P).T


def lay_out(i):
    i = {k: np.asarray(v) for k, v in i.items()}
    d = constants()

    def tokens(v):
        return v[0].T.reshape(KD, P, -1).transpose(1, 0, 2).copy()

    d["x"], d["ctx"], d["mem"] = tokens(i["x"]), tokens(i["ctx"]), tokens(i["mem_2"])
    d["positions"] = i["positions_2"].astype(np.int32).reshape(T)

    w_in = i["w_in"][0]
    part = lambda w, lo, n: np.ascontiguousarray(w[:, lo:lo + n])
    st = [slots_by_tile(i["w_ada"][0]), slots_by_tile(part(w_in, 0, 512)), slots_by_tile(part(w_in, 512, 512)),
          slots_of(part(w_in, 1024, 512), 2, 512), slots_by_tile(part(w_in, 1536, 1536)),
          slots_merge([part(w_in, 3072, 1024), part(w_in, 4096, 1024)], [i["w_na_o"][0], i["w_hy_o"][0]]),
          slots_by_tile(i["w_out"][0]), slots_pairs(i["ffn_w1"][0], i["ffn_w3"][0]), slots_down(i["ffn_w2"][0])]
    w_mem = i["w_mem_kv_2"][0]
    st += [slots_by_tile(part(w_mem, 0, 512)), slots_of(part(w_mem, 512, 512), 2, 512)]
    w2 = i["w_in_2"][0]
    kr = np.zeros((D, P), np.float32)
    kr[:, 64:96] = w2[:, QL + KVL:QL + KVL + DROPE]
    o = QL + KVL + DROPE
    st += [slots_by_tile(part(w2, 0, QL + KVL)), slots_by_tile(kr), slots_by_tile(part(w2, o + 512, 512)),
           slots_by_tile(part(w2, o, 512))]
    qb = k_tiles(i["w_q_b_2"][0]).reshape(P, 3, HEADS, DQK)
    for j in range(4):
        blocks = np.zeros((P, 2, 3, P), np.float32)
        blocks[:, :, :, :DQK] = qb[:, :, 2 * j:2 * j + 2].transpose(0, 2, 1, 3)
        st.append(padded(blocks.reshape(P, -1)))
    kvb = k_tiles(i["w_kv_b_2"][0]).reshape(P, 2, HEADS, 2, 64)
    st.append(kvb[:, :, :, 0].reshape(P, 2, 4, P).transpose(0, 2, 1, 3).reshape(1, P, SLOT))
    st.append(kvb[:, :, :, 1].reshape(1, P, SLOT))
    st.append(slots_by_tile(i["w_glu_2"][0]).reshape(2, 2, P, 512).transpose(0, 2, 1, 3).reshape(2, P, SLOT))
    gates = o + 1024
    st += [slots_merge([part(w2, gates + 1024 * b, 1024) for b in range(3)],
                       [i["w_o_mla_2"][0], i["w_o_ssm_2"][0], i["w_o_cross_2"][0]]),
           slots_by_tile(i["w_out_2"][0]), slots_pairs(part(i["w_up_2"][0], 0, FF), part(i["w_up_2"][0], FF, FF)),
           slots_down(i["w_down_2"][0])]
    d["stream"] = np.concatenate(st)
    assert d["stream"].shape == (ADA_SLOTS + NS, P, SLOT), d["stream"].shape

    rpb = i["na_rpb"][0]
    cq_ = np.arange(GRID_W)
    start = np.clip(cq_ - WIN_W // 2, 0, GRID_W - WIN_W)
    bias = np.full((HEADS, 2, GRID_W, TAPS, GRID_W), NEG, np.float32)
    for c in range(GRID_W):
        lo = start[c]
        for rr in range(2):
            rows = np.arange(TAPS) + 1 - rr
            bias[:, rr, c, :, lo:lo + WIN_W] = rpb[:, rows][:, :, lo - c + WIN_W - 1:lo - c + WIN_W - 1 + WIN_W]
    d["bias"] = bias.reshape(HEADS, P, TAPS * GRID_W)

    w3 = i["hy_ffn_w3"][0]
    d["hy_w3"] = w3.reshape(FW, 4, HYW).copy()
    w12 = np.zeros((FW, 2 * FW), np.float32)
    w12[:EMB, :FW] = i["hy_ffn_w1"][0]
    w12[:, FW:] = i["hy_ffn_w2"][0]
    d["hy_w12"] = w12

    b_all = np.zeros((2, ST, P, P), np.float32)
    c_all = np.zeros((ST, P, 2, P), np.float32)
    for r, (bn, cn) in enumerate((("ssm_b_re_2", "ssm_c_re_2"), ("ssm_b_im_2", "ssm_c_im_2"))):
        bm, cm = i[bn][0], i[cn][0]
        for g in range(32):
            s, half, ch = g // 2, g % 2, (g % 8) * 16
            b_all[r, s, ch:ch + 16, half * 64:half * 64 + 64] = bm[g].T
            c_all[s, half * 64:half * 64 + 64, r, ch:ch + 16] = cm[g].T
    d["ssm_b"] = b_all.reshape(2, 2, 8, P, P).transpose(1, 3, 0, 2, 4).reshape(2, P, 4, 512).copy()
    d["ssm_c"] = c_all.reshape(ST, P, 2 * P)

    sign = np.zeros(P, np.float32)
    sign[64:80], sign[80:96] = -1.0, 1.0
    freq = np.zeros(P, np.float32)
    inv = (np.float32(10000.0) ** (-np.arange(0, DROPE, 2, dtype=np.float32) / np.float32(DROPE))).astype(np.float32)
    freq[64:96] = np.tile(inv, 2)
    named = {
        "c": i["c"], "c_ctx": i["c_ctx"], "b_ada": i["b_ada"], "norm1": i["norm1_g"], "norm2": i["norm2_g"],
        "final": i["final_g"], "norm_mix": i["norm_mix_g_2"], "mem_norm": i["mem_norm_g_2"], "norm_ffn": i["norm_ffn_g_2"],
        "hy_conv_w": i["hy_conv_w"], "hy_conv_b": i["hy_conv_b"], "hy_bias": i["hy_bias"], "hy_b1": i["hy_ffn_b1"],
        "hy_b2": i["hy_ffn_b2"], "hy_freq": i["hy_sin_freq"], "conv_w": i["conv_w_2"], "conv_b": i["conv_b_2"],
        "b_gate": i["b_gate_2"], "b_glu": i["b_glu_2"], "q_a": i["q_a_norm_g_2"], "kv_a": i["kv_a_norm_g_2"],
        "q_norm": i["q_norm_g_2"], "k_norm": i["k_norm_g_2"], "xq": i["xq_norm_g_2"], "xk": i["xk_norm_g_2"],
        "lam_re": i["ssm_lambda_re_2"], "lam_im": i["ssm_lambda_im_2"],
        "log_dt": np.repeat(i["ssm_log_dt_2"].reshape(32, 1), NSTATE, 1), "ssm_d": i["ssm_d_2"],
        "inv_freq": freq, "rope_sign": sign, "zero": np.zeros(8 * P, np.float32), "half_pi": np.zeros(P, np.float32),
    }
    columns = [feature_columns(named[name]) for name, _ in VECTORS]
    assert [c.shape[1] for c in columns] == [n for _, n in VECTORS]
    d["vectors"] = np.concatenate(columns, 1).astype(np.float32, copy=False)
    return {k: np.ascontiguousarray(d[k]) for k in INS}


def kernel(**inputs):
    import concourse.bacc as bacc
    from concourse.bass_utils import run_bass_kernel_spmd

    arrays = lay_out(inputs)
    nc = bacc.Bacc("TRN2", target_bir_lowering=False, num_devices=1)
    aps = {k: nc.dram_tensor(f"in_{k}", v.shape, mybir.dt.from_np(v.dtype), kind="ExternalInput").ap()
           for k, v in arrays.items()}
    out = nc.dram_tensor("out_0", (KD, P, T), F32, kind="ExternalOutput").ap()
    build(nc, aps, out)
    r = run_bass_kernel_spmd(nc, [{f"in_{k}": v for k, v in arrays.items()}], core_ids=[0])
    y = r.results[0]["out_0"]
    return np.ascontiguousarray(y.reshape(D, T).T)[None]
```

```python
import math
from contextlib import ExitStack

import numpy as np

import concourse.bass as bass
from concourse import mybir

F32 = mybir.dt.float32
F32R = mybir.dt.float32r
I32 = mybir.dt.int32
ALU = mybir.AluOpType
ACT = mybir.ActivationFunctionType
AX = mybir.AxisListType

P = 128
T = 512
TT = T // P
D = 1024
KD = D // P
CTX = 256
CT = CTX // P
HEADS = 8
HD = 64
GRID_W = 64
GRID_R = T // GRID_W
WIN_H, WIN_W = 8, 16
NEG = -1e30
HYW = 512
HT = HYW // P
EMB = 33
FW = 64
FF = 2816
FT = FF // P
QL, KVL = 384, 256
DQK, DNOPE, DROPE, DV = 96, 64, 32, 64
XH = 4
NSTATE = 64
ST = 16
LOW = 32
RING = 4
SLOT = 1024
EPS = 1e-6
TAPS = 14

VECTORS = [
    ("b_ada", 48), ("norm1", 8), ("norm2", 8), ("final", 8), ("norm_mix", 8),
    ("mem_norm", 8), ("norm_ffn", 8), ("hy_conv_w", 36), ("hy_conv_b", 12), ("hy_bias", 8),
    ("hy_b1", 1), ("hy_b2", 1), ("hy_freq", 1), ("conv_w", 132), ("conv_b", 44), ("b_gate", 24),
    ("b_glu", 4), ("q_a", 3), ("kv_a", 2), ("q_norm", 1), ("k_norm", 1), ("xq", 1), ("xk", 1),
    ("lam_re", 16), ("lam_im", 16), ("log_dt", 16), ("ssm_d", 4), ("inv_freq", 1), ("rope_sign", 1),
    ("zero", 8), ("eps", 1),
]
VECTOR_AT = {}
NV = 0
for _name, _n in VECTORS:
    VECTOR_AT[_name] = (NV, _n)
    NV += _n

ADA_SLOTS = 48
ADA_FIRST = 16
LATE_RING = 4
STAGES = [
    ("q", 4), ("k", 4), ("v", 4), ("hyena_in", 12), ("merge1", 24), ("out1", 8), ("up1", 44),
    ("down1", 22), ("mem_k", 4), ("mem_v", 4), ("in2", 14), ("q_b", 4), ("kv_b", 2), ("glu", 2),
    ("merge2", 36), ("out2", 8), ("up2", 44), ("down2", 22),
]
FIRST = {}
NS = 0
for _name, _n in STAGES:
    FIRST[_name] = NS
    NS += _n

BASE = 16512
TILE_BYTES = 2048
X_AT, RAW_AT, RHIGH_AT, RLOW_AT, HHIGH_AT, HLOW_AT, W = 0, 8, 16, 24, 32, 40, 48
SMALL_AT = 100

MASK_SWAP = [(i + 16) % 32 for i in range(32)]


class Chain:

    def __init__(self, engine, semaphore):
        self.engine, self.semaphore, self.count = engine, semaphore, 0

    def mark(self, instruction):
        instruction.then_inc(self.semaphore, 1)
        self.count = self.count + 1
        return self.count

    def wait(self, count):
        self.engine.wait_ge(self.semaphore, count)

    def __call__(self, instruction):
        self.wait(self.mark(instruction))


def build(nc, a, out, STOP=99, dumps=None):
    ctx = ExitStack()
    with ctx:
        def at(name, tile, tiles, dtype=F32, width=512):
            return nc.alloc_sbuf_tensor_at(name, [P, tiles, width], dtype, offset=BASE + tile * TILE_BYTES)

        def sem(name):
            return ctx.enter_context(nc.semaphore(name))

        small_bytes = [0]

        def small(name, columns, dtype=F32):
            t = nc.alloc_sbuf_tensor_at(name, [P, columns], dtype, offset=BASE + SMALL_AT * TILE_BYTES + small_bytes[0])
            small_bytes[0] += (columns * 4 + 31) // 32 * 32
            return t

        bank = ctx.enter_context(nc.psum_tensor("bank", [P, 8, 512], F32))

        x = at("x", X_AT, 8)
        raw = at("raw", RAW_AT, RING, width=SLOT)
        ring_high = at("ring_high", RHIGH_AT, RING, F32R, SLOT)
        ring_low = at("ring_low", RLOW_AT, RING, F32R, SLOT)
        h_high = at("h_high", HHIGH_AT, 8, F32R)
        h_low = at("h_low", HLOW_AT, 8, F32R)

        vec = small("vec", NV)
        ones = small("ones", P)
        ident = small("ident", P)
        mod = small("mod", 48)
        mod_c = small("mod_c", 16)
        gain1 = small("gain1", 8)
        gain1_c = small("gain1_c", 8)
        gain2 = small("gain2", 8)
        att_max = small("att_max", 4)
        att_neg = small("att_neg", 2)
        att_sums = small("att_sums", 4)
        att_total = small("att_total", 2)
        s5 = small("s5", 16 * 19)

        def v_(name, i=0, n=1, p0=0, p1=P):
            return vec[p0:p1, VECTOR_AT[name][0] + i:VECTOR_AT[name][0] + i + n]

        y_high = at("y_high", W + 28, 12, F32R)
        y_low = at("y_low", W + 40, 12, F32R)

        q_scaled = at("q_scaled", W, 4)
        q_rot = at("q_rot", W + 4, 4)
        k_rot = at("k_rot", W + 8, 4)
        v_tok = at("v_tok", W + 12, 4)
        kc = at("kc", W + 16, 4, width=CTX)
        vc = at("vc", W + 18, 2)
        trig1 = at("trig1", W + 20, 2)
        bias1 = at("bias1", W + 22, 2, width=TAPS * GRID_W)
        hc_high = at("hc_high", W + 32, 8, F32R, CTX)
        hc_low = at("hc_low", W + 36, 8, F32R, CTX)
        ctx_in = at("ctx_in", W, 8, width=CTX)
        att1 = dict(s=at("att1_s", W + 32, 2), p=at("att1_p", W + 34, 2, width=768),
                    pt=at("att1_pt", W + 37, 2, width=768))
        rope_t = at("rope_t", W + 26, 2)
        k_plain = at("k_plain", W + 44, 4)
        o_tok1 = at("o_tok1", W + 44, 4)

        first_tiles = [at("ada_first0", W + 4, 12, width=SLOT), at("ada_first1", W + 32, 4, width=SLOT)]
        ada_first = [first_tiles[i // 12][:, i % 12] for i in range(ADA_FIRST)]
        late_tiles = [at(f"ada_late{i}", W + tile, 2, width=SLOT) for i, tile in enumerate((28, 40))]
        ada_late = [late_tiles[i // 2][:, i % 2] for i in range(LATE_RING)]

        silu_rows = at("silu_rows", W + 48, 1, width=SLOT)
        silu_rows_c = at("silu_rows_c", W + 28, 1, width=SLOT)
        ada_prod = at("ada_prod", W + 50, 1, width=SLOT)

        w3f = at("w3f", W + 0, 4)
        zt = at("zt", W + 4, 1)
        hid = at("hid", W + 5, 2)
        arg = at("arg", W + 7, 2)
        w12f = at("w12f", W + 9, 1)
        decay = at("decay", W + 44, 4)
        filt = at("filt", W + 32, 8)
        hyu = at("hyu", W + 0, 12)
        dft = at("dft", W + 12, 8)
        spec = [at("spec1", W + 20, 8), at("spec2", X_AT, 8)]
        z_tok = at("z_tok", W + 32, 4)
        y_re = at("y_re", W + 36, 4)
        y_im = at("y_im", W + 48, 4)
        hyt = at("hyt", W + 44, 2)
        hyz = at("hyz", W + 20, 4)

        merged = at("merged", W + 8, 8)
        m_high = at("m_high", W + 0, 8, F32R)
        m_low = at("m_low", W + 16, 8, F32R)
        sig = at("sig", W + 24, 2)
        mprod = at("mprod", W + 26, 2)

        hid_high = at("hid_high", W + 0, 22, F32R)
        hid_low = at("hid_low", W + 22, 22, F32R)
        ff_a = at("ff_a", W + 44, 2)
        ff_v = at("ff_v", W + 46, 2)
        ff_s = at("ff_s", W + 48, 2)
        ff_p = at("ff_p", W + 50, 2)

        mem_in = at("mem_in", W + 12, 8, width=CTX)
        hm_high = at("hm_high", W + 0, 8, F32R, CTX)
        hm_low = at("hm_low", W + 4, 8, F32R, CTX)
        kx = at("kx", W + 8, 4, width=CTX)
        vx = at("vx", W + 10, 2)
        cq = at("cq", W + 12, 3)
        ckv = at("ckv", W + 15, 2)
        kr = at("kr", W + 17, 1)
        xq = at("xq", W + 18, 4)
        u_ssm = at("u_ssm", W + 22, 4)
        cmask = at("cmask", W + 26, 1)
        cq_high = at("cq_high", W + 28, 3, F32R)
        cq_low = at("cq_low", W + 31, 3, F32R)
        ckv_high = at("ckv_high", W + 40, 2, F32R)
        ckv_low = at("ckv_low", W + 42, 2, F32R)
        att2 = dict(s=at("att2_s", W + 0, 2), p=at("att2_p", W + 2, 2, width=768),
                    pt=at("att2_pt", W + 5, 2, width=768))
        o_tok2 = at("o_tok2", W + 44, 4)
        qh = at("qh", W + 0, 8)
        kh = at("kh", W + 12, 4)
        kh2 = at("kh2", W + 18, 4)
        k_head = [kh[:, i] for i in range(4)] + [kh2[:, i] for i in range(4)]
        v_mla = at("v_mla", W + 8, 4)
        rope2 = at("rope2", W + 30, 2)
        rope_w = at("rope_w", W + 28, 2)
        rope_a = at("rope_a", W + 27, 1)
        pos_i = at("pos_i", W + 27, 1, I32)
        att3 = dict(s=at("att3_s", W + 40, 2), p=at("att3_p", W + 42, 2, width=768),
                    pt=at("att3_pt", W + 45, 2, width=768))
        o_tok3 = at("o_tok3", W + 32, 4)
        powers = at("powers", W + 16, 2)
        powers_high = at("powers_high", W + 27, 1)
        tab = at("tab", W + 0, 4)
        tab_tmp = at("tab_tmp", W + 4, 2)
        cmat = at("cmat", W + 6, 4, width=2 * P)
        bmat = at("bmat", W + 8, 8)
        s5s = at("s5s", W + 18, 4)
        s5r = at("s5r", W + 32, 2)
        s5t = at("s5t", W + 34, 2)
        c_tmp = at("c_tmp", W + 26, 1)[:, 0, 0:2 * P]
        gy = at("gy", W + 44, 4)
        gy_high = at("gy_high", W + 4, 4, F32R)
        gy_low = at("gy_low", W + 8, 4, F32R)
        gsig = at("gsig", W + 12, 2)
        gprod = at("gprod", W + 14, 2)

        raw_loaded = [sem(f"raw_loaded{i}") for i in range(RING)]
        ada_first_loaded = [sem(f"ada_first_loaded{i}") for i in range(4)]
        ada_first_used = sem("ada_first_used")
        ada_late_loaded = [sem(f"ada_late_loaded{i}") for i in range(LATE_RING)]
        ada_late_used = sem("ada_late_used")
        high_ready = sem("high_ready")
        low_ready = sem("low_ready")
        slot_used = sem("slot_used")
        dve_step = sem("dve_step")
        act_step = sem("act_step")
        pool_step = sem("pool_step")
        s5_powers, s5_table = sem("s5_powers"), sem("s5_table")
        first_loaded = sem("first_loaded")
        x_loaded = sem("x_loaded")
        ctx_loaded = sem("ctx_loaded")
        silu_loaded, silu_ready = sem("silu_loaded"), sem("silu_ready")
        mod_ready = sem("mod_ready")
        norm_squared, norm_summed, norm_mean, norm_root, norm_scaled, norm_rounded, norm_done = (
            sem("norm_" + s) for s in ("squared", "summed", "mean", "root", "scaled", "rounded", "done"))
        att_scored, att_biased, att_exp, att_turned, att_copied, att_copied2, att_summed, att_written, att_totalled = (
            sem("att_" + s) for s in ("scored", "biased", "exp", "turned", "copied", "copied2", "summed", "written",
                                      "totalled"))
        y_turned, y_rounded, y_split = sem("y_turned"), sem("y_rounded"), sem("y_split")
        in_copied = sem("in_copied")
        heads_squared, heads_summed, heads_log, heads_root, heads_done = (
            sem("heads_" + s) for s in ("squared", "summed", "log", "root", "done"))
        out_added = sem("out_added")
        bias_loaded = [sem("bias_loaded0"), sem("bias_loaded1")]
        trig_loaded = sem("trig_loaded")
        qkv_copied, rope_done, qkv_copied2 = sem("qkv_copied"), sem("rope_done"), sem("qkv_copied2")

        def norm(name, tiles, width, size, gains, shifts=None, outs=None, split=None, scratch=W + 40, ready=None):
            rows = tiles[0].shape[0]
            return dict(name=name, tiles=tiles, width=width, size=size, gains=gains, shifts=shifts, outs=outs,
                        split=split, rows=rows, ready=ready,
                        sq=at(f"{name}_sq", scratch, 2), scratch=scratch,
                        t=at(f"{name}_t", scratch + 5, 2))

        def cols(t, n, rows=P):
            return [t[0:rows, i:i + 1] for i in range(n)]

        def vcols(name, n, rows=P):
            return [v_(name, i, 1, 0, rows) for i in range(n)]

        NORMS = [
            norm("n_x1", [x[:, k] for k in range(8)], T, D, cols(gain1, 8), cols(mod, 8),
                 split=([h_high[:, k] for k in range(8)], [h_low[:, k] for k in range(8)])),
            norm("n_ctx", [ctx_in[:, k] for k in range(8)], CTX, D, cols(gain1_c, 8), cols(mod_c, 8),
                 split=([hc_high[:, k] for k in range(8)], [hc_low[:, k] for k in range(8)])),
            norm("n_x2", [x[:, k] for k in range(8)], T, D, cols(gain2, 8), [mod[:, 24 + i:25 + i] for i in range(8)],
                 ready=(out_added, 4),
                 split=([h_high[:, k] for k in range(8)], [h_low[:, k] for k in range(8)])),
            norm("n_final", [x[:, k] for k in range(8)], T, D, vcols("final", 8), outs=[x[:, k] for k in range(8)],
                 scratch=W + 44, ready=(out_added, 4 + 16 - 8)),
            norm("n_mem", [mem_in[:, k] for k in range(8)], CTX, D, vcols("mem_norm", 8), scratch=W + 44,
                 split=([hm_high[:, k] for k in range(8)], [hm_low[:, k] for k in range(8)])),
            norm("n_mix", [x[:, k] for k in range(8)], T, D, vcols("norm_mix", 8), scratch=W + 44, ready=(norm_done, 24),
                 split=([h_high[:, k] for k in range(8)], [h_low[:, k] for k in range(8)])),
        ]
        NORMS += [
            norm("n_cq", [cq[:, k] for k in range(3)], T, QL, vcols("q_a", 3), scratch=W + 0, ready=(in_copied, 6),
                 split=([cq_high[:, k] for k in range(3)], [cq_low[:, k] for k in range(3)])),
            norm("n_ckv", [ckv[:, k] for k in range(2)], T, KVL, vcols("kv_a", 2), scratch=W + 0, ready=(in_copied, 9),
                 split=([ckv_high[:, k] for k in range(2)], [ckv_low[:, k] for k in range(2)])),
        ]
        NORMS += [norm("n_ffn", [x[:, k] for k in range(8)], T, D, vcols("norm_ffn", 8), ready=(out_added, 4 + 16),
                       split=([h_high[:, k] for k in range(8)], [h_low[:, k] for k in range(8)]))]
        NORM = {}
        squares = outputs = rounds = 0
        for i, n in enumerate(NORMS):
            n.update(index=i, bank=6 + i % 2, root=at(n["name"] + "_root", n["scratch"] + 2 + i % 2, 1), squares=squares, outputs=outputs, rounds=rounds)
            squares += len(n["tiles"])
            outputs += len(n["tiles"])
            rounds += len(n["tiles"]) if n["split"] else 0
            n["done"] = outputs
            NORM[n["name"]] = n

        def norm_scalar(act, *names):
            def squares(n):
                w, r = n["width"], n["rows"]
                for k, t in enumerate(n["tiles"]):
                    i = n["squares"] + k
                    if n["ready"]:
                        act.wait_ge(n["ready"][0], n["ready"][1] + k + 1)
                    if i >= 2:
                        act.wait_ge(norm_summed, i - 1)
                    nc.scalar.activation(n["sq"][0:r, i % 2, 0:w], t, ACT.Square, scale=float(n["size"]) ** -0.5) \
                      .then_inc(norm_squared, 1)

            norms = [NORM[name] for name in names]
            squares(norms[0])
            for n, later in zip(norms, norms[1:] + [None]):
                if later:
                    squares(later)
                w, r = n["width"], n["rows"]
                act.wait_ge(norm_summed, n["squares"] + len(n["tiles"]))
                if n["index"] >= 2:
                    act.wait_ge(norm_done, NORMS[n["index"] - 2]["done"])
                nc.scalar.activation(n["root"][0:r, 0, 0:w], bank[0:r, n["bank"], 0:w], ACT.Ln, bias=v_("eps", 0, 1, 0, r)) \
                  .then_inc(norm_mean, 1)
                act.wait_ge(norm_mean, n["index"] + 1)
                nc.scalar.activation(n["root"][0:r, 0, 0:w], n["root"][0:r, 0, 0:w], ACT.Exp, scale=-0.5) \
                  .then_inc(norm_root, 1)
                if n["split"]:
                    for k in range(len(n["tiles"])):
                        act.wait_ge(norm_scaled, n["rounds"] + k + 1)
                        shift = n["shifts"][k] if n["shifts"] else v_("zero")
                        nc.scalar.activation(n["split"][0][k], n["t"][0:r, k % 2, 0:w], ACT.Identity,
                                             bias=shift).then_inc(norm_rounded, 1)

        def norm_tensor(pe, n):
            w, r = n["width"], n["rows"]
            if n["index"] >= 2:
                pe.wait_ge(norm_mean, n["index"] - 1)
            for k in range(len(n["tiles"])):
                i = n["squares"] + k
                pe.wait_ge(norm_squared, i + 1)
                nc.tensor.matmul(bank[0:r, n["bank"], 0:w], ones[0:r, 0:r], n["sq"][0:r, i % 2, 0:w],
                                 start=(k == 0), stop=(k == len(n["tiles"]) - 1)).then_inc(norm_summed, 1)

        def norm_vector(dve, link, n):
            w, r = n["width"], n["rows"]
            m = len(n["tiles"])
            dve.wait_ge(norm_root, n["index"] + 1)
            root = n["root"][0:r, 0, 0:w]
            if not n["split"]:
                for k in range(m):
                    nc.vector.scalar_tensor_tensor(out=n["outs"][k], in0=n["tiles"][k], scalar=n["gains"][k], in1=root,
                                                   op0=ALU.mult, op1=ALU.mult).then_inc(norm_done, 1)
                dve.wait_ge(norm_done, n["done"])
                return
            for k in range(m + 1):
                if k < m:
                    if k >= 2:
                        dve.wait_ge(norm_done, n["outputs"] + k - 1)
                    nc.vector.scalar_tensor_tensor(out=n["t"][0:r, k % 2, 0:w], in0=n["tiles"][k], scalar=n["gains"][k],
                                                   in1=root, op0=ALU.mult, op1=ALU.mult).then_inc(norm_scaled, 1)
                if k >= 1:
                    j = k - 1
                    dve.wait_ge(norm_rounded, n["rounds"] + j + 1)
                    shift = n["shifts"][j] if n["shifts"] else v_("zero")
                    nc.vector.scalar_tensor_tensor(out=n["split"][1][j], in0=n["t"][0:r, j % 2, 0:w], scalar=shift,
                                                   in1=n["split"][0][j], op0=ALU.add, op1=ALU.subtract).then_inc(norm_done, 1)
            dve.wait_ge(norm_done, n["done"])

        def group(tiles, width, rows, gain, scratch, ready):
            i = len(GROUPS)
            GROUPS.append(dict(index=i, tiles=tiles, width=width, rows=rows, gain=v_(gain, 0, 1, 0, rows), ready=ready,
                               bank=4 * (i % 2), sq=at(f"heads{i}_sq", scratch, 2), root=at(f"heads{i}_root", scratch + 2, 4)))

        GROUPS = []
        group([kx[:, i] for i in range(4)], CTX, P, "xk", W + 28, 4)
        group([xq[:, i] for i in range(4)], T, P, "xq", W + 28, 12 + 4)
        for i in (0, 4):
            group([qh[0:DQK, i + j] for j in range(4)], T, DQK, "q_norm", W + 40, 48)
        for i in (0, 4):
            group([k_head[i + j][0:DQK] for j in range(4)], T, DQK, "k_norm", W + 40, 48)

        def heads_scalar(act, lo, hi):
            def squares(g):
                act.wait_ge(in_copied, g["ready"])
                for k, t in enumerate(g["tiles"]):
                    i = 4 * g["index"] + k
                    if i >= 2:
                        act.wait_ge(heads_summed, i - 1)
                    nc.scalar.activation(g["sq"][0:g["rows"], i % 2, 0:g["width"]], t, ACT.Square,
                                         scale=float(g["rows"]) ** -0.5).then_inc(heads_squared, 1)

            squares(GROUPS[lo])
            for g in GROUPS[lo:hi]:
                if g["index"] + 1 < hi:
                    squares(GROUPS[g["index"] + 1])
                i, w, r = g["index"], g["width"], g["rows"]
                root = g["root"][0:r, :, 0:w]
                act.wait_ge(heads_summed, 4 * i + 4)
                if i:
                    act.wait_ge(heads_done, 4 * i)
                nc.scalar.activation(root, bank[0:r, g["bank"]:g["bank"] + 4, 0:w], ACT.Ln,
                                     bias=v_("eps", 0, 1, 0, r)).then_inc(heads_log, 1)
                act.wait_ge(heads_log, i + 1)
                nc.scalar.activation(root, root, ACT.Exp, scale=-0.5).then_inc(heads_root, 1)

        def heads_tensor(pe, lo, hi):
            for g in GROUPS[lo:hi]:
                if g["index"] >= 2:
                    pe.wait_ge(heads_log, g["index"] - 1)
                for k in range(4):
                    i, w, r = 4 * g["index"] + k, g["width"], g["rows"]
                    pe.wait_ge(heads_squared, i + 1)
                    nc.tensor.matmul(bank[0:r, g["bank"] + k, 0:w], ones[0:r, 0:r], g["sq"][0:r, i % 2, 0:w],
                                     start=True, stop=True).then_inc(heads_summed, 1)

        def heads_vector(dve, lo, hi):
            for g in GROUPS[lo:hi]:
                dve.wait_ge(heads_root, g["index"] + 1)
                for k, t in enumerate(g["tiles"]):
                    nc.vector.scalar_tensor_tensor(out=t, in0=t, scalar=g["gain"], in1=g["root"][0:g["rows"], k, 0:g["width"]],
                                                   op0=ALU.mult, op1=ALU.mult).then_inc(heads_done, 1)

        ATT = []

        def half_rows(t, i, h):
            return t[64 * (h % 2):64 * (h % 2) + 64, i]

        for h in range(HEADS):
            for t in range(TT):
                qs = slice(t * P, t * P + P)
                ATT.append(dict(
                    at=att1, q=half_rows(q_rot, h // 2, h)[:, qs], k=half_rows(k_rot, h // 2, h),
                    table=bias1[:, h % 2, (6 - 2 * t) * GRID_W:(6 - 2 * t + 8) * GRID_W], width=T, scale=1.0,
                    q2=half_rows(q_scaled, h // 2, h)[:, qs], k2=half_rows(kc, h // 2, h), width2=CTX,
                    values=[v_tok[:, i, h * HD:(h + 1) * HD] for i in range(TT)]
                    + [vc[:, i, h * HD:(h + 1) * HD] for i in range(CT)],
                    out=o_tok1[:, t, h * HD:(h + 1) * HD], head=h, first=(t == 0)))
        ATT1 = len(ATT)
        for h in range(XH):
            for t in range(TT):
                ATT.append(dict(
                    at=att2, q=xq[:, h, t * P:t * P + P], k=kx[:, h], table=cmask[:, 0, 0:CTX], width=CTX,
                    scale=float(P) ** -0.5, q2=None,
                    values=[vx[:, i, h * P:(h + 1) * P] for i in range(CT)], out=o_tok2[:, t, h * P:(h + 1) * P]))
        ATT2 = len(ATT)
        for h in range(HEADS):
            for t in range(TT):
                w = (t + 1) * P
                ATT.append(dict(
                    at=att3, q=qh[0:DQK, h, t * P:t * P + P], k=k_head[h][0:DQK, 0:w], table=cmask[:, 0, T - w:T], width=w,
                    scale=float(DQK) ** -0.5, q2=None,
                    values=[v_mla[:, i, h * DV:(h + 1) * DV] for i in range(t + 1)], out=o_tok3[:, t, h * DV:(h + 1) * DV]))
        ATT3 = len(ATT)
        seconds = 0
        for s in ATT:
            keys = len(s["values"])
            s["near"] = min(keys, (keys + 1) // 2)
            s["seconds"] = seconds
            seconds += keys > s["near"]
            s["seconds_done"] = seconds

        def att_tensor(pe, lo, hi):
            def scores(n):
                s = ATT[n]
                if n >= 2:
                    pe.wait_ge(att_biased, n - 1)
                    pe.wait_ge(att_exp, n - 1)
                if n >= ATT2 and (n - ATT2) % TT == 0:
                    pe.wait_ge(mla_roped, (n - ATT2) // TT * 2 + 2)
                mm = nc.tensor.matmul(bank[:, n % 2, 0:s["width"]], s["q"], s["k"], start=True, stop=True)
                if s["q2"] is not None:
                    mm = nc.tensor.matmul(bank[:, 2 + n % 2, 0:CTX], s["q2"], s["k2"], start=True, stop=True)
                mm.then_inc(att_scored, 1)

            def turn(n):
                s = ATT[n]
                keys, near = len(s["values"]), s["near"]
                pe.wait_ge(att_exp, n + 1)
                if n >= 1:
                    pe.wait_ge(att_copied, n)
                if s["seconds"] >= 1:
                    pe.wait_ge(att_copied2, s["seconds"])
                for i in range(keys):
                    b, c = (4, i) if i < near else (5, i - near)
                    mm = nc.tensor.transpose(bank[:, b, c * P:(c + 1) * P], s["at"]["p"][:, n % 2, i * P:(i + 1) * P], ident[:, :])
                mm.then_inc(att_turned, 1)

            def weigh(n):
                s = ATT[n]
                keys, near = len(s["values"]), s["near"]
                pe.wait_ge(att_copied, n + 1)
                if keys > near:
                    pe.wait_ge(att_copied2, s["seconds_done"])
                if n >= 2:
                    pe.wait_ge(att_written, n - 1)
                dv = s["values"][0].shape[1]
                for i in range(keys):
                    mm = nc.tensor.matmul(bank[:, 6 + n % 2, 0:dv], s["at"]["pt"][:, n % 2, i * P:(i + 1) * P], s["values"][i],
                                          start=(i == 0), stop=(i == keys - 1))
                mm.then_inc(att_summed, 1)

            scores(lo)
            scores(lo + 1)
            turn(lo)
            for n in range(lo, hi):
                if n + 2 < hi:
                    scores(n + 2)
                if n + 1 < hi:
                    turn(n + 1)
                weigh(n)

        def att_scalar(act, lo, hi, between=None):
            def exps(n):
                s = ATT[n]
                act.wait_ge(att_biased, n + 1)
                if n >= 2:
                    act.wait_ge(att_turned, n - 1)
                    act.wait_ge(att_totalled, n - 1)
                j = n % 2
                neg = att_neg[:, j:j + 1]
                e = nc.scalar.activation(s["at"]["p"][:, j, 0:s["width"]], s["at"]["s"][:, j, 0:s["width"]], ACT.Exp,
                                         bias=neg, accum_out=att_sums[:, 2 * j:2 * j + 1])
                if s["q2"] is not None:
                    e = nc.scalar.activation(s["at"]["p"][:, j, T:T + CTX], bank[:, 2 + j, 0:CTX], ACT.Exp,
                                             bias=neg, accum_out=att_sums[:, 2 * j + 1:2 * j + 2])
                e.then_inc(att_exp, 1)

            exps(lo)
            for n in range(lo, hi):
                if n + 1 < hi:
                    exps(n + 1)
                s = ATT[n]
                keys, near = len(s["values"]), s["near"]
                if between:
                    between(n)
                if keys > near:
                    act.wait_ge(att_turned, n + 1)
                    if n >= 2:
                        act.wait_ge(att_summed, n - 1)
                    nc.scalar.activation(s["at"]["pt"][:, n % 2, near * P:keys * P], bank[:, 5, 0:(keys - near) * P],
                                         ACT.Copy).then_inc(att_copied2, 1)

        def att_vector(dve, link, lo, hi, between=None):
            def biased(n):
                s = ATT[n]
                j = n % 2
                dve.wait_ge(att_scored, n + 1)
                if n >= 2:
                    dve.wait_ge(att_exp, n - 1)
                if n < ATT1 and s["first"]:
                    dve.wait_ge(bias_loaded[s["head"] % 2], 16 * (s["head"] // 2 + 1))
                w = s["width"]
                start = NEG
                if s["q2"] is not None:
                    link(nc.vector.reduce_max(att_max[:, j:j + 1], bank[:, 2 + j, 0:CTX], AX.X))
                    start = att_max[:, j:j + 1]
                link(nc.vector.tensor_tensor_reduce(s["at"]["s"][:, j, 0:w], bank[:, j, 0:w], s["table"], s["scale"], start,
                                                    ALU.add, ALU.max, att_max[:, 2 + j:3 + j]))
                nc.vector.tensor_scalar(att_neg[:, j:j + 1], att_max[:, 2 + j:3 + j], -1.0, None,
                                        ALU.mult).then_inc(att_biased, 1)

            def written(n):
                s = ATT[n]
                j = n % 2
                dv = s["values"][0].shape[1]
                dve.wait_ge(att_exp, n + 1)
                total = att_sums[:, 2 * j:2 * j + 1]
                if s["q2"] is not None:
                    link(nc.vector.tensor_tensor(att_total[:, j:j + 1], total, att_sums[:, 2 * j + 1:2 * j + 2], ALU.add))
                    total = att_total[:, j:j + 1]
                nc.vector.reciprocal(att_total[:, j:j + 1], total).then_inc(att_totalled, 1)
                dve.wait_ge(att_totalled, n + 1)
                dve.wait_ge(att_summed, n + 1)
                nc.vector.tensor_scalar(s["out"], bank[:, 6 + j, 0:dv], att_total[:, j:j + 1], None,
                                        ALU.mult).then_inc(att_written, 1)

            biased(lo)
            for n in range(lo, hi):
                if n + 1 < hi:
                    biased(n + 1)
                s = ATT[n]
                dve.wait_ge(att_turned, n + 1)
                if n >= 2:
                    dve.wait_ge(att_summed, n - 1)
                near = s["near"]
                nc.vector.tensor_copy(s["at"]["pt"][:, n % 2, 0:near * P], bank[:, 4, 0:near * P]).then_inc(att_copied, 1)
                if n > lo:
                    written(n - 1)
                if between:
                    between(n)
            written(hi - 1)

        def turn_tensor(pe, o_tok, steps, before):
            pe.wait_ge(att_written, steps)
            for c in range(4):
                for t in range(TT):
                    mm = nc.tensor.transpose(bank[:, c, t * P:(t + 1) * P], o_tok[:, t, c * P:(c + 1) * P], ident[:, :])
                mm.then_inc(y_turned, 1)

        def turn_scalar(act, branch, before):
            for c in range(4):
                act.wait_ge(y_turned, before + c + 1)
                nc.scalar.activation(y_high[:, 4 * branch + c], bank[:, c], ACT.Copy).then_inc(y_rounded, 1)

        def turn_vector(dve, branch, before):
            for c in range(4):
                dve.wait_ge(y_rounded, before + c + 1)
                nc.vector.tensor_tensor(y_low[:, 4 * branch + c], bank[:, c], y_high[:, 4 * branch + c],
                                        ALU.subtract).then_inc(y_split, 1)
            dve.wait_ge(y_split, before + 4)

        def product(o, w_high, w_low, a_high, a_low, start, stop):
            nc.tensor.matmul(o, w_high, a_high, start=start, stop=False)
            nc.tensor.matmul(o, w_high, a_low, start=False, stop=False)
            return nc.tensor.matmul(o, w_low, a_high, start=False, stop=stop)

        def block_of(position, k, n=P):
            return ring_high[:, position, k * P:k * P + n], ring_low[:, position, k * P:k * P + n]

        def tile_product(o, position, first, acts, stop_all=True):
            for k, (ah, al) in enumerate(acts):
                wh, wl = block_of(position, first + k)
                mm = product(o, wh, wl, ah, al, k == 0, k == len(acts) - 1)
            return mm

        def split_high(act, n, it=0):
            if isinstance(it, int) and n >= NS:
                return
            act.wait_ge(raw_loaded[n % RING], 16 * (n // RING + 1) + it * 16)
            if n >= RING:
                act.wait_ge(slot_used, it * 4 + (n - RING + 1))
            nc.scalar.activation(ring_high[:, n % RING], raw[:, n % RING], ACT.Copy).then_inc(high_ready, 1)

        H = [(h_high[:, k], h_low[:, k]) for k in range(8)]

        HC = [(hc_high[:, k], hc_low[:, k]) for k in range(8)]
        HM = [(hm_high[:, k], hm_low[:, k]) for k in range(8)]
        M_ = [(m_high[:, k], m_low[:, k]) for k in range(8)]
        CQ = [(cq_high[:, k], cq_low[:, k]) for k in range(3)]
        CKV = [(ckv_high[:, k], ckv_low[:, k]) for k in range(2)]
        GY = [(gy_high[:, k], gy_low[:, k]) for k in range(4)]

        filt_loaded, hid_made, arg_ready, hid_ready = (sem(s) for s in ("filt_loaded", "hid_made", "arg_ready", "hid_ready"))
        filt_made, filt_summed, k_made, k_copied, dft_loaded = (
            sem(s) for s in ("filt_made", "filt_summed", "k_made", "k_copied", "dft_loaded"))
        conv_centre, conv_done = sem("conv_centre"), sem("conv_done")
        z_turned, z_copied, u_made, y_made, z_back, z_done = (
            sem(s) for s in ("z_turned", "z_copied", "u_made", "y_made", "z_back", "z_done"))
        merge_sig, merge_added, merge_rounded, merge_low = (
            sem("merge_" + s) for s in ("sig", "added", "rounded", "low"))
        up_gate, up_prod, up_rounded, up_low, up_centre, up_conv = (
            sem("up_" + s) for s in ("gate", "prod", "rounded", "low", "centre", "conv"))
        mem_loaded, mask_loaded, mla_roped, pos_loaded, rope_arg, rope_sin = (
            sem(s) for s in ("mem_loaded", "mask_loaded", "mla_roped", "pos_loaded", "rope_arg", "rope_sin"))
        s5_arg, s5_sin, s5_in, s5_rotated, s5_states, s5_out, s5_y, s5_gelu, s5_b = (
            sem("s5_" + s) for s in ("arg", "sin", "in", "rotated", "states", "out", "y", "gelu", "b"))
        s5_c = [sem(f"s5_c{i}") for i in range(4)]
        s5_c_ready = sem("s5_c_ready")
        glu_rounded, glu_low, glu_sig, glu_prod = (sem("glu_" + s) for s in ("rounded", "low", "sig", "prod"))
        stored = sem("stored")

        IN_MEM, IN_IN2, IN_QB, IN_K, IN_V = 6, 20, 28, 36, 40
        IN_KR = 48

        block = ctx.enter_context(nc.Block())

        @block.sync
        def _(sp):
            def load(position, index):
                sp.dma_start(raw[:, position], a["stream"][bass.ds(index, 1)].rearrange("a p n -> (a p) n")) \
                  .then_inc(raw_loaded[position], 16)

            for j in range(ADA_FIRST):
                sp.dma_start(ada_first[j], a["stream"][j]).then_inc(ada_first_loaded[j // 4], 16)
            for j in range(RING):
                load(j, ADA_SLOTS + j)
            with sp.Fori(1, NS // RING) as i:
                for j in range(RING):
                    sp.wait_ge(low_ready, i * RING + (j - RING + 1))
                    load(j, i * RING + (ADA_SLOTS + j))
            for n in range(NS // RING * RING, NS):
                sp.wait_ge(low_ready, n - RING + 1)
                load(n % RING, ADA_SLOTS + n)

        @block.gpsimd
        def _(pool):
            def split_low(position, n):
                pool.wait_ge(high_ready, n)
                nc.gpsimd.tensor_tensor(ring_low[:, position], raw[:, position], ring_high[:, position],
                                        ALU.subtract).then_inc(low_ready, 1)

            def split_rounds(lo, hi):
                with pool.Fori(lo, hi) as i:
                    for j in range(RING):
                        split_low(j, i * RING + (j + 1))

            s5_slot = FIRST["glu"] + 2
            assert s5_slot % RING == 0
            split_rounds(0, s5_slot // RING)

            link = Chain(pool, pool_step)
            tt = nc.gpsimd.tensor_tensor
            pool.wait_ge(y_turned, 12)
            pool.wait_ge(s5_powers, 1)
            for s in range(ST):
                if s >= 2:
                    pool.wait_ge(s5_states, s - 1)
                shape = [P, T // LOW, LOW]
                low_re, low_im = (powers[:, r, s * LOW:(s + 1) * LOW].rearrange("p (a n) -> p a n", a=1).to_broadcast(shape)
                                  for r in range(2))
                high_re, high_im = (powers_high[:, 0, r * 256 + s * 16:r * 256 + s * 16 + 16]
                                    .rearrange("p (a n) -> p a n", n=1).to_broadcast(shape) for r in range(2))
                e_re, e_im, t0, t1 = (v.rearrange("p (a n) -> p a n", n=LOW) for v in (
                    tab[:, 2 * (s % 2)], tab[:, 2 * (s % 2) + 1], tab_tmp[:, 0], tab_tmp[:, 1]))
                link.mark(tt(e_re, low_re, high_re, ALU.mult))
                first = link.mark(tt(t0, low_im, high_im, ALU.mult))
                link.mark(tt(e_im, low_re, high_im, ALU.mult))
                second = link.mark(tt(t1, low_im, high_re, ALU.mult))
                link.wait(first)
                link.mark(tt(e_re, e_re, t0, ALU.subtract))
                link.wait(second)
                tt(e_im, e_im, t1, ALU.add).then_inc(s5_table, 1)
                pool.wait_ge(s5_table, s + 1)

            split_rounds(s5_slot // RING, NS // RING)
            for n in range(NS // RING * RING, NS):
                split_low(n % RING, n + 1)

        @block.scalar
        def _(act):
            copy = nc.scalar.activation
            link = Chain(act, act_step)
            act.dma_start(silu_rows[:, 0], a["c"].partition_broadcast(P)).then_inc(silu_loaded, 16)
            act.dma_start(silu_rows_c[:, 0], a["c_ctx"].partition_broadcast(P)).then_inc(silu_loaded, 16)
            act.dma_start(vec[:, :], a["vectors"]).then_inc(first_loaded, 16)
            act.dma_start(ones[:, :], a["ones"]).then_inc(first_loaded, 16)
            act.dma_start(ident[:, :], a["identity"]).then_inc(first_loaded, 16)
            act.dma_start(x[:, :, :], a["x"]).then_inc(x_loaded, 16)
            act.dma_start(ctx_in[:, :, :], a["ctx"]).then_inc(ctx_loaded, 16)

            act.wait_ge(silu_loaded, 32)
            copy(silu_rows[:, 0], silu_rows[:, 0], ACT.Silu).then_inc(silu_ready, 1)
            copy(silu_rows_c[:, 0], silu_rows_c[:, 0], ACT.Silu).then_inc(silu_ready, 1)
            act.wait_ge(x_loaded, 16)
            norm_scalar(act, "n_x1")
            for n in range(RING):
                split_high(act, n)
            act.wait_ge(ctx_loaded, 16)
            norm_scalar(act, "n_ctx")

            act.wait_ge(norm_done, NORM["n_ctx"]["done"])
            act.dma_start(trig1[:, :, :], a["trig1"]).then_inc(trig_loaded, 16)
            for h in range(2):
                act.dma_start(bias1[:, h], a["bias"][h]).then_inc(bias_loaded[h], 16)
            for i in range(LATE_RING - 1):
                act.dma_start(ada_late[i], a["stream"][ADA_FIRST + i]).then_inc(ada_late_loaded[i], 16)
            for j in range(4):
                n = FIRST["q"] + j
                if n + 2 >= RING:
                    split_high(act, n + 2)
                act.wait_ge(slot_used, n + 1)
                copy(q_scaled[:, j], bank[:, j], ACT.Copy, scale=HD ** -0.5).then_inc(qkv_copied, 1)
            for j in range(4):
                n = FIRST["k"] + j
                split_high(act, n + 2)
                act.wait_ge(slot_used, n + 1)
                copy(k_plain[:, j], bank[:, j], ACT.Copy).then_inc(qkv_copied, 1)
                copy(kc[:, j], bank[:, 4 + j, 0:CTX], ACT.Copy).then_inc(qkv_copied, 1)
            for j in range(4):
                split_high(act, FIRST["v"] + j + 2)
            act.wait_ge(slot_used, FIRST["v"] + 4)
            for t in range(TT):
                copy(v_tok[:, t], bank[:, t], ACT.Copy).then_inc(qkv_copied, 1)
            for t in range(CT):
                copy(vc[:, t], bank[:, 4 + t], ACT.Copy).then_inc(qkv_copied, 1)

            def load_late(i):
                if i < ADA_SLOTS - ADA_FIRST:
                    if i >= LATE_RING:
                        act.wait_ge(ada_late_used, i - LATE_RING + 1)
                    act.dma_start(ada_late[i % LATE_RING], a["stream"][ADA_FIRST + i]) \
                       .then_inc(ada_late_loaded[i % LATE_RING], 16)

            def next_loads(n):
                load_late(n + LATE_RING - 1)
                h = n // TT + 1
                if n % TT == 1 and 2 <= h < HEADS:
                    act.wait_ge(att_biased, TT * (h - 1))
                    act.dma_start(bias1[:, h % 2], a["bias"][h]).then_inc(bias_loaded[h % 2], 16)

            att_scalar(act, 0, ATT1, next_loads)
            turn_scalar(act, 0, 0)

            act.wait_ge(y_turned, 4)
            for dst, src in ((w3f[0:FW, :, :], "hy_w3"), (zt[0:EMB, 0], "hy_z"), (w12f[0:FW, 0, 0:2 * FW], "hy_w12"),
                             (decay[:, :, :], "decay"), (dft[:, :, :], "dft1")):
                act.dma_start(dst, a[src]).then_inc(filt_loaded, 16)
            for i in range(2):
                act.wait_ge(arg_ready, i + 1)
                copy(hid[0:FW, i], arg[0:FW, 0], ACT.Sin).then_inc(hid_ready, 1)
            for n in range(2):
                for f in range(4):
                    act.wait_ge(k_made, 4 * n + f + 1)
                    b = 4 + 2 * (f % 2)
                    link(copy(spec[n][:, f], bank[:, b], ACT.Copy, scale=1.0 / T))
                    copy(spec[n][:, 4 + f], bank[:, b + 1], ACT.Copy, scale=1.0 / T).then_inc(k_copied, 1)
            act.dma_start(dft[:, :, :], a["dft2"]).then_inc(dft_loaded, 16)

            with act.Fori(0, 3) as part:
                for j in range(4):
                    n = FIRST["hyena_in"] + j
                    split_high(act, n + 2, part)
                    act.wait_ge(slot_used, part * 4 + (n + 1))
                    wc, bc = VECTOR_AT["hy_conv_w"][0] + 12 + j, VECTOR_AT["hy_conv_b"][0] + j
                    copy(hyu[:, bass.ds(part * 4 + j, 1)].rearrange("p a n -> p (a n)"), bank[:, j], ACT.Identity,
                         scale=vec[:, bass.ds(part * 4 + wc, 1)], bias=vec[:, bass.ds(part * 4 + bc, 1)]).then_inc(conv_centre, 1)
            for n in range(2):
                for t in range(TT):
                    act.wait_ge(z_turned, 4 * n + t + 1)
                    copy(z_tok[:, t], bank[:, t], ACT.Copy).then_inc(z_copied, 1)
            act.wait_ge(y_made, 8)
            act.dma_start(x[:, :, :], a["x"]).then_inc(x_loaded, 16)
            for c in range(4):
                act.wait_ge(z_done, 4 + c + 1)
                copy(y_high[:, 4 + c], hyz[:, c], ACT.Copy).then_inc(y_rounded, 1)

            def merge_scalar(stage, branches, tiles, bias):
                with act.Fori(0, branches) as b:
                    for p in range(4):
                        q = 4 * (p % 2)
                        for i in range(2):
                            n = FIRST[stage] + 3 * p + i
                            g = 2 * p + i
                            split_high(act, n + 2, b * 3)
                            act.wait_ge(slot_used, b * 12 + (n + 1))
                            act.wait_ge(merge_added, b * 8 + (tiles + g + 3))
                            shift = vec[:, bass.ds(b * 8 + (bias + g), 1)] if bias is not None else v_("zero")
                            copy(sig[:, i], bank[:, q + i], ACT.Sigmoid, bias=shift).then_inc(merge_sig, 1)
                        split_high(act, FIRST[stage] + 3 * p + 4, b * 3)
                        for i in range(2):
                            g = 2 * p + i
                            act.wait_ge(merge_added, b * 8 + (tiles + g + 5))
                            copy(m_high[:, g], merged[:, g], ACT.Copy).then_inc(merge_rounded, 1)

            def splits(stage):
                with act.Fori(0, 2) as i:
                    for j in range(4):
                        split_high(act, FIRST[stage] + j + 2, i)

            def down_splits(stage):
                for half in range(2):
                    n = FIRST[stage] + 11 * half
                    split_high(act, n + 2)
                    with act.Fori(0, 2) as i:
                        for j in range(4):
                            split_high(act, n + 1 + j + 2, i)
                    split_high(act, n + 11)
                    split_high(act, n + 12)

            merge_scalar("merge1", 2, 0, None)
            splits("out1")
            norm_scalar(act, "n_x2")

            with act.Fori(0, 11) as i:
                for q in range(2):
                    n = FIRST["up1"] + 2 * q
                    split_high(act, n + 2, i)
                    act.wait_ge(slot_used, i * 4 + (n + 1))
                    act.wait_ge(up_prod, i * 2 + (q + 1))
                    copy(ff_s[:, q], bank[:, 2 * q], ACT.Silu).then_inc(up_gate, 1)
                    split_high(act, n + 3, i)
                    act.wait_ge(up_prod, i * 2 + (q + 3))
                    copy(hid_high[:, bass.ds(i * 2 + q, 1)].rearrange("p a n -> p (a n)"), ff_p[:, q], ACT.Copy) \
                        .then_inc(up_rounded, 1)
            down_splits("down1")

            act.wait_ge(slot_used, FIRST["down1"] + 22)
            act.dma_start(mem_in[:, :, :], a["mem"]).then_inc(mem_loaded, 16)
            act.dma_start(cmask[:, 0], a["cmask"]).then_inc(mask_loaded, 16)
            act.dma_start(pos_i[64:96, 0], a["positions"].partition_broadcast(DROPE)).then_inc(pos_loaded, 16)
            norm_scalar(act, "n_final")
            act.wait_ge(mem_loaded, 16)
            norm_scalar(act, "n_mem", "n_mix")
            for j in range(4):
                n = FIRST["mem_k"] + j
                split_high(act, n + 2)
                act.wait_ge(slot_used, n + 1)
                copy(kx[:, j], bank[:, j, 0:CTX], ACT.Copy).then_inc(in_copied, 1)
            for j in range(4):
                split_high(act, FIRST["mem_v"] + j + 2)
            act.wait_ge(slot_used, FIRST["mem_v"] + 4)
            for t in range(CT):
                copy(vx[:, t], bank[:, 4 + t], ACT.Copy).then_inc(in_copied, 1)
            dests = [cq[:, i] for i in range(3)] + [ckv[:, i] for i in range(2)] + [kr[64:96, 0]] \
                + [xq[:, i] for i in range(4)] + [u_ssm[:, i] for i in range(4)]
            act.wait_ge(norm_done, NORM["n_mem"]["done"])
            for j, dst in enumerate(dests):
                n = FIRST["in2"] + j
                split_high(act, n + 2)
                act.wait_ge(slot_used, n + 1)
                src = bank[64:96, j % 4] if j == 5 else bank[:, j % 4]
                copy(dst, src, ACT.Copy).then_inc(in_copied, 1)
            for i in range(2):
                act.wait_ge(s5_arg, i + 1)
                copy(s5[:, 16 * (6 + i):16 * (7 + i)], s5[:, 16 * 5:16 * 6], ACT.Sin).then_inc(s5_sin, 1)
            heads_scalar(act, 0, 2)
            att_scalar(act, ATT1, ATT2)
            turn_scalar(act, 2, 4)

            norm_scalar(act, "n_cq", "n_ckv")
            for j in range(4):
                n = FIRST["q_b"] + j
                split_high(act, n + 2)
                act.wait_ge(slot_used, n + 1)
                for i in range(2):
                    copy(qh[0:DQK, 2 * j + i], bank[0:DQK, (2 * j + i) % 4], ACT.Copy).then_inc(in_copied, 1)
            n = FIRST["kv_b"]
            split_high(act, n + 2)
            act.wait_ge(slot_used, n + 1)
            for h in range(HEADS):
                copy(k_head[h][0:DNOPE], bank[64 * (h % 2):64 * (h % 2) + 64, h // 2], ACT.Copy).then_inc(in_copied, 1)
            split_high(act, n + 3)
            act.wait_ge(slot_used, n + 2)
            for t in range(TT):
                copy(v_mla[:, t], bank[:, 4 + t], ACT.Copy).then_inc(in_copied, 1)
            for h in range(HEADS):
                copy(k_head[h][64:96], kr[64:96, 0], ACT.Copy).then_inc(in_copied, 1)
            act.wait_ge(in_copied, IN_KR)
            for i in range(2):
                act.wait_ge(rope_arg, i + 1)
                copy(rope2[64:96, 1 - i], rope_a[64:96, 0], ACT.Sin).then_inc(rope_sin, 1)
            heads_scalar(act, 2, 6)
            att_scalar(act, ATT2, ATT3)
            turn_scalar(act, 0, 8)

            act.wait_ge(y_split, 16)
            act.wait_ge(y_turned, 12)
            for half in range(2):
                act.dma_start(bmat[:, 4 * half:4 * half + 4], a["ssm_b"][half]).then_inc(s5_b, 16)
            for s in range(4):
                act.dma_start(cmat[:, s], a["ssm_c"][s]).then_inc(s5_c[s], 16)
            for s in range(ST):
                act.wait_ge(s5_out, s + 1)
                if s + 4 < ST:
                    act.dma_start(cmat[:, s % 4], a["ssm_c"][s + 4]).then_inc(s5_c[s % 4], 16)
                if s % 4 == 3:
                    i = s // 4
                    act.wait_ge(s5_y, i + 1)
                    copy(gy[:, i], gy[:, i], ACT.Gelu_apprx_tanh).then_inc(s5_gelu, 1)
            act.wait_ge(s5_gelu, 4)
            for c in range(4):
                copy(gy_high[:, c], gy[:, c], ACT.Copy).then_inc(glu_rounded, 1)
            for c in range(4):
                n = FIRST["glu"] + c // 2
                if c % 2 == 0:
                    split_high(act, n + 2)
                    act.wait_ge(slot_used, n + 1)
                if c >= 2:
                    act.wait_ge(glu_prod, c - 1)
                copy(gsig[:, c % 2], bank[:, c], ACT.Sigmoid, bias=v_("b_glu", c)).then_inc(glu_sig, 1)
                act.wait_ge(glu_prod, c + 1)
                copy(y_high[:, 4 + c], gprod[:, c % 2], ACT.Copy).then_inc(y_rounded, 1)

            merge_scalar("merge2", 3, 16, VECTOR_AT["b_gate"][0])
            splits("out2")
            norm_scalar(act, "n_ffn")

            with act.Fori(0, 11) as i:
                for q in range(2):
                    n = FIRST["up2"] + 2 * q
                    for g, dst in ((0, ff_a), (1, ff_v)):
                        split_high(act, n + 2 + g, i)
                        act.wait_ge(slot_used, i * 4 + (n + 1 + g))
                        if g == 0:
                            act.wait_ge(up_prod, i * 2 + (22 + q + 1))
                        wc, bc = VECTOR_AT["conv_w"][0] + 88 + 22 * g + q, VECTOR_AT["conv_b"][0] + 22 * g + q
                        copy(dst[:, q], bank[:, 2 * q + g], ACT.Identity, scale=vec[:, bass.ds(i * 2 + wc, 1)],
                             bias=vec[:, bass.ds(i * 2 + bc, 1)]).then_inc(up_centre, 1)
                    act.wait_ge(up_conv, i * 4 + (4 + 2 * q + 1))
                    copy(ff_s[:, q], ff_a[:, q], ACT.Silu).then_inc(up_gate, 1)
                    act.wait_ge(up_prod, i * 2 + (22 + q + 3))
                    copy(hid_high[:, bass.ds(i * 2 + q, 1)].rearrange("p a n -> p (a n)"), ff_p[:, q], ACT.Copy) \
                        .then_inc(up_rounded, 1)
            down_splits("down2")
            for k in range(8):
                act.wait_ge(out_added, 4 + 24 + k + 1)
                act.dma_start(out[k], x[:, k]).then_inc(stored, 16)
            act.wait_ge(stored, 16 * 8)

        @block.tensor
        def _(pe):
            mm = nc.tensor.matmul
            pe.wait_ge(first_loaded, 48)
            norm_tensor(pe, NORM["n_x1"])
            norm_tensor(pe, NORM["n_ctx"])

            def ready(n):
                pe.wait_ge(low_ready, n + 1)

            pe.wait_ge(norm_done, NORM["n_x1"]["done"])
            for j in range(4):
                n = FIRST["q"] + j
                ready(n)
                tile_product(bank[:, j], n % RING, 0, H).then_inc(slot_used, 1)
            pe.wait_ge(norm_done, NORM["n_ctx"]["done"])
            for j in range(4):
                n = FIRST["k"] + j
                ready(n)
                pe.wait_ge(qkv_copied, j + 1)
                tile_product(bank[:, j], n % RING, 0, H)
                tile_product(bank[:, 4 + j, 0:CTX], n % RING, 0, HC).then_inc(slot_used, 1)
            pe.wait_ge(qkv_copied, 12)

            def token_major(stage, groups):
                for i in range(4):
                    n = FIRST[stage] + i
                    ready(n)
                    for kk in range(2):
                        k = 2 * i + kk
                        wh, wl = (r[:, n % RING, kk * 512:kk * 512 + 512] for r in (ring_high, ring_low))
                        for b, (ah, al), t in groups:
                            s = slice(t * P, (t + 1) * P)
                            last = product(bank[:, b], ah[:, k, s], al[:, k, s], wh, wl, k == 0, k == 7)
                    last.then_inc(slot_used, 1)

            token_major("v", [(t, (h_high, h_low), t) for t in range(TT)] + [(4 + t, (hc_high, hc_low), t) for t in range(CT)])
            pe.wait_ge(qkv_copied, 18)
            pe.wait_ge(rope_done, 8)
            att_tensor(pe, 0, ATT1)
            turn_tensor(pe, o_tok1, ATT1, 0)

            pe.wait_ge(filt_loaded, 16 * 5)
            pe.wait_ge(y_split, 4)
            mm(bank[0:FW, 0], w12f[0:EMB, 0, 0:FW], zt[0:EMB, 0], start=True, stop=True).then_inc(hid_made, 1)
            pe.wait_ge(hid_ready, 1)
            mm(bank[0:FW, 0], w12f[0:FW, 0, FW:2 * FW], hid[0:FW, 0], start=True, stop=True).then_inc(hid_made, 1)
            pe.wait_ge(hid_ready, 2)
            for n in range(2):
                for t in range(TT):
                    if 4 * n + t >= 2:
                        pe.wait_ge(filt_summed, 4 * n + t - 1)
                    for d in range(2):
                        last = mm(bank[:, 2 * (t % 2) + d], hid[0:FW, 1, t * P:(t + 1) * P], w3f[0:FW, 2 * d + n],
                                  start=True, stop=True)
                    last.then_inc(filt_made, 1)
                pe.wait_ge(filt_summed, 4 * n + 4)
                for f in range(4):
                    if 4 * n + f >= 2:
                        pe.wait_ge(k_copied, 4 * n + f - 1)
                    for d in range(2):
                        for t in range(TT):
                            last = mm(bank[:, 4 + 2 * (f % 2) + d], dft[:, 4 * d + t, f * P:(f + 1) * P], filt[:, 4 * d + t],
                                      start=(t == 0), stop=(t == 3))
                    last.then_inc(k_made, 1)

            with pe.Fori(0, 3) as part:
                for j in range(4):
                    n = FIRST["hyena_in"] + j
                    pe.wait_ge(low_ready, part * 4 + (n + 1))
                    pe.wait_ge(conv_done, part * 4 + (j + 1))
                    tile_product(bank[:, j], n % RING, 0, H).then_inc(slot_used, 1)
            pe.wait_ge(conv_done, 4 + 12)
            pe.wait_ge(k_copied, 8)
            for n in range(2):
                for t in range(TT):
                    for c in range(4):
                        last = nc.tensor.transpose(bank[:, t, c * P:(c + 1) * P], hyu[:, c, t * P:(t + 1) * P], ident[:, :])
                    last.then_inc(z_turned, 1)
                pe.wait_ge(z_copied, 4 * n + 4)
                pe.wait_ge(dft_loaded, 16)
                for f in range(4):
                    if 4 * n + f >= 2:
                        pe.wait_ge(y_made, 4 * n + f - 1)
                    for d in range(2):
                        for t in range(TT):
                            last = mm(bank[:, 4 + 2 * (f % 2) + d], dft[:, 4 * d + t, f * P:(f + 1) * P], z_tok[:, t],
                                      start=(t == 0), stop=(t == 3))
                    last.then_inc(u_made, 1)
                pe.wait_ge(y_made, 4 * n + 4)
                for c in range(4):
                    for f in range(4):
                        mm(bank[:, c], y_re[:, f, c * P:(c + 1) * P], dft[:, f], start=(f == 0), stop=False)
                        last = mm(bank[:, c], y_im[:, f, c * P:(c + 1) * P], dft[:, 4 + f], start=False, stop=(f == 3))
                    last.then_inc(z_back, 1)
                pe.wait_ge(z_done, 4 * n + 4)

            def merge_tensor(stage, branches, tiles):
                with pe.Fori(0, branches) as b:
                    for p in range(4):
                        q = 4 * (p % 2)
                        for i in range(2):
                            n = FIRST[stage] + 3 * p + i
                            pe.wait_ge(low_ready, b * 12 + (n + 1))
                            pe.wait_ge(merge_added, b * 8 + (tiles + 2 * p + i + 1))
                            tile_product(bank[:, q + i], n % RING, 0, H).then_inc(slot_used, 1)
                        n = FIRST[stage] + 3 * p + 2
                        pe.wait_ge(low_ready, b * 12 + (n + 1))
                        ys = [(y_high[:, bass.ds(b * 4 + k, 1)].rearrange("p a n -> p (a n)"),
                               y_low[:, bass.ds(b * 4 + k, 1)].rearrange("p a n -> p (a n)")) for k in range(4)]
                        for i in range(2):
                            last = tile_product(bank[:, q + 2 + i], n % RING, 4 * i, ys)
                        last.then_inc(slot_used, 1)

            def out_tensor(stage, tiles):
                with pe.Fori(0, 2) as i:
                    for j in range(4):
                        n = FIRST[stage] + j
                        pe.wait_ge(low_ready, i * 4 + (n + 1))
                        pe.wait_ge(out_added, i * 4 + (tiles + j + 1))
                        tile_product(bank[:, j], n % RING, 0, M_).then_inc(slot_used, 1)

            def up_tensor(stage, freed, before, each):
                with pe.Fori(0, 11) as i:
                    for q in range(2):
                        for g in range(2):
                            n = FIRST[stage] + 2 * q + g
                            pe.wait_ge(low_ready, i * 4 + (n + 1))
                            if g == 0:
                                pe.wait_ge(freed, i * (2 * each) + (before + each * (q + 1)))
                            tile_product(bank[:, 2 * q + g], n % RING, 0, H).then_inc(slot_used, 1)

            def down_tensor(stage):
                for half in range(2):
                    def one(n, hidden, wait, start, stop):
                        pe.wait_ge(low_ready, wait)
                        for kk in range(2):
                            ah, al = hidden(kk)
                            for m in range(4):
                                wh, wl = block_of(n % RING, 4 * kk + m)
                                last = product(bank[:, 4 * half + m], wh, wl, ah, al, start and kk == 0, stop and kk == 1)
                        last.then_inc(slot_used, 1)

                    base = FIRST[stage] + 11 * half
                    one(base, lambda kk: (hid_high[:, kk], hid_low[:, kk]), base + 1, True, False)
                    with pe.Fori(0, 2) as i:
                        for j in range(4):
                            def tiles(kk, j=j):
                                k = bass.ds(i * 8 + (2 * (1 + j) + kk), 1)
                                return tuple(t[:, k].rearrange("p a n -> p (a n)") for t in (hid_high, hid_low))
                            one(base + 1 + j, tiles, i * 4 + (base + 1 + j + 1), False, False)
                    for m in (9, 10):
                        one(base + m, lambda kk, m=m: (hid_high[:, 2 * m + kk], hid_low[:, 2 * m + kk]), base + m + 1,
                            False, m == 10)

            pe.wait_ge(y_split, 8)
            merge_tensor("merge1", 2, 0)
            pe.wait_ge(merge_low, 16)
            out_tensor("out1", 0)
            norm_tensor(pe, NORM["n_x2"])
            pe.wait_ge(norm_done, NORM["n_x2"]["done"])
            up_tensor("up1", up_prod, 0, 1)
            pe.wait_ge(up_low, 22)
            down_tensor("down1")
            pe.wait_ge(out_added, 4 + 16)
            norm_tensor(pe, NORM["n_final"])
            norm_tensor(pe, NORM["n_mem"])
            norm_tensor(pe, NORM["n_mix"])
            pe.wait_ge(norm_done, NORM["n_mix"]["done"])
            for j in range(4):
                n = FIRST["mem_k"] + j
                ready(n)
                tile_product(bank[:, j, 0:CTX], n % RING, 0, HM).then_inc(slot_used, 1)
            token_major("mem_v", [(4 + t, (hm_high, hm_low), t) for t in range(CT)])
            for j in range(14):
                n = FIRST["in2"] + j
                ready(n)
                pe.wait_ge(in_copied, j + 1 if j < 4 else IN_MEM + j - 3)
                tile_product(bank[:, j % 4], n % RING, 0, H).then_inc(slot_used, 1)
            pe.wait_ge(in_copied, IN_IN2)
            heads_tensor(pe, 0, 2)
            pe.wait_ge(heads_done, 8)
            att_tensor(pe, ATT1, ATT2)
            turn_tensor(pe, o_tok2, ATT2, 8)

            norm_tensor(pe, NORM["n_cq"])
            norm_tensor(pe, NORM["n_ckv"])
            pe.wait_ge(y_split, 12)
            pe.wait_ge(norm_done, NORM["n_ckv"]["done"])
            for j in range(4):
                n = FIRST["q_b"] + j
                ready(n)
                for i in range(2):
                    h = 2 * j + i
                    if h >= 4:
                        pe.wait_ge(in_copied, IN_IN2 + h - 3)
                    for k, (ah, al) in enumerate(CQ):
                        wh, wl = block_of(n % RING, 3 * i + k, DQK)
                        last = product(bank[0:DQK, h % 4], wh, wl, ah, al, k == 0, k == 2)
                last.then_inc(slot_used, 1)
            n = FIRST["kv_b"]
            ready(n)
            pe.wait_ge(in_copied, IN_QB)
            for m in range(4):
                last = tile_product(bank[:, m], n % RING, 2 * m, CKV)
            last.then_inc(slot_used, 1)
            ready(n + 1)
            for t in range(TT):
                for k in range(2):
                    s = slice(t * P, (t + 1) * P)
                    wh, wl = (r[:, (n + 1) % RING, k * 512:k * 512 + 512] for r in (ring_high, ring_low))
                    last = product(bank[:, 4 + t], ckv_high[:, k, s], ckv_low[:, k, s], wh, wl, k == 0, k == 1)
            last.then_inc(slot_used, 1)
            pe.wait_ge(in_copied, IN_V)
            heads_tensor(pe, 2, 6)
            pe.wait_ge(in_copied, IN_KR)
            att_tensor(pe, ATT2, ATT3)
            turn_tensor(pe, o_tok3, ATT3, 12)

            pe.wait_ge(y_split, 16)

            def s5_output(s):
                pe.wait_ge(s5_states, s + 1)
                i = s // 4
                if s % 4 == 0 and i >= 2:
                    pe.wait_ge(s5_y, i - 1)
                for r in range(2):
                    last = mm(bank[:, 4 + i % 2], cmat[:, s % 4, r * P:(r + 1) * P], s5s[:, 2 * (s % 2) + r],
                              start=(s % 4 == 0 and r == 0), stop=(s % 4 == 3 and r == 1))
                last.then_inc(s5_out, 1)

            for s in range(ST):
                if s == 0:
                    pe.wait_ge(s5_b, 16 * 2)
                if s >= 2:
                    pe.wait_ge(s5_rotated, s - 1)
                for r in range(2):
                    last = mm(bank[:, 2 * (s % 2) + r], bmat[:, 4 * (s // 8) + 2 * r + s % 8 // 4, (s % 4) * P:(s % 4 + 1) * P],
                              u_ssm[:, s // 4], start=True, stop=True)
                last.then_inc(s5_in, 1)
                if s >= 1:
                    s5_output(s - 1)
            s5_output(ST - 1)
            pe.wait_ge(glu_low, 4)
            pe.wait_ge(s5_rotated, ST)
            for j in range(2):
                n = FIRST["glu"] + j
                ready(n)
                for i in range(2):
                    last = tile_product(bank[:, 2 * j + i], n % RING, 4 * i, GY)
                last.then_inc(slot_used, 1)
            pe.wait_ge(y_split, 20)
            merge_tensor("merge2", 3, 16)
            pe.wait_ge(merge_low, 16 + 24)
            out_tensor("out2", 16)
            norm_tensor(pe, NORM["n_ffn"])
            pe.wait_ge(norm_done, NORM["n_ffn"]["done"])
            up_tensor("up2", up_conv, 0, 2)
            pe.wait_ge(up_low, 44)
            down_tensor("down2")

        @block.vector
        def _(dve):
            link = Chain(dve, dve_step)
            tt, ts, stt = nc.vector.tensor_tensor, nc.vector.tensor_scalar, nc.vector.scalar_tensor_tensor
            MAGIC = 12582912.0
            TAU = (6.28125, 0.0019350051879882812, 3.019915981956753e-07)

            def reduce_angle(value, whole, last):
                link(ts(whole, value, 1.0 / (2 * math.pi), MAGIC, ALU.mult, ALU.add))
                link(ts(whole, whole, -MAGIC, None, ALU.add))
                for part in TAU:
                    link(stt(out=value, in0=whole, scalar=-part, in1=value, op0=ALU.mult, op1=ALU.add))
                return ts(last, value, 3.1415925, -3.1415925, ALU.min, ALU.max)

            dve.sem_inc(conv_done, 4)
            dve.sem_inc(merge_added, 4)
            dve.sem_inc(out_added, 4)
            dve.sem_inc(up_prod, 2)
            dve.sem_inc(up_conv, 4)

            dve.wait_ge(first_loaded, 48)

            def modulation(weights, rows, m, target, used):
                nc.vector.tensor_tensor_reduce(ada_prod[:, 0], weights, rows[:, 0], 1.0, v_("b_ada", m), ALU.mult, ALU.add,
                                               target[:, m:m + 1]).then_inc(used, 1)

            for which, (rows, target) in enumerate(((silu_rows, mod), (silu_rows_c, mod_c))):
                dve.wait_ge(silu_ready, which + 1)
                for m in range(ADA_FIRST):
                    if which == 0 and m % 4 == 0:
                        dve.wait_ge(ada_first_loaded[m // 4], 16 * 4)
                    n = which * ADA_FIRST + m
                    if n:
                        dve.wait_ge(ada_first_used, n)
                    modulation(ada_first[m], rows, m, target, ada_first_used)
                dve.wait_ge(ada_first_used, (which + 1) * ADA_FIRST)
                gain = (gain1, gain1_c)[which]
                stt(out=gain[:, :], in0=target[:, 8:16], scalar=1.0, in1=v_("norm1", 0, 8), op0=ALU.add, op1=ALU.mult) \
                    .then_inc(mod_ready, 1)
                dve.wait_ge(mod_ready, which + 1)
                norm_vector(dve, link, NORM["n_ctx" if which else "n_x1"])

            dve.wait_ge(trig_loaded, 16)
            for src, dst, count in [(q_scaled, q_rot, lambda j: j + 1), (k_plain, k_rot, lambda j: 4 + 2 * j + 1)]:
                for j in range(4):
                    dve.wait_ge(qkv_copied, count(j))
                    link(nc.vector.stream_shuffle(rope_t[:, 0], src[:, j], mask=MASK_SWAP))
                    link(tt(rope_t[:, 0], rope_t[:, 0], trig1[:, 1], ALU.mult))
                    link(tt(rope_t[:, 1], src[:, j], trig1[:, 0], ALU.mult))
                    tt(dst[:, j], rope_t[:, 0], rope_t[:, 1], ALU.add).then_inc(rope_done, 1)
                    dve.wait_ge(rope_done, j + 1 if src is q_scaled else 5 + j)
            def late_modulation(n):
                dve.wait_ge(ada_late_loaded[n % LATE_RING], 16 * (n // LATE_RING + 1))
                if n:
                    dve.wait_ge(ada_late_used, n)
                modulation(ada_late[n % LATE_RING], silu_rows, ADA_FIRST + n, mod, ada_late_used)

            att_vector(dve, link, 0, ATT1, late_modulation)
            dve.wait_ge(ada_late_used, ADA_SLOTS - ADA_FIRST)
            link(stt(out=gain2[:, :], in0=mod[:, 32:40], scalar=1.0, in1=v_("norm2", 0, 8), op0=ALU.add, op1=ALU.mult))
            turn_vector(dve, 0, 0)

            dve.wait_ge(filt_loaded, 16 * 5)
            for i in range(2):
                dve.wait_ge(hid_made, i + 1)
                if i:
                    dve.wait_ge(hid_ready, 1)
                link(ts(arg[0:FW, 0], bank[0:FW, 0], v_(f"hy_b{i + 1}", 0, 1, 0, FW), v_("hy_freq", 0, 1, 0, FW), ALU.add, ALU.mult))
                reduce_angle(arg[0:FW, 0], arg[0:FW, 1], arg[0:FW, 0]).then_inc(arg_ready, 1)
            dve.wait_ge(hid_ready, 2)
            for n in range(2):
                for t in range(TT):
                    dve.wait_ge(filt_made, 4 * n + t + 1)
                    if n and t == 0:
                        dve.wait_ge(k_made, 4)
                    b = 2 * (t % 2)
                    link(tt(arg[:, 0], bank[:, b], decay[:, t], ALU.mult))
                    link(tt(arg[:, 1], bank[:, b + 1], decay[:, t], ALU.mult))
                    if t == 0:
                        link(nc.vector.memset(arg[0:1, 1], 0.0))
                    link(tt(filt[:, t], arg[:, 0], arg[:, 1], ALU.add))
                    tt(filt[:, 4 + t], arg[:, 0], arg[:, 1], ALU.subtract).then_inc(filt_summed, 1)
                    dve.wait_ge(filt_summed, 4 * n + t + 1)

            with dve.Fori(0, 3) as part:
                start = link.count
                link.count = start + part * 4
                for j in range(4):
                    dve.wait_ge(conv_centre, part * 4 + (j + 1))
                    tile = bass.ds(part * 4 + j, 1)
                    later = hyu[:, tile, 1:T].rearrange("p a n -> p (a n)")
                    sooner = hyu[:, tile, 0:T - 1].rearrange("p a n -> p (a n)")
                    w0, w2 = (VECTOR_AT["hy_conv_w"][0] + tap * 12 + j for tap in (0, 2))
                    link(stt(out=later, in0=bank[:, j, 0:T - 1], scalar=vec[:, bass.ds(part * 4 + w0, 1)], in1=later,
                             op0=ALU.mult, op1=ALU.add))
                    stt(out=sooner, in0=bank[:, j, 1:T], scalar=vec[:, bass.ds(part * 4 + w2, 1)], in1=sooner,
                        op0=ALU.mult, op1=ALU.add).then_inc(conv_done, 1)
            link.count = start + 12
            dve.wait_ge(conv_done, 4 + 12)
            dve.wait_ge(k_copied, 8)
            for n in range(2):
                for f in range(4):
                    dve.wait_ge(u_made, 4 * n + f + 1)
                    b = 4 + 2 * (f % 2)
                    kre, kim = spec[n][:, f], spec[n][:, 4 + f]
                    link(tt(y_re[:, f], bank[:, b], kre, ALU.mult))
                    link(tt(hyt[:, 0], bank[:, b + 1], kim, ALU.mult))
                    link(tt(y_re[:, f], y_re[:, f], hyt[:, 0], ALU.subtract))
                    link(tt(y_im[:, f], bank[:, b], kim, ALU.mult))
                    link(tt(hyt[:, 1], bank[:, b + 1], kre, ALU.mult))
                    tt(y_im[:, f], y_im[:, f], hyt[:, 1], ALU.add).then_inc(y_made, 1)
                    dve.wait_ge(y_made, 4 * n + f + 1)
                for c in range(4):
                    dve.wait_ge(z_back, 4 * n + c + 1)
                    link(stt(out=hyz[:, c], in0=hyu[:, c], scalar=v_("hy_bias", 4 * n + c), in1=bank[:, c],
                             op0=ALU.mult, op1=ALU.add))
                    dst = hyu[:, c] if n == 0 else hyz[:, c]
                    tt(dst, hyz[:, c], hyu[:, 4 + 4 * n + c], ALU.mult).then_inc(z_done, 1)
                    dve.wait_ge(z_done, 4 * n + c + 1)
            for c in range(4):
                dve.wait_ge(y_rounded, 4 + c + 1)
                tt(y_low[:, 4 + c], hyz[:, c], y_high[:, 4 + c], ALU.subtract).then_inc(y_split, 1)
            dve.wait_ge(y_split, 8)

            def merge_vector(stage, branches, tiles):
                link(nc.vector.memset(merged[:, :, :].rearrange("p a n -> p (a n)"), 0.0))
                start = link.count
                with dve.Fori(0, branches) as b:
                    link.count = start + b * 8
                    for p in range(4):
                        q = 4 * (p % 2)
                        dve.wait_ge(slot_used, b * 12 + (FIRST[stage] + 3 * p + 3))
                        for i in range(2):
                            g = 2 * p + i
                            dve.wait_ge(merge_sig, b * 8 + (tiles + g + 1))
                            link(tt(mprod[:, i], sig[:, i], bank[:, q + 2 + i], ALU.mult))
                            tt(merged[:, g], merged[:, g], mprod[:, i], ALU.add).then_inc(merge_added, 1)
                        for i in range(2):
                            g = 2 * p + i
                            dve.wait_ge(merge_rounded, b * 8 + (tiles + g + 1))
                            tt(m_low[:, g], merged[:, g], m_high[:, g], ALU.subtract).then_inc(merge_low, 1)
                link.count = start + branches * 8
                dve.wait_ge(merge_low, tiles + branches * 8)

            def add_to_x(k, b, gate):
                xk = x[:, k] if isinstance(k, int) else x[:, bass.ds(k, 1)].rearrange("p a n -> p (a n)")
                if gate is None:
                    return tt(xk, xk, bank[:, b], ALU.add)
                g = mod[:, gate + k:gate + k + 1] if isinstance(k, int) else mod[:, bass.ds(k + gate, 1)]
                return stt(out=xk, in0=bank[:, b], scalar=g, in1=xk, op0=ALU.mult, op1=ALU.add)

            def out_vector(stage, gate):
                with dve.Fori(0, 2) as i:
                    for j in range(4):
                        dve.wait_ge(slot_used, i * 4 + (FIRST[stage] + j + 1))
                        add_to_x(i * 4 + j, j, gate).then_inc(out_added, 1)

            def down_vector(stage, gate):
                for half in range(2):
                    dve.wait_ge(slot_used, FIRST[stage] + 11 * (half + 1))
                    for m in range(4):
                        add_to_x(4 * half + m, 4 * half + m, gate).then_inc(out_added, 1)

            merge_vector("merge1", 2, 0)
            dve.wait_ge(x_loaded, 32)
            out_vector("out1", 16)
            norm_vector(dve, link, NORM["n_x2"])
            with dve.Fori(0, 11) as i:
                for q in range(2):
                    hidden = bass.ds(i * 2 + q, 1)
                    dve.wait_ge(up_gate, i * 2 + (q + 1))
                    dve.wait_ge(slot_used, i * 4 + (FIRST["up1"] + 2 * q + 2))
                    tt(ff_p[:, q], ff_s[:, q], bank[:, 2 * q + 1], ALU.mult).then_inc(up_prod, 1)
                    dve.wait_ge(up_rounded, i * 2 + (q + 1))
                    tt(hid_low[:, hidden].rearrange("p a n -> p (a n)"), ff_p[:, q],
                       hid_high[:, hidden].rearrange("p a n -> p (a n)"), ALU.subtract).then_inc(up_low, 1)
                    dve.wait_ge(up_low, i * 2 + (q + 1))
            down_vector("down1", 40)

            norm_vector(dve, link, NORM["n_final"])
            norm_vector(dve, link, NORM["n_mem"])
            norm_vector(dve, link, NORM["n_mix"])
            def s5v(i, n=16):
                return s5[:, 16 * i:16 * i + n]

            LOG2E, LN2_HIGH, LN2_LOW = 1.4426950408889634, 0.693359375, -2.12194440e-4

            def exact_exp(dst, src, whole, rest, poly):
                bias = MAGIC + 127.0
                link(ts(rest, src, 88.0, -87.0, ALU.min, ALU.max))
                link(ts(whole, rest, LOG2E, bias, ALU.mult, ALU.add))
                link(ts(poly, whole, -bias, None, ALU.add))
                link(stt(out=rest, in0=poly, scalar=-LN2_HIGH, in1=rest, op0=ALU.mult, op1=ALU.add))
                link(stt(out=rest, in0=poly, scalar=-LN2_LOW, in1=rest, op0=ALU.mult, op1=ALU.add))
                link(ts(whole.bitcast(I32), whole.bitcast(I32), 23, None, ALU.logical_shift_left))
                link(ts(poly, rest, 1.0 / math.factorial(7), None, ALU.mult))
                for d in range(6, 0, -1):
                    link(stt(out=poly, in0=poly, scalar=1.0 / math.factorial(d), in1=rest, op0=ALU.add, op1=ALU.mult))
                link(stt(out=dst, in0=poly, scalar=1.0, in1=whole, op0=ALU.add, op1=ALU.mult))

            DT, TH, WH, RE, PO, AN, SI, CO, MAG, ARE, AIM, DEN, FRE, FIM, PR, PI_, NPR, NPI, NFI = range(19)
            exact_exp(s5v(DT), v_("log_dt", 0, 16), s5v(WH), s5v(RE), s5v(PO))
            link(tt(s5v(TH), v_("lam_im", 0, 16), s5v(DT), ALU.mult))
            reduce_angle(s5v(TH), s5v(WH), s5v(AN)).then_inc(s5_arg, 1)
            dve.wait_ge(s5_sin, 1)
            link(ts(s5v(TH), s5v(AN), math.pi / 2, None, ALU.add))
            reduce_angle(s5v(TH), s5v(WH), s5v(AN)).then_inc(s5_arg, 1)
            link(tt(s5v(ARE), v_("lam_re", 0, 16), s5v(DT), ALU.mult))
            exact_exp(s5v(MAG), s5v(ARE), s5v(WH), s5v(RE), s5v(PO))
            dve.wait_ge(s5_sin, 2)
            lr, li = v_("lam_re", 0, 16), v_("lam_im", 0, 16)
            link(tt(s5v(ARE), s5v(MAG), s5v(CO), ALU.mult))
            link(ts(s5v(ARE), s5v(ARE), -1.0, None, ALU.add))
            link(tt(s5v(AIM), s5v(MAG), s5v(SI), ALU.mult))
            link(tt(s5v(DEN), lr, lr, ALU.mult))
            link(tt(s5v(WH), li, li, ALU.mult))
            link(tt(s5v(DEN), s5v(DEN), s5v(WH), ALU.add))
            link(nc.vector.reciprocal(s5v(DEN), s5v(DEN)))
            link(tt(s5v(FRE), s5v(ARE), lr, ALU.mult))
            link(tt(s5v(WH), s5v(AIM), li, ALU.mult))
            link(tt(s5v(FRE), s5v(FRE), s5v(WH), ALU.add))
            link(tt(s5v(FRE), s5v(FRE), s5v(DEN), ALU.mult))
            link(tt(s5v(FIM), s5v(AIM), lr, ALU.mult))
            link(tt(s5v(WH), s5v(ARE), li, ALU.mult))
            link(tt(s5v(FIM), s5v(FIM), s5v(WH), ALU.subtract))
            link(tt(s5v(FIM), s5v(FIM), s5v(DEN), ALU.mult))
            link(ts(s5v(NFI), s5v(FIM), -1.0, None, ALU.mult))

            heads_vector(dve, 0, 2)
            dve.wait_ge(mask_loaded, 16)
            att_vector(dve, link, ATT1, ATT2)
            turn_vector(dve, 2, 8)

            norm_vector(dve, link, NORM["n_cq"])
            norm_vector(dve, link, NORM["n_ckv"])
            dve.wait_ge(pos_loaded, 16)
            dve.wait_ge(slot_used, FIRST["q_b"] + 4)
            value, whole = rope_w[64:96, 0], rope_w[64:96, 1]
            angle = rope_a[64:96, 0]
            link(nc.vector.tensor_copy(value, pos_i[64:96, 0]))
            link(ts(value, value, v_("inv_freq", 0, 1, 64, 96), None, ALU.mult))
            reduce_angle(value, whole, angle).then_inc(rope_arg, 1)
            dve.wait_ge(rope_sin, 1)
            link(ts(rope2[64:96, 1], rope2[64:96, 1], v_("rope_sign", 0, 1, 64, 96), None, ALU.mult))
            link(ts(value, angle, math.pi / 2, None, ALU.add))
            reduce_angle(value, whole, angle).then_inc(rope_arg, 1)
            dve.wait_ge(rope_sin, 2)
            heads_vector(dve, 2, 6)
            dve.wait_ge(heads_done, 24)

            def rotate(count, head):
                link(nc.vector.stream_shuffle(value, head, mask=MASK_SWAP))
                link(tt(value, value, rope2[64:96, 1], ALU.mult))
                link(tt(whole, head, rope2[64:96, 0], ALU.mult))
                tt(head, value, whole, ALU.add).then_inc(mla_roped, 1)
                dve.wait_ge(mla_roped, count + 1)

            for h in range(2):
                rotate(2 * h, qh[64:96, h])
                rotate(2 * h + 1, k_head[h][64:96])

            def double(k):
                pr, pi, npr, npi = s5v(PR), s5v(PI_), s5v(NPR), s5v(NPI)
                low_bits = LOW.bit_length() - 1
                if k < low_bits:
                    re, im = (powers[:, r].rearrange("p (a n) -> p a n", a=ST) for r in range(2))
                    m = 2 ** k
                else:
                    re, im = (powers_high[:, 0, r * 256:r * 256 + 256].rearrange("p (a n) -> p a n", a=ST) for r in range(2))
                    m = 2 ** (k - low_bits)
                if k == 0:
                    link(nc.vector.tensor_copy(pr, s5v(CO)))
                    link(nc.vector.tensor_copy(pi, s5v(SI)))
                if m == 1:
                    link(nc.vector.memset(re[:, :, 0:1], 1.0))
                    link(nc.vector.memset(im[:, :, 0:1], 0.0))
                new_re, new_im = re[:, :, m:2 * m], im[:, :, m:2 * m]
                tmp = rope_w[:, 0, 0:ST * m].rearrange("p (a n) -> p a n", a=ST)
                br, bi = (v.rearrange("p (a n) -> p a n", n=1).to_broadcast([P, ST, m]) for v in (pr, pi))
                link(tt(new_re, re[:, :, 0:m], br, ALU.mult))
                link(tt(tmp, im[:, :, 0:m], bi, ALU.mult))
                link(tt(new_re, new_re, tmp, ALU.subtract))
                link(tt(new_im, re[:, :, 0:m], bi, ALU.mult))
                link(tt(tmp, im[:, :, 0:m], br, ALU.mult))
                if 2 ** (k + 1) == T:
                    tt(new_im, new_im, tmp, ALU.add).then_inc(s5_powers, 1)
                    dve.wait_ge(s5_powers, 1)
                    return
                link(tt(new_im, new_im, tmp, ALU.add))
                link(tt(npr, pr, pr, ALU.mult))
                link(tt(npi, pi, pi, ALU.mult))
                link(tt(npr, npr, npi, ALU.subtract))
                link(tt(npi, pr, pi, ALU.mult))
                link(ts(pi, npi, 2.0, None, ALU.mult))
                link(nc.vector.tensor_copy(pr, npr))

            def rotate_ahead(n):
                h, t = divmod(n - ATT2, TT)
                if h + 2 < HEADS and t == 0:
                    rotate(2 * h + 4, qh[64:96, h + 2])
                if h + 2 < HEADS and t == 2:
                    rotate(2 * h + 5, k_head[h + 2][64:96])
                if t % 2 and (n - ATT2) // 2 < T.bit_length() - 1:
                    double((n - ATT2) // 2)

            att_vector(dve, link, ATT2, ATT3, rotate_ahead)
            turn_vector(dve, 0, 12)

            for s in range(ST):
                e_re, e_im = tab[:, 2 * (s % 2)], tab[:, 2 * (s % 2) + 1]
                in_re, in_im = bank[:, 2 * (s % 2)], bank[:, 2 * (s % 2) + 1]
                r0, r1, t0, t1 = s5r[:, 0], s5r[:, 1], s5t[:, 0], s5t[:, 1]
                o0, o1 = s5s[:, 2 * (s % 2)], s5s[:, 2 * (s % 2) + 1]
                dve.wait_ge(s5_in, s + 1)
                dve.wait_ge(s5_table, s + 1)
                link.mark(tt(r0, in_re, e_re, ALU.mult))
                real = link.mark(tt(t0, in_im, e_im, ALU.mult))
                link.mark(tt(r1, in_im, e_re, ALU.mult))
                imag = link.mark(tt(t1, in_re, e_im, ALU.mult))
                link.wait(real)
                real = link.mark(tt(r0, r0, t0, ALU.add))
                link.wait(imag)
                tt(r1, r1, t1, ALU.subtract).then_inc(s5_rotated, 1)
                decay_b = s5[:, 16 * MAG + s:16 * MAG + s + 1].to_broadcast([P, T])
                link.wait(real)
                link.mark(nc.vector.tensor_tensor_scan(t0, decay_b, r0, 0.0, ALU.mult, ALU.add))
                dve.wait_ge(s5_rotated, s + 1)
                scanned = link.mark(nc.vector.tensor_tensor_scan(t1, decay_b, r1, 0.0, ALU.mult, ALU.add))
                dve.wait_ge(s5_c[s % 4], 16 * (s // 4 + 1))
                c_re, c_im = cmat[:, s % 4, 0:P], cmat[:, s % 4, P:2 * P]
                f_re, f_im, nf_im = (s5[:, 16 * i + s:16 * i + s + 1] for i in (FRE, FIM, NFI))
                link.mark(ts(c_tmp[:, 0:P], c_im, f_im, None, ALU.mult))
                link(ts(c_tmp[:, P:2 * P], c_im, f_re, None, ALU.mult))
                link(stt(out=c_im, in0=c_re, scalar=nf_im, in1=c_tmp[:, P:2 * P], op0=ALU.mult, op1=ALU.subtract))
                link.mark(stt(out=c_re, in0=c_re, scalar=f_re, in1=c_tmp[:, 0:P], op0=ALU.mult, op1=ALU.subtract))
                if s >= 2:
                    dve.wait_ge(s5_out, s - 1)
                link.wait(scanned)
                link.mark(tt(o0, t0, e_re, ALU.mult))
                real = link.mark(tt(r0, t1, e_im, ALU.mult))
                link.mark(tt(o1, t0, e_im, ALU.mult))
                imag = link.mark(tt(r1, t1, e_re, ALU.mult))
                link.wait(real)
                link.mark(tt(o0, o0, r0, ALU.subtract))
                link.wait(imag)
                tt(o1, o1, r1, ALU.add).then_inc(s5_states, 1)
                dve.wait_ge(s5_states, s + 1)
                if s % 4 == 3:
                    i = s // 4
                    dve.wait_ge(s5_out, s + 1)
                    stt(out=gy[:, i], in0=u_ssm[:, i], scalar=v_("ssm_d", i), in1=bank[:, 4 + i % 2],
                        op0=ALU.mult, op1=ALU.add).then_inc(s5_y, 1)
            for c in range(4):
                dve.wait_ge(glu_rounded, c + 1)
                tt(gy_low[:, c], gy[:, c], gy_high[:, c], ALU.subtract).then_inc(glu_low, 1)
            for c in range(4):
                dve.wait_ge(glu_sig, c + 1)
                tt(gprod[:, c % 2], gsig[:, c % 2], gy[:, c], ALU.mult).then_inc(glu_prod, 1)
                dve.wait_ge(y_rounded, 16 + c + 1)
                tt(y_low[:, 4 + c], gprod[:, c % 2], y_high[:, 4 + c], ALU.subtract).then_inc(y_split, 1)
            dve.wait_ge(y_split, 20)

            merge_vector("merge2", 3, 16)
            out_vector("out2", None)
            norm_vector(dve, link, NORM["n_ffn"])
            start = link.count
            with dve.Fori(0, 11) as i:
                link.count = start + i * 4
                for q in range(2):
                    hidden = bass.ds(i * 2 + q, 1)
                    for g, dst in ((0, ff_a), (1, ff_v)):
                        dve.wait_ge(up_centre, i * 4 + (2 * q + g + 1))
                        w0, w1 = (VECTOR_AT["conv_w"][0] + 44 * tap + 22 * g + q for tap in (0, 1))
                        link(stt(out=dst[:, q, 1:T], in0=bank[:, 2 * q + g, 0:T - 1], scalar=vec[:, bass.ds(i * 2 + w1, 1)],
                                 in1=dst[:, q, 1:T], op0=ALU.mult, op1=ALU.add))
                        stt(out=dst[:, q, 2:T], in0=bank[:, 2 * q + g, 0:T - 2], scalar=vec[:, bass.ds(i * 2 + w0, 1)],
                            in1=dst[:, q, 2:T], op0=ALU.mult, op1=ALU.add).then_inc(up_conv, 1)
                    dve.wait_ge(up_conv, i * 4 + (4 + 2 * q + 2))
                    dve.wait_ge(up_gate, i * 2 + (22 + q + 1))
                    tt(ff_p[:, q], ff_s[:, q], ff_v[:, q], ALU.mult).then_inc(up_prod, 1)
                    dve.wait_ge(up_rounded, i * 2 + (22 + q + 1))
                    tt(hid_low[:, hidden].rearrange("p a n -> p (a n)"), ff_p[:, q],
                       hid_high[:, hidden].rearrange("p a n -> p (a n)"), ALU.subtract).then_inc(up_low, 1)
            link.count = start + 44
            down_vector("down2", None)
    return locals()


INS = ["x", "c", "c_ctx", "ctx", "mem", "stream", "vectors", "ones", "identity", "trig1", "bias", "hy_w3", "hy_z", "hy_w12", "decay",
       "dft1", "dft2", "cmask", "positions", "ssm_b", "ssm_c"]


def constants():
    out = {"ones": np.ones((P, P), np.float32), "identity": np.eye(P, dtype=np.float32)}
    t = np.arange(T)
    nf = HD // 4
    inv = 10000.0 ** (-np.arange(nf, dtype=np.float32) / nf)
    trig = np.zeros((P, 2, T), np.float32)
    for p in range(P):
        d = p % HD
        pos = (t // GRID_W if d < HD // 2 else t % GRID_W).astype(np.float32)
        ang = (pos * np.float32(inv[d % nf])).astype(np.float32).astype(np.float64)
        trig[p, 0] = np.cos(ang)
        trig[p, 1] = np.sin(ang) * (-1 if d % 32 < nf else 1)
    out["trig1"] = trig
    f32 = np.float32
    tl = np.linspace(0.0, 1.0, T, dtype=f32)
    w = (2.0 * math.pi * np.arange(T, dtype=f32) / T).astype(f32)
    bands = np.linspace(1e-4, (EMB - 1) // 2 - 1, (EMB - 1) // 2, dtype=f32)
    arg = (bands[:, None] * w[None, :]).astype(f32)
    out["hy_z"] = np.concatenate([tl[None], np.cos(arg), np.sin(-arg)], 0).astype(f32)
    deltas = np.abs(np.linspace(math.log(1e-2) / 1.5, math.log(1e-2) / 0.3, HYW, dtype=f32))
    out["decay"] = np.exp(-tl[:, None] * deltas[None, :]).astype(f32).reshape(TT, P, HYW).transpose(1, 0, 2).copy()
    n = np.arange(T, dtype=np.float64)
    for name, shift in (("dft1", 0.0), ("dft2", 0.5)):
        ang = 2 * math.pi * np.outer(n + shift, n + 0.5) / (2 * T)
        both = np.stack([np.cos(ang), np.sin(ang)]).astype(f32)
        out[name] = both.reshape(2, TT, P, T).transpose(2, 0, 1, 3).reshape(P, 8, T).copy()
    mask = np.zeros((P, T), f32)
    mask[:, T - P:] = np.where(np.arange(P)[None, :] <= np.arange(P)[:, None], 0.0, NEG)
    out["cmask"] = mask
    return out


def k_tiles(w, columns=P):
    k, n = w.shape
    return w.reshape(k // P, P, n).transpose(1, 0, 2)


def slots_by_tile(w):
    k, n = w.shape
    return w.reshape(k // P, P, n // P, P).transpose(2, 1, 0, 3).reshape(n // P, P, -1)


def slots_of(w, k_each, n_all):
    k, n = w.shape
    return w.reshape(k // P // k_each, k_each, P, n).transpose(0, 2, 1, 3).reshape(-1, P, k_each * n)


def slots_down(w):
    return np.concatenate([slots_of(np.ascontiguousarray(w[:, h * 512:h * 512 + 512]), 2, 512) for h in range(2)])


def slots_pairs(w1, w2):
    s1, s2 = slots_by_tile(w1), slots_by_tile(w2)
    return np.stack([s1, s2], 1).reshape(-1, P, SLOT)


def slots_merge(gates, outs):
    parts = []
    for g, o in zip(gates, outs):
        gs = slots_by_tile(g)
        os_ = slots_by_tile(o).reshape(4, 2, P, 512).transpose(0, 2, 1, 3).reshape(4, P, SLOT)
        for p in range(4):
            parts += [gs[2 * p:2 * p + 1], gs[2 * p + 1:2 * p + 2], os_[p:p + 1]]
    return np.concatenate(parts)


def padded(blocks, n=SLOT):
    out = np.zeros((1, P, n), blocks.dtype)
    out[0, :, :blocks.shape[1]] = blocks
    return out


def feature_columns(v):
    v = np.asarray(v).reshape(-1)
    if v.size % P:
        out = np.zeros((P, 1), np.float32)
        out[:v.size, 0] = v
        return out
    return v.reshape(-1, P).T


def lay_out(i):
    i = {k: np.asarray(v) for k, v in i.items()}
    d = constants()

    def tokens(v):
        return v[0].T.reshape(KD, P, -1).transpose(1, 0, 2).copy()

    d["x"], d["ctx"], d["mem"] = tokens(i["x"]), tokens(i["ctx"]), tokens(i["mem_2"])
    d["c"], d["c_ctx"] = i["c"].reshape(D), i["c_ctx"].reshape(D)
    d["positions"] = i["positions_2"].astype(np.int32).reshape(T)

    w_in = i["w_in"][0]
    part = lambda w, lo, n: np.ascontiguousarray(w[:, lo:lo + n])
    st = [np.ascontiguousarray(i["w_ada"][0].T).reshape(ADA_SLOTS, P, D), slots_by_tile(part(w_in, 0, 512)), slots_by_tile(part(w_in, 512, 512)),
          slots_of(part(w_in, 1024, 512), 2, 512), slots_by_tile(part(w_in, 1536, 1536)),
          slots_merge([part(w_in, 3072, 1024), part(w_in, 4096, 1024)], [i["w_na_o"][0], i["w_hy_o"][0]]),
          slots_by_tile(i["w_out"][0]), slots_pairs(i["ffn_w1"][0], i["ffn_w3"][0]), slots_down(i["ffn_w2"][0])]
    w_mem = i["w_mem_kv_2"][0]
    st += [slots_by_tile(part(w_mem, 0, 512)), slots_of(part(w_mem, 512, 512), 2, 512)]
    w2 = i["w_in_2"][0]
    kr = np.zeros((D, P), np.float32)
    kr[:, 64:96] = w2[:, QL + KVL:QL + KVL + DROPE]
    o = QL + KVL + DROPE
    st += [slots_by_tile(part(w2, 0, QL + KVL)), slots_by_tile(kr), slots_by_tile(part(w2, o + 512, 512)),
           slots_by_tile(part(w2, o, 512))]
    qb = k_tiles(i["w_q_b_2"][0]).reshape(P, 3, HEADS, DQK)
    for j in range(4):
        blocks = np.zeros((P, 2, 3, P), np.float32)
        blocks[:, :, :, :DQK] = qb[:, :, 2 * j:2 * j + 2].transpose(0, 2, 1, 3)
        st.append(padded(blocks.reshape(P, -1)))
    kvb = k_tiles(i["w_kv_b_2"][0]).reshape(P, 2, HEADS, 2, 64)
    st.append(kvb[:, :, :, 0].reshape(P, 2, 4, P).transpose(0, 2, 1, 3).reshape(1, P, SLOT))
    st.append(kvb[:, :, :, 1].reshape(1, P, SLOT))
    st.append(slots_by_tile(i["w_glu_2"][0]).reshape(2, 2, P, 512).transpose(0, 2, 1, 3).reshape(2, P, SLOT))
    gates = o + 1024
    st += [slots_merge([part(w2, gates + 1024 * b, 1024) for b in range(3)],
                       [i["w_o_mla_2"][0], i["w_o_ssm_2"][0], i["w_o_cross_2"][0]]),
           slots_by_tile(i["w_out_2"][0]), slots_pairs(part(i["w_up_2"][0], 0, FF), part(i["w_up_2"][0], FF, FF)),
           slots_down(i["w_down_2"][0])]
    d["stream"] = np.concatenate(st)
    assert d["stream"].shape == (ADA_SLOTS + NS, P, SLOT), d["stream"].shape

    rpb = i["na_rpb"][0]
    cq_ = np.arange(GRID_W)
    start = np.clip(cq_ - WIN_W // 2, 0, GRID_W - WIN_W)
    bias = np.full((HEADS, 2, GRID_W, TAPS, GRID_W), NEG, np.float32)
    for c in range(GRID_W):
        lo = start[c]
        for rr in range(2):
            rows = np.arange(TAPS) + 1 - rr
            bias[:, rr, c, :, lo:lo + WIN_W] = rpb[:, rows][:, :, lo - c + WIN_W - 1:lo - c + WIN_W - 1 + WIN_W]
    d["bias"] = bias.reshape(HEADS, P, TAPS * GRID_W)

    w3 = i["hy_ffn_w3"][0]
    d["hy_w3"] = w3.reshape(FW, 4, HYW).copy()
    w12 = np.zeros((FW, 2 * FW), np.float32)
    w12[:EMB, :FW] = i["hy_ffn_w1"][0]
    w12[:, FW:] = i["hy_ffn_w2"][0]
    d["hy_w12"] = w12

    b_all = np.zeros((2, ST, P, P), np.float32)
    c_all = np.zeros((ST, P, 2, P), np.float32)
    for r, (bn, cn) in enumerate((("ssm_b_re_2", "ssm_c_re_2"), ("ssm_b_im_2", "ssm_c_im_2"))):
        bm, cm = i[bn][0], i[cn][0]
        for g in range(32):
            s, half, ch = g // 2, g % 2, (g % 8) * 16
            b_all[r, s, ch:ch + 16, half * 64:half * 64 + 64] = bm[g].T
            c_all[s, half * 64:half * 64 + 64, r, ch:ch + 16] = cm[g].T
    d["ssm_b"] = b_all.reshape(2, 2, 8, P, P).transpose(1, 3, 0, 2, 4).reshape(2, P, 4, 512).copy()
    d["ssm_c"] = c_all.reshape(ST, P, 2 * P)

    sign = np.zeros(P, np.float32)
    sign[64:80], sign[80:96] = -1.0, 1.0
    freq = np.zeros(P, np.float32)
    inv = (np.float32(10000.0) ** (-np.arange(0, DROPE, 2, dtype=np.float32) / np.float32(DROPE))).astype(np.float32)
    freq[64:96] = np.tile(inv, 2)
    named = {
        "b_ada": i["b_ada"], "norm1": i["norm1_g"], "norm2": i["norm2_g"],
        "final": i["final_g"], "norm_mix": i["norm_mix_g_2"], "mem_norm": i["mem_norm_g_2"], "norm_ffn": i["norm_ffn_g_2"],
        "hy_conv_w": i["hy_conv_w"], "hy_conv_b": i["hy_conv_b"], "hy_bias": i["hy_bias"], "hy_b1": i["hy_ffn_b1"],
        "hy_b2": i["hy_ffn_b2"], "hy_freq": i["hy_sin_freq"], "conv_w": i["conv_w_2"], "conv_b": i["conv_b_2"],
        "b_gate": i["b_gate_2"], "b_glu": i["b_glu_2"], "q_a": i["q_a_norm_g_2"], "kv_a": i["kv_a_norm_g_2"],
        "q_norm": i["q_norm_g_2"], "k_norm": i["k_norm_g_2"], "xq": i["xq_norm_g_2"], "xk": i["xk_norm_g_2"],
        "lam_re": i["ssm_lambda_re_2"], "lam_im": i["ssm_lambda_im_2"],
        "log_dt": np.repeat(i["ssm_log_dt_2"].reshape(32, 1), NSTATE, 1), "ssm_d": i["ssm_d_2"],
        "inv_freq": freq, "rope_sign": sign, "zero": np.zeros(8 * P, np.float32), "eps": np.full(P, EPS, np.float32),
    }
    columns = [feature_columns(named[name]) for name, _ in VECTORS]
    assert [c.shape[1] for c in columns] == [n for _, n in VECTORS]
    d["vectors"] = np.concatenate(columns, 1).astype(np.float32, copy=False)
    return {k: np.ascontiguousarray(d[k]) for k in INS}


def kernel(**inputs):
    import concourse.bacc as bacc
    from concourse.bass_utils import run_bass_kernel_spmd

    arrays = lay_out(inputs)
    nc = bacc.Bacc("TRN2", target_bir_lowering=False, num_devices=1)
    aps = {k: nc.dram_tensor(f"in_{k}", v.shape, mybir.dt.from_np(v.dtype), kind="ExternalInput").ap()
           for k, v in arrays.items()}
    out = nc.dram_tensor("out_0", (KD, P, T), F32, kind="ExternalOutput").ap()
    build(nc, aps, out)
    r = run_bass_kernel_spmd(nc, [{f"in_{k}": v for k, v in arrays.items()}], core_ids=[0])
    y = r.results[0]["out_0"]
    return np.ascontiguousarray(y.reshape(D, T).T)[None]
```

```python
import math
from contextlib import ExitStack

import numpy as np

import concourse.bass as bass
from concourse import mybir

F32 = mybir.dt.float32
F32R = mybir.dt.float32r
I32 = mybir.dt.int32
ALU = mybir.AluOpType
ACT = mybir.ActivationFunctionType
AX = mybir.AxisListType

P = 128
T = 512
TT = T // P
D = 1024
KD = D // P
CTX = 256
CT = CTX // P
HEADS = 8
HD = 64
GRID_W = 64
GRID_R = T // GRID_W
WIN_H, WIN_W = 8, 16
NEG = -1e30
HYW = 512
HT = HYW // P
EMB = 33
FW = 64
FF = 2816
FT = FF // P
QL, KVL = 384, 256
DQK, DNOPE, DROPE, DV = 96, 64, 32, 64
XH = 4
NSTATE = 64
ST = 16
LOW = 32
RING = 4
SLOT = 1024
EPS = 1e-6
TAPS = 14

VECTORS = [
    ("b_ada", 48), ("norm1", 8), ("norm2", 8), ("final", 8), ("norm_mix", 8),
    ("mem_norm", 8), ("norm_ffn", 8), ("hy_conv_w", 36), ("hy_conv_b", 12), ("hy_bias", 8),
    ("hy_b1", 1), ("hy_b2", 1), ("hy_freq", 1), ("conv_w", 132), ("conv_b", 44), ("b_gate", 24),
    ("b_glu", 4), ("q_a", 3), ("kv_a", 2), ("q_norm", 1), ("k_norm", 1), ("xq", 1), ("xk", 1),
    ("lam_re", 16), ("lam_im", 16), ("log_dt", 16), ("ssm_d", 4), ("inv_freq", 1), ("rope_sign", 1),
    ("zero", 8), ("eps", 1),
]
VECTOR_AT = {}
NV = 0
for _name, _n in VECTORS:
    VECTOR_AT[_name] = (NV, _n)
    NV += _n

ADA_SLOTS = 48
ADA_FIRST = 16
LATE_RING = 4
STAGES = [
    ("q", 4), ("k", 4), ("v", 4), ("hyena_in", 12), ("merge1", 24), ("out1", 8), ("up1", 44),
    ("down1", 22), ("mem_k", 4), ("mem_v", 4), ("in2", 14), ("q_b", 4), ("kv_b", 2), ("glu", 2),
    ("merge2", 36), ("out2", 8), ("up2", 44), ("down2", 22),
]
FIRST = {}
NS = 0
for _name, _n in STAGES:
    FIRST[_name] = NS
    NS += _n

BASE = 16512
TILE_BYTES = 2048
X_AT, RAW_AT, RHIGH_AT, RLOW_AT, HHIGH_AT, HLOW_AT, W = 0, 8, 16, 24, 32, 40, 48
SMALL_AT = 100

MASK_SWAP = [(i + 16) % 32 for i in range(32)]


class Chain:

    def __init__(self, engine, semaphore):
        self.engine, self.semaphore, self.count = engine, semaphore, 0

    def mark(self, instruction):
        instruction.then_inc(self.semaphore, 1)
        self.count = self.count + 1
        return self.count

    def wait(self, count):
        self.engine.wait_ge(self.semaphore, count)

    def __call__(self, instruction):
        self.wait(self.mark(instruction))


def build(nc, a, out):
    ctx = ExitStack()
    with ctx:
        def at(name, tile, tiles, dtype=F32, width=512):
            return nc.alloc_sbuf_tensor_at(name, [P, tiles, width], dtype, offset=BASE + tile * TILE_BYTES)

        def sem(name):
            return ctx.enter_context(nc.semaphore(name))

        small_bytes = [0]

        def small(name, columns, dtype=F32):
            t = nc.alloc_sbuf_tensor_at(name, [P, columns], dtype, offset=BASE + SMALL_AT * TILE_BYTES + small_bytes[0])
            small_bytes[0] += (columns * 4 + 31) // 32 * 32
            return t

        bank = ctx.enter_context(nc.psum_tensor("bank", [P, 8, 512], F32))

        x = at("x", X_AT, 8)
        raw = at("raw", RAW_AT, RING, width=SLOT)
        ring_high = at("ring_high", RHIGH_AT, RING, F32R, SLOT)
        ring_low = at("ring_low", RLOW_AT, RING, F32R, SLOT)
        h_high = at("h_high", HHIGH_AT, 8, F32R)
        h_low = at("h_low", HLOW_AT, 8, F32R)

        vec = small("vec", NV)
        ones = small("ones", P)
        ident = small("ident", P)
        one_column = small("one_column", 31)
        mod = small("mod", 48)
        mod_c = small("mod_c", 16)
        gain1 = small("gain1", 8)
        gain1_c = small("gain1_c", 8)
        gain2 = small("gain2", 8)
        att_max = small("att_max", 4)
        att_neg = small("att_neg", 2)
        att_sums = small("att_sums", 4)
        att_total = small("att_total", 2)
        s5 = small("s5", 16 * 18)

        def v_(name, i=0, n=1, p0=0, p1=P):
            return vec[p0:p1, VECTOR_AT[name][0] + i:VECTOR_AT[name][0] + i + n]

        y_high = at("y_high", W + 28, 12, F32R)
        y_low = at("y_low", W + 40, 12, F32R)

        q_scaled = at("q_scaled", W, 4)
        q_rot = at("q_rot", W + 4, 4)
        k_rot = at("k_rot", W + 8, 4)
        v_tok = at("v_tok", W + 12, 4)
        kc = at("kc", W + 16, 4, width=CTX)
        vc = at("vc", W + 18, 2)
        trig1 = at("trig1", W + 20, 2)
        bias1 = at("bias1", W + 22, 2, width=TAPS * GRID_W)
        hc_high = at("hc_high", W + 32, 8, F32R, CTX)
        hc_low = at("hc_low", W + 36, 8, F32R, CTX)
        ctx_in = at("ctx_in", W, 8, width=CTX)
        att1_p = at("att1_p", W + 32, 2, width=768)
        att1 = dict(p=[att1_p[:, i] for i in range(2)], pt=at("att1_pt", W + 35, 2, width=768))
        rope_t = at("rope_t", W + 26, 2)
        k_plain = at("k_plain", W + 44, 4)

        first_tiles = [at("ada_first0", W + 4, 12, width=SLOT), at("ada_first1", W + 32, 4, width=SLOT)]
        ada_first = [first_tiles[i // 12][:, i % 12] for i in range(ADA_FIRST)]
        late_tiles = [at(f"ada_late{i}", W + tile, 1, width=SLOT) for i, tile in enumerate((38, 26, 44, 46))]
        ada_late = [late_tiles[i][:, 0] for i in range(LATE_RING)]

        silu_rows = at("silu_rows", W + 48, 1, width=SLOT)
        silu_rows_c = at("silu_rows_c", W + 28, 1, width=SLOT)
        ada_prod = at("ada_prod", W + 50, 1, width=SLOT)

        w3f = at("w3f", W + 0, 4)
        zt = at("zt", W + 4, 1)
        hid = at("hid", W + 5, 2)
        arg = at("arg", W + 7, 2)
        w12f = at("w12f", W + 9, 1)
        decay = at("decay", W + 44, 4)
        filt = at("filt", W + 32, 8)
        hyu = at("hyu", W + 0, 12)
        dft = at("dft", W + 12, 8)
        spec = [at("spec1", W + 20, 8), at("spec2", X_AT, 8)]
        z_tok = at("z_tok", W + 32, 4)
        y_re = at("y_re", W + 36, 4)
        y_im = at("y_im", W + 48, 4)
        hyt = at("hyt", W + 44, 2)
        hyz = at("hyz", W + 20, 4)

        merged = at("merged", W + 8, 8)
        m_high = at("m_high", W + 0, 8, F32R)
        m_low = at("m_low", W + 16, 8, F32R)
        sig = at("sig", W + 24, 2)
        mprod = at("mprod", W + 26, 2)

        hid_high = at("hid_high", W + 0, 22, F32R)
        hid_low = at("hid_low", W + 22, 22, F32R)
        ff_a = at("ff_a", W + 44, 2)
        ff_v = at("ff_v", W + 46, 2)
        ff_s = at("ff_s", W + 48, 2)
        ff_p = at("ff_p", W + 50, 2)

        mem_in = at("mem_in", W + 12, 8, width=CTX)
        hm_high = at("hm_high", W + 0, 8, F32R, CTX)
        hm_low = at("hm_low", W + 4, 8, F32R, CTX)
        kx = at("kx", W + 8, 4, width=CTX)
        vx = at("vx", W + 10, 2)
        cq = at("cq", W + 12, 3)
        ckv = at("ckv", W + 15, 2)
        kr = at("kr", W + 17, 1)
        xq = at("xq", W + 18, 4)
        u_ssm = at("u_ssm", W + 22, 4)
        cmask = at("cmask", W + 26, 1)
        cq_high = at("cq_high", W + 28, 3, F32R)
        cq_low = at("cq_low", W + 47, 3, F32R)
        ckv_high = at("ckv_high", W + 40, 2, F32R)
        ckv_low = at("ckv_low", W + 42, 2, F32R)
        att2_p = at("att2_p", W + 28, 3, width=CTX)
        att2 = dict(p=[att2_p[:, i] for i in range(3)], pt=at("att2_pt", W + 30, 2, width=CTX))
        qh = at("qh", W + 0, 8)
        kh = at("kh", W + 12, 4)
        kh2 = at("kh2", W + 18, 4)
        k_head = [kh[:, i] for i in range(4)] + [kh2[:, i] for i in range(4)]
        v_mla = at("v_mla", W + 8, 4)
        rope2 = at("rope2", W + 32, 2)
        rope_w = at("rope_w", W + 34, 2)
        rope_a = at("rope_a", W + 27, 1)
        pos_i = at("pos_i", W + 27, 1, I32)
        att3_p = at("att3_p", W + 43, 3)
        att3 = dict(p=[att3_p[:, i] for i in range(3)], pt=at("att3_pt", W + 46, 2))
        powers = at("powers", W + 16, 2)
        powers_high = at("powers_high", W + 27, 1)
        powers_tmp = at("powers_tmp", W + 31, 1)
        tab = at("tab", W + 0, 4)
        tab_tmp = at("tab_tmp", W + 4, 2)
        cmat = at("cmat", W + 6, 2)
        cmat_minus = at("cmat_minus", W + 26, 1)
        bmat = [at("bmat0", W + 12, 4), at("bmat1", W + 8, 4)]
        s5s = at("s5s", W + 18, 4)
        s5r = at("s5r", W + 32, 2)
        s5t = at("s5t", W + 34, 2)
        gy = at("gy", W + 44, 4)
        gy_high = at("gy_high", W + 4, 4, F32R)
        gy_low = at("gy_low", W + 8, 4, F32R)
        gsig = at("gsig", W + 12, 2)
        gprod = at("gprod", W + 14, 2)

        raw_loaded = [sem(f"raw_loaded{i}") for i in range(RING)]
        ada_first_loaded = [sem(f"ada_first_loaded{i}") for i in range(4)]
        ada_first_used = sem("ada_first_used")
        ada_late_loaded = [sem(f"ada_late_loaded{i}") for i in range(LATE_RING)]
        ada_late_used = sem("ada_late_used")
        high_ready = sem("high_ready")
        low_ready = sem("low_ready")
        slot_used = sem("slot_used")
        dve_step = sem("dve_step")
        act_step = sem("act_step")
        pool_step = sem("pool_step")
        s5_powers, s5_table = sem("s5_powers"), sem("s5_table")
        first_loaded = sem("first_loaded")
        x_loaded = sem("x_loaded")
        ctx_loaded = sem("ctx_loaded")
        silu_loaded, silu_ready = sem("silu_loaded"), sem("silu_ready")
        mod_ready = sem("mod_ready")
        norm_squared, norm_summed, norm_mean, norm_root, norm_scaled, norm_rounded, norm_done = (
            sem("norm_" + s) for s in ("squared", "summed", "mean", "root", "scaled", "rounded", "done"))
        att_scored, att_biased, att_exp, att_turned, att_copied, att_copied2, att_summed, att_scaled = (
            sem("att_" + s) for s in ("scored", "biased", "exp", "turned", "copied", "copied2", "summed", "scaled"))
        y_rounded, y_split = sem("y_rounded"), sem("y_split")
        in_copied, kr_copied, partner_shuffled = sem("in_copied"), sem("kr_copied"), sem("partner_shuffled")
        heads_squared, heads_summed, heads_log, heads_root, heads_spread, heads_done = (
            sem("heads_" + s) for s in ("squared", "summed", "log", "root", "spread", "done"))
        out_added = sem("out_added")
        bias_loaded = [sem("bias_loaded0"), sem("bias_loaded1")]
        trig_loaded = sem("trig_loaded")
        qkv_copied, rope_done = sem("qkv_copied"), sem("rope_done")

        def norm(name, tiles, width, size, gains, shifts=None, outs=None, split=None, scratch=W + 40, ready=None):
            rows = tiles[0].shape[0]
            return dict(name=name, tiles=tiles, width=width, size=size, gains=gains, shifts=shifts, outs=outs,
                        split=split, rows=rows, ready=ready,
                        sq=at(f"{name}_sq", scratch, 2), scratch=scratch,
                        t=at(f"{name}_t", scratch + 5, 2))

        def cols(t, n, rows=P):
            return [t[0:rows, i:i + 1] for i in range(n)]

        def vcols(name, n, rows=P):
            return [v_(name, i, 1, 0, rows) for i in range(n)]

        NORMS = [
            norm("n_x1", [x[:, k] for k in range(8)], T, D, cols(gain1, 8), cols(mod, 8),
                 split=([h_high[:, k] for k in range(8)], [h_low[:, k] for k in range(8)])),
            norm("n_ctx", [ctx_in[:, k] for k in range(8)], CTX, D, cols(gain1_c, 8), cols(mod_c, 8),
                 split=([hc_high[:, k] for k in range(8)], [hc_low[:, k] for k in range(8)])),
            norm("n_x2", [x[:, k] for k in range(8)], T, D, cols(gain2, 8), [mod[:, 24 + i:25 + i] for i in range(8)],
                 ready=(out_added, 4),
                 split=([h_high[:, k] for k in range(8)], [h_low[:, k] for k in range(8)])),
            norm("n_final", [x[:, k] for k in range(8)], T, D, vcols("final", 8), outs=[x[:, k] for k in range(8)],
                 scratch=W + 44, ready=(out_added, 4 + 16 - 8)),
            norm("n_mem", [mem_in[:, k] for k in range(8)], CTX, D, vcols("mem_norm", 8), scratch=W + 44,
                 split=([hm_high[:, k] for k in range(8)], [hm_low[:, k] for k in range(8)])),
            norm("n_mix", [x[:, k] for k in range(8)], T, D, vcols("norm_mix", 8), scratch=W + 44, ready=(norm_done, 24),
                 split=([h_high[:, k] for k in range(8)], [h_low[:, k] for k in range(8)])),
        ]
        NORMS += [
            norm("n_cq", [cq[:, k] for k in range(3)], T, QL, vcols("q_a", 3), scratch=W + 0, ready=(in_copied, 6),
                 split=([cq_high[:, k] for k in range(3)], [cq_low[:, k] for k in range(3)])),
            norm("n_ckv", [ckv[:, k] for k in range(2)], T, KVL, vcols("kv_a", 2), scratch=W + 0, ready=(in_copied, 9),
                 split=([ckv_high[:, k] for k in range(2)], [ckv_low[:, k] for k in range(2)])),
        ]
        NORMS += [norm("n_ffn", [x[:, k] for k in range(8)], T, D, vcols("norm_ffn", 8), ready=(out_added, 4 + 16),
                       split=([h_high[:, k] for k in range(8)], [h_low[:, k] for k in range(8)]))]
        NORM = {}
        squares = outputs = rounds = 0
        for i, n in enumerate(NORMS):
            n.update(index=i, bank=6 + i % 2, root=at(n["name"] + "_root", n["scratch"] + 2 + i % 2, 1), squares=squares, outputs=outputs, rounds=rounds)
            squares += len(n["tiles"])
            outputs += len(n["tiles"])
            rounds += len(n["tiles"]) if n["split"] else 0
            n["done"] = outputs
            NORM[n["name"]] = n

        def norm_scalar(act, *names, before_rounding=None):
            def squares(n):
                w, r = n["width"], n["rows"]
                for k, t in enumerate(n["tiles"]):
                    i = n["squares"] + k
                    if n["ready"]:
                        act.wait_ge(n["ready"][0], n["ready"][1] + k + 1)
                    if i >= 2:
                        act.wait_ge(norm_summed, i - 1)
                    nc.scalar.activation(n["sq"][0:r, i % 2, 0:w], t, ACT.Square, scale=float(n["size"]) ** -0.5) \
                      .then_inc(norm_squared, 1)

            norms = [NORM[name] for name in names]
            squares(norms[0])
            for n, later in zip(norms, norms[1:] + [None]):
                if later:
                    squares(later)
                w, r = n["width"], n["rows"]
                act.wait_ge(norm_summed, n["squares"] + len(n["tiles"]))
                if n["index"] >= 2:
                    act.wait_ge(norm_done, NORMS[n["index"] - 2]["done"])
                nc.scalar.activation(n["root"][0:r, 0, 0:w], bank[0:r, n["bank"], 0:w], ACT.Ln, bias=v_("eps", 0, 1, 0, r)) \
                  .then_inc(norm_mean, 1)
                act.wait_ge(norm_mean, n["index"] + 1)
                nc.scalar.activation(n["root"][0:r, 0, 0:w], n["root"][0:r, 0, 0:w], ACT.Exp, scale=-0.5) \
                  .then_inc(norm_root, 1)
                if before_rounding:
                    before_rounding()
                if n["split"]:
                    for k in range(len(n["tiles"])):
                        act.wait_ge(norm_scaled, n["rounds"] + k + 1)
                        shift = n["shifts"][k] if n["shifts"] else v_("zero")
                        nc.scalar.activation(n["split"][0][k], n["t"][0:r, k % 2, 0:w], ACT.Identity,
                                             bias=shift).then_inc(norm_rounded, 1)

        def norm_tensor(pe, n):
            w, r = n["width"], n["rows"]
            if n["index"] >= 2:
                pe.wait_ge(norm_mean, n["index"] - 1)
            for k in range(len(n["tiles"])):
                i = n["squares"] + k
                pe.wait_ge(norm_squared, i + 1)
                nc.tensor.matmul(bank[0:r, n["bank"], 0:w], ones[0:r, 0:r], n["sq"][0:r, i % 2, 0:w],
                                 start=(k == 0), stop=(k == len(n["tiles"]) - 1)).then_inc(norm_summed, 1)

        def norm_vector(dve, link, n):
            w, r = n["width"], n["rows"]
            m = len(n["tiles"])
            dve.wait_ge(norm_root, n["index"] + 1)
            root = n["root"][0:r, 0, 0:w]
            if not n["split"]:
                for k in range(m):
                    nc.vector.scalar_tensor_tensor(out=n["outs"][k], in0=n["tiles"][k], scalar=n["gains"][k], in1=root,
                                                   op0=ALU.mult, op1=ALU.mult).then_inc(norm_done, 1)
                dve.wait_ge(norm_done, n["done"])
                return
            for k in range(m + 1):
                if k < m:
                    if k >= 2:
                        dve.wait_ge(norm_done, n["outputs"] + k - 1)
                    nc.vector.scalar_tensor_tensor(out=n["t"][0:r, k % 2, 0:w], in0=n["tiles"][k], scalar=n["gains"][k],
                                                   in1=root, op0=ALU.mult, op1=ALU.mult).then_inc(norm_scaled, 1)
                if k >= 1:
                    j = k - 1
                    dve.wait_ge(norm_rounded, n["rounds"] + j + 1)
                    shift = n["shifts"][j] if n["shifts"] else v_("zero")
                    nc.vector.scalar_tensor_tensor(out=n["split"][1][j], in0=n["t"][0:r, j % 2, 0:w], scalar=shift,
                                                   in1=n["split"][0][j], op0=ALU.add, op1=ALU.subtract).then_inc(norm_done, 1)
            dve.wait_ge(norm_done, n["done"])

        BATCHES = []

        def batch(heads, ready, scratch):
            first = BATCHES[-1]["first"] + len(BATCHES[-1]["heads"]) if BATCHES else 0
            BATCHES.append(dict(index=len(BATCHES), heads=heads, ready=ready, first=first, done=first + len(heads),
                                sq=at(f"heads{len(BATCHES)}_sq", scratch, 2),
                                root=at(f"heads{len(BATCHES)}_root", scratch + 2, 1)[0:len(heads), 0]))

        batch([pair for h in range(XH) for pair in ((xq[:, h], "xq"), (kx[:, h], "xk"))]
              + [(qh[0:DQK, h], "q_norm") for h in range(HEADS)], 28, W + 44)
        batch([(k_head[h][0:DQK], "k_norm") for h in range(HEADS)], 36, W + 40)

        def heads_scalar(act, g):
            act.wait_ge(in_copied, g["ready"])
            for k, (t, _) in enumerate(g["heads"]):
                i = g["first"] + k
                r, w = t.shape
                if i >= 2:
                    act.wait_ge(heads_summed, i - 1)
                nc.scalar.activation(g["sq"][0:r, i % 2, 0:w], t, ACT.Square, scale=float(r) ** -0.5).then_inc(heads_squared, 1)
            n = len(g["heads"])
            act.wait_ge(heads_summed, g["done"])
            nc.scalar.activation(g["root"], bank[0:n, 6], ACT.Ln, bias=v_("eps", 0, 1, 0, n)).then_inc(heads_log, 1)
            act.wait_ge(heads_log, g["index"] + 1)
            nc.scalar.activation(g["root"], g["root"], ACT.Exp, scale=-0.5).then_inc(heads_root, 1)

        def heads_tensor(pe, g):
            n = len(g["heads"])
            for k, (t, _) in enumerate(g["heads"]):
                r, w = t.shape
                pe.wait_ge(heads_squared, g["first"] + k + 1)
                nc.tensor.matmul(bank[0:n, 6, 0:w], one_column[0:r, 15 - k:15 - k + n], g["sq"][0:r, (g["first"] + k) % 2, 0:w],
                                 start=(k == 0), stop=(k == n - 1)).then_inc(heads_summed, 1)
            pe.wait_ge(heads_root, g["index"] + 1)

        def spread(pe, g, k):
            r, w = g["heads"][k][0].shape
            n = len(g["heads"])
            if k >= 2:
                pe.wait_ge(heads_done, g["first"] + k - 1)
            nc.tensor.matmul(bank[0:r, 2 + k % 2, 0:w], ident[0:n, k:k + 1].to_broadcast([n, r]), g["root"][:, 0:w],
                             start=True, stop=True).then_inc(heads_spread, 1)

        def apply_roots(dve, g, k):
            t, gain = g["heads"][k]
            r, w = t.shape
            dve.wait_ge(heads_spread, g["first"] + k + 1)
            nc.vector.scalar_tensor_tensor(out=t, in0=t, scalar=v_(gain, 0, 1, 0, r), in1=bank[0:r, 2 + k % 2, 0:w],
                                           op0=ALU.mult, op1=ALU.mult).then_inc(heads_done, 1)

        ATT = []

        def half_rows(t, i, h):
            return t[64 * (h % 2):64 * (h % 2) + 64, i]

        for h in range(HEADS):
            for t in range(TT):
                qs = slice(t * P, t * P + P)
                ATT.append(dict(
                    at=att1, q=half_rows(q_rot, h // 2, h)[:, qs], k=half_rows(k_rot, h // 2, h),
                    table=bias1[:, h % 2, (6 - 2 * t) * GRID_W:(6 - 2 * t + 8) * GRID_W], width=T, scale=1.0,
                    q2=half_rows(q_scaled, h // 2, h)[:, qs], k2=half_rows(kc, h // 2, h),
                    values=[v_tok[:, i, h * HD:(h + 1) * HD] for i in range(TT)]
                    + [vc[:, i, h * HD:(h + 1) * HD] for i in range(CT)],
                    tile=h // 2, rows=64 * (h % 2), queries=qs, head=h, first=(t == 0)))
        ATT1 = len(ATT)
        for h in range(XH):
            for t in range(TT):
                ATT.append(dict(
                    at=att2, q=xq[:, h, t * P:t * P + P], k=kx[:, h], table=cmask[:, 0, 0:CTX], width=CTX,
                    scale=float(P) ** -0.5, q2=None,
                    values=[vx[:, i, h * P:(h + 1) * P] for i in range(CT)], tile=h, rows=0,
                    queries=slice(t * P, t * P + P)))
        ATT2 = len(ATT)
        for h in range(HEADS):
            for t in range(TT):
                w = (t + 1) * P
                ATT.append(dict(
                    at=att3, q=qh[0:DQK, h, t * P:t * P + P], k=k_head[h][0:DQK, 0:w], table=cmask[:, 0, T - w:T], width=w,
                    scale=float(DQK) ** -0.5, q2=None,
                    values=[v_mla[:, i, h * DV:(h + 1) * DV] for i in range(t + 1)], tile=h // 2, rows=64 * (h % 2),
                    queries=slice(t * P, t * P + P)))
        ATT3 = len(ATT)
        seconds = 0
        for s in ATT:
            keys = len(s["values"])
            s["near"] = (keys + 2) // 3
            s["seconds"] = seconds
            seconds += keys > s["near"]
            s["seconds_done"] = seconds
        for n, s in enumerate(ATT):
            s["buffers"] = len(s["at"]["p"])
            s["p"] = s["at"]["p"][n % s["buffers"]]
        ATT_Y = {0: (0, 0), ATT1: (2, 8), ATT2: (0, 12)}

        def ahead(n):
            h, t = divmod(n - ATT2, TT)
            return h + 2 if t == 0 and h + 2 < HEADS else None

        def last_of_tile(n, lo, hi):
            if lo <= n < hi and (n == hi - 1 or ATT[n + 1]["tile"] != ATT[n]["tile"]):
                return ATT[n]["tile"]
            return None

        def att_tensor(pe, lo, hi, between=None):
            def scores(n):
                s = ATT[n]
                if n >= 2:
                    pe.wait_ge(att_biased, n - 1)
                    pe.wait_ge(att_exp, n - 1)
                if ATT1 <= n < ATT2 and (n - ATT1) % TT == 0:
                    pe.wait_ge(heads_done, (n - ATT1) // TT * 2 + 2)
                if n >= ATT2 and (n - ATT2) % TT == 0:
                    pe.wait_ge(mla_roped, HEADS + (n - ATT2) // TT + 1)
                mm = nc.tensor.matmul(bank[:, n % 2, 0:s["width"]], s["q"], s["k"], start=True, stop=True)
                if s["q2"] is not None:
                    mm = nc.tensor.matmul(bank[:, 2 + n % 2, 0:CTX], s["q2"], s["k2"], start=True, stop=True)
                mm.then_inc(att_scored, 1)

            def turn(n):
                s = ATT[n]
                keys, near = len(s["values"]), s["near"]
                pe.wait_ge(att_scaled, n + 1)
                if n >= 1:
                    pe.wait_ge(att_copied, n)
                if s["seconds"] >= 1:
                    pe.wait_ge(att_copied2, s["seconds"])
                for i in range(keys):
                    b, c = (4, i) if i < near else (5, i - near)
                    mm = nc.tensor.transpose(bank[:, b, c * P:(c + 1) * P], s["p"][:, i * P:(i + 1) * P], ident[:, :])
                mm.then_inc(att_turned, 1)

            def weigh(n):
                s = ATT[n]
                keys, near, tile, r = len(s["values"]), s["near"], s["tile"], s["rows"]
                pe.wait_ge(att_copied, n + 1)
                if keys > near:
                    pe.wait_ge(att_copied2, s["seconds_done"])
                if tile >= 2:
                    pe.wait_ge(y_split, ATT_Y[lo][1] + tile - 1)
                dv = s["values"][0].shape[1]
                for i in range(keys):
                    mm = nc.tensor.matmul(bank[r:r + dv, 6 + tile % 2, s["queries"]], s["values"][i],
                                          s["at"]["pt"][:, n % 2, i * P:(i + 1) * P], start=(i == 0), stop=(i == keys - 1))
                mm.then_inc(att_summed, 1)

            scores(lo)
            scores(lo + 1)
            for n in range(lo, hi + 1):
                if n + 2 < hi:
                    scores(n + 2)
                if n < hi:
                    turn(n)
                if n > lo:
                    weigh(n - 1)
                if between and n < hi:
                    between(n)

        def att_scalar(act, lo, hi, between=None):
            branch, before = ATT_Y[lo]

            def exps(n):
                s = ATT[n]
                act.wait_ge(att_biased, n + 1)
                if n >= 2:
                    act.wait_ge(att_scaled, n - 1)
                j = n % 2
                neg = att_neg[:, j:j + 1]
                near = s["p"][:, 0:s["width"]]
                e = nc.scalar.activation(near, near, ACT.Exp, bias=neg, accum_out=att_sums[:, 2 * j:2 * j + 1])
                if s["q2"] is not None:
                    e = nc.scalar.activation(s["p"][:, T:T + CTX], bank[:, 2 + j, 0:CTX], ACT.Exp,
                                             bias=neg, accum_out=att_sums[:, 2 * j + 1:2 * j + 2])
                e.then_inc(att_exp, 1)

            def copied(n):
                s = ATT[n]
                keys, near = len(s["values"]), s["near"]
                if keys > near:
                    act.wait_ge(att_turned, n + 1)
                    if n >= 2:
                        act.wait_ge(att_summed, n - 1)
                    nc.scalar.activation(s["at"]["pt"][:, n % 2, near * P:keys * P], bank[:, 5, 0:(keys - near) * P],
                                         ACT.Copy).then_inc(att_copied2, 1)

            def rounded(n):
                c = last_of_tile(n, lo, hi)
                if c is not None:
                    act.wait_ge(att_summed, n + 1)
                    if lo == ATT2 and c == 3:
                        act.wait_ge(s5_powers, 1)
                    nc.scalar.activation(y_high[:, 4 * branch + c], bank[:, 6 + c % 2], ACT.Copy).then_inc(y_rounded, 1)

            exps(lo)
            for n in range(lo, hi):
                if n + 1 < hi:
                    exps(n + 1)
                if between:
                    between(n)
                if n > lo:
                    copied(n - 1)
                rounded(n - 2)
            copied(hi - 1)
            rounded(hi - 2)
            rounded(hi - 1)

        def att_vector(dve, link, lo, hi, between=None):
            branch, before = ATT_Y[lo]

            def biased(n):
                s = ATT[n]
                j = n % 2
                dve.wait_ge(att_scored, n + 1)
                if n >= s["buffers"]:
                    dve.wait_ge(att_turned, n - s["buffers"] + 1)
                if n < ATT1 and s["first"]:
                    dve.wait_ge(bias_loaded[s["head"] % 2], 16 * (s["head"] // 2 + 1))
                w = s["width"]
                start = NEG
                if s["q2"] is not None:
                    link(nc.vector.reduce_max(att_max[:, j:j + 1], bank[:, 2 + j, 0:CTX], AX.X))
                    start = att_max[:, j:j + 1]
                link(nc.vector.tensor_tensor_reduce(s["p"][:, 0:w], bank[:, j, 0:w], s["table"], s["scale"], start,
                                                    ALU.add, ALU.max, att_max[:, 2 + j:3 + j]))
                nc.vector.tensor_scalar(att_neg[:, j:j + 1], att_max[:, 2 + j:3 + j], -1.0, None,
                                        ALU.mult).then_inc(att_biased, 1)

            def summed(n):
                s = ATT[n]
                j = n % 2
                dve.wait_ge(att_exp, n + 1)
                total = att_sums[:, 2 * j:2 * j + 1]
                if s["q2"] is not None:
                    link(nc.vector.tensor_tensor(att_total[:, j:j + 1], total, att_sums[:, 2 * j + 1:2 * j + 2], ALU.add))
                    total = att_total[:, j:j + 1]
                link(nc.vector.reciprocal(att_total[:, j:j + 1], total))

            def scaled(n):
                s = ATT[n]
                p = s["p"][:, 0:len(s["values"]) * P]
                nc.vector.tensor_scalar(p, p, att_total[:, n % 2:n % 2 + 1], None, ALU.mult).then_inc(att_scaled, 1)

            def copied(n):
                s = ATT[n]
                dve.wait_ge(att_turned, n + 1)
                if n >= 2:
                    dve.wait_ge(att_summed, n - 1)
                near = s["near"]
                nc.vector.tensor_copy(s["at"]["pt"][:, n % 2, 0:near * P], bank[:, 4, 0:near * P]).then_inc(att_copied, 1)

            def split(n):
                c = last_of_tile(n, lo, hi)
                if c is not None:
                    dve.wait_ge(y_rounded, before + c + 1)
                    nc.vector.tensor_tensor(y_low[:, 4 * branch + c], bank[:, 6 + c % 2], y_high[:, 4 * branch + c],
                                            ALU.subtract).then_inc(y_split, 1)

            biased(lo)
            for n in range(lo, hi):
                if n + 1 < hi:
                    biased(n + 1)
                summed(n)
                if n > lo:
                    copied(n - 1)
                scaled(n)
                if between:
                    between(n)
                split(n - 3)
            copied(hi - 1)
            for n in range(hi - 3, hi):
                split(n)
            dve.wait_ge(y_split, before + 4)

        def product(o, w_high, w_low, a_high, a_low, start, stop):
            nc.tensor.matmul(o, w_high, a_high, start=start, stop=False)
            nc.tensor.matmul(o, w_high, a_low, start=False, stop=False)
            return nc.tensor.matmul(o, w_low, a_high, start=False, stop=stop)

        def block_of(position, k, n=P):
            return ring_high[:, position, k * P:k * P + n], ring_low[:, position, k * P:k * P + n]

        def tile_product(o, position, first, acts, each=None):
            for k, (ah, al) in enumerate(acts):
                if each:
                    each(k)
                wh, wl = block_of(position, first + k)
                mm = product(o, wh, wl, ah, al, k == 0, k == len(acts) - 1)
            return mm

        def split_high(act, n, it=0):
            if isinstance(it, int) and n >= NS:
                return
            act.wait_ge(raw_loaded[n % RING], 16 * (n // RING + 1) + it * 16)
            if n >= RING:
                act.wait_ge(slot_used, it * 4 + (n - RING + 1))
            nc.scalar.activation(ring_high[:, n % RING], raw[:, n % RING], ACT.Copy).then_inc(high_ready, 1)

        H = [(h_high[:, k], h_low[:, k]) for k in range(8)]

        HC = [(hc_high[:, k], hc_low[:, k]) for k in range(8)]
        HM = [(hm_high[:, k], hm_low[:, k]) for k in range(8)]
        M_ = [(m_high[:, k], m_low[:, k]) for k in range(8)]
        CQ = [(cq_high[:, k], cq_low[:, k]) for k in range(3)]
        CKV = [(ckv_high[:, k], ckv_low[:, k]) for k in range(2)]
        GY = [(gy_high[:, k], gy_low[:, k]) for k in range(4)]

        filt_loaded, hid_made, arg_ready, hid_ready = (sem(s) for s in ("filt_loaded", "hid_made", "arg_ready", "hid_ready"))
        filt_made, filt_summed, k_made, k_copied, dft_loaded = (
            sem(s) for s in ("filt_made", "filt_summed", "k_made", "k_copied", "dft_loaded"))
        decay_loaded = sem("decay_loaded")
        conv_centre, conv_done = sem("conv_centre"), sem("conv_done")
        z_turned, z_copied, u_made, y_made, z_back, z_done = (
            sem(s) for s in ("z_turned", "z_copied", "u_made", "y_made", "z_back", "z_done"))
        merge_sig, merge_added, merge_rounded, merge_low = (
            sem("merge_" + s) for s in ("sig", "added", "rounded", "low"))
        up_gate, up_prod, up_rounded, up_low, up_centre, up_conv = (
            sem("up_" + s) for s in ("gate", "prod", "rounded", "low", "centre", "conv"))
        mem_loaded, mask_loaded, mla_roped, pos_loaded, rope_arg, rope_sin = (
            sem(s) for s in ("mem_loaded", "mask_loaded", "mla_roped", "pos_loaded", "rope_arg", "rope_sin"))
        s5_arg, s5_sin, s5_in, s5_rotated, s5_states, s5_out, s5_y, s5_gelu = (
            sem("s5_" + s) for s in ("arg", "sin", "in", "rotated", "states", "out", "y", "gelu"))
        s5_b = [sem("s5_b0"), sem("s5_b1")]
        s5_c = sem("s5_c")
        glu_rounded, glu_low, glu_sig, glu_prod = (sem("glu_" + s) for s in ("rounded", "low", "sig", "prod"))
        stored = sem("stored")

        IN_MEM, IN_IN2, IN_QB, IN_K = 6, 20, 28, 36

        def s5v(i, n=16):
            return s5[:, 16 * i:16 * i + n]

        DT, TH, WH, RE, PO, AN, SI, CO, MAG, ARE, AIM, DEN, FRE, FIM, PR, PI_, NPR, NPI = range(18)

        block = ctx.enter_context(nc.Block())

        @block.sync
        def _(sp):
            def load(position, index):
                sp.dma_start(raw[:, position], a["stream"][bass.ds(index, 1)].rearrange("a p n -> (a p) n")) \
                  .then_inc(raw_loaded[position], 16)

            for j in range(2):
                load(j, ADA_SLOTS + j)
            for j in range(ADA_FIRST):
                sp.dma_start(ada_first[j], a["stream"][j]).then_inc(ada_first_loaded[j // 4], 16)
            for j in range(2, RING):
                load(j, ADA_SLOTS + j)
            with sp.Fori(1, NS // RING) as i:
                for j in range(RING):
                    sp.wait_ge(low_ready, i * RING + (j - RING + 1))
                    load(j, i * RING + (ADA_SLOTS + j))
            for n in range(NS // RING * RING, NS):
                sp.wait_ge(low_ready, n - RING + 1)
                load(n % RING, ADA_SLOTS + n)

        @block.gpsimd
        def _(pool):
            def split_low(position, n):
                pool.wait_ge(high_ready, n)
                nc.gpsimd.tensor_tensor(ring_low[:, position], raw[:, position], ring_high[:, position],
                                        ALU.subtract).then_inc(low_ready, 1)

            def split_rounds(lo, hi):
                with pool.Fori(lo, hi) as i:
                    for j in range(RING):
                        split_low(j, i * RING + (j + 1))

            s5_slot = FIRST["glu"] + 2
            assert s5_slot % RING == 0 and FIRST["kv_b"] == s5_slot - RING
            split_rounds(0, s5_slot // RING - 1)

            link = Chain(pool, pool_step)
            tt = nc.gpsimd.tensor_tensor
            value, whole = rope_w[64:96, 0], rope_w[64:96, 1]

            def turn(head, shuffled, roped):
                pool.wait_ge(partner_shuffled, shuffled)
                link(tt(value, value, rope2[64:96, 1], ALU.mult))
                link(tt(whole, head, rope2[64:96, 0], ALU.mult))
                tt(head, value, whole, ALU.add).then_inc(mla_roped, 1)
                pool.wait_ge(mla_roped, roped)

            for n in (s5_slot - 4, s5_slot - 3):
                split_low(n % RING, n + 1)
            pool.wait_ge(low_ready, s5_slot - 2)
            for h in range(HEADS):
                turn(qh[64:96, h], h + 1, h + 1)
            for n in (s5_slot - 2, s5_slot - 1):
                split_low(n % RING, n + 1)

            def double(k):
                pr, pi, npr, npi = s5v(PR), s5v(PI_), s5v(NPR), s5v(NPI)
                low_bits = LOW.bit_length() - 1
                if k < low_bits:
                    re, im = (powers[:, r].rearrange("p (a n) -> p a n", a=ST) for r in range(2))
                    m = 2 ** k
                else:
                    re, im = (powers_high[:, 0, r * 256:r * 256 + 256].rearrange("p (a n) -> p a n", a=ST) for r in range(2))
                    m = 2 ** (k - low_bits)
                if k == 0:
                    link(nc.gpsimd.tensor_copy(pr, s5v(CO)))
                    link(nc.gpsimd.tensor_copy(pi, s5v(SI)))
                if m == 1:
                    link(nc.gpsimd.memset(re[:, :, 0:1], 1.0))
                    link(nc.gpsimd.memset(im[:, :, 0:1], 0.0))
                new_re, new_im = re[:, :, m:2 * m], im[:, :, m:2 * m]
                tmp = powers_tmp[:, 0, 0:ST * m].rearrange("p (a n) -> p a n", a=ST)
                br, bi = (v.rearrange("p (a n) -> p a n", n=1).to_broadcast([P, ST, m]) for v in (pr, pi))
                link(tt(new_re, re[:, :, 0:m], br, ALU.mult))
                link(tt(tmp, im[:, :, 0:m], bi, ALU.mult))
                link(tt(new_re, new_re, tmp, ALU.subtract))
                link(tt(new_im, re[:, :, 0:m], bi, ALU.mult))
                link(tt(tmp, im[:, :, 0:m], br, ALU.mult))
                if 2 ** (k + 1) == T:
                    tt(new_im, new_im, tmp, ALU.add).then_inc(s5_powers, 1)
                    pool.wait_ge(s5_powers, 1)
                    return
                link(tt(new_im, new_im, tmp, ALU.add))
                link(tt(npr, pr, pr, ALU.mult))
                link(tt(npi, pi, pi, ALU.mult))
                link(tt(npr, npr, npi, ALU.subtract))
                link(tt(npi, pr, pi, ALU.mult))
                link(nc.gpsimd.tensor_scalar(pi, npi, 2.0, None, ALU.mult))
                link(nc.gpsimd.tensor_copy(pr, npr))

            pool.wait_ge(s5_sin, 2)
            pool.wait_ge(kr_copied, HEADS)
            for k in range(T.bit_length() - 1):
                double(k)
                if k >= 1 and k + 1 < HEADS:
                    turn(k_head[k + 1][64:96], HEADS + k, HEADS + k + 2)
            pool.wait_ge(att_scored, ATT2 + 24)
            for s in range(ST):
                if s >= 2:
                    pool.wait_ge(s5_states, s - 1)
                shape = [P, T // LOW, LOW]
                low_re, low_im = (powers[:, r, s * LOW:(s + 1) * LOW].rearrange("p (a n) -> p a n", a=1).to_broadcast(shape)
                                  for r in range(2))
                high_re, high_im = (powers_high[:, 0, r * 256 + s * 16:r * 256 + s * 16 + 16]
                                    .rearrange("p (a n) -> p a n", n=1).to_broadcast(shape) for r in range(2))
                e_re, e_im, t0, t1 = (v.rearrange("p (a n) -> p a n", n=LOW) for v in (
                    tab[:, 2 * (s % 2)], tab[:, 2 * (s % 2) + 1], tab_tmp[:, 0], tab_tmp[:, 1]))
                link.mark(tt(e_re, low_re, high_re, ALU.mult))
                first = link.mark(tt(t0, low_im, high_im, ALU.mult))
                link.mark(tt(e_im, low_re, high_im, ALU.mult))
                second = link.mark(tt(t1, low_im, high_re, ALU.mult))
                link.wait(first)
                link.mark(tt(e_re, e_re, t0, ALU.subtract))
                link.wait(second)
                tt(e_im, e_im, t1, ALU.add).then_inc(s5_table, 1)
                pool.wait_ge(s5_table, s + 1)

            split_rounds(s5_slot // RING, NS // RING)
            for n in range(NS // RING * RING, NS):
                split_low(n % RING, n + 1)

        @block.scalar
        def _(act):
            copy = nc.scalar.activation
            link = Chain(act, act_step)
            act.dma_start(silu_rows[:, 0], a["c"].partition_broadcast(P)).then_inc(silu_loaded, 16)
            act.dma_start(silu_rows_c[:, 0], a["c_ctx"].partition_broadcast(P)).then_inc(silu_loaded, 16)
            act.dma_start(vec[:, :], a["vectors"]).then_inc(first_loaded, 16)
            act.dma_start(ones[:, :], a["ones"]).then_inc(first_loaded, 16)
            act.dma_start(ident[:, :], a["identity"]).then_inc(first_loaded, 16)
            act.dma_start(one_column[:, :], a["one_column"]).then_inc(first_loaded, 16)
            act.dma_start(x[:, :, :], a["x"]).then_inc(x_loaded, 16)
            act.dma_start(ctx_in[:, :, :], a["ctx"]).then_inc(ctx_loaded, 16)

            act.wait_ge(silu_loaded, 32)
            copy(silu_rows[:, 0], silu_rows[:, 0], ACT.Silu).then_inc(silu_ready, 1)
            copy(silu_rows_c[:, 0], silu_rows_c[:, 0], ACT.Silu).then_inc(silu_ready, 1)
            act.wait_ge(x_loaded, 16)

            def first_slots():
                for n in range(2):
                    split_high(act, n)

            norm_scalar(act, "n_x1", before_rounding=first_slots)
            for n in range(2, RING):
                split_high(act, n)
            act.wait_ge(ctx_loaded, 16)
            norm_scalar(act, "n_ctx")

            act.wait_ge(norm_done, NORM["n_ctx"]["done"])
            act.dma_start(trig1[:, :, :], a["trig1"]).then_inc(trig_loaded, 16)
            for h in range(2):
                act.dma_start(bias1[:, h], a["bias"][h]).then_inc(bias_loaded[h], 16)
            for j in range(4):
                n = FIRST["q"] + j
                if n + 2 >= RING:
                    split_high(act, n + 2)
                act.wait_ge(slot_used, n + 1)
                copy(q_scaled[:, j], bank[:, j], ACT.Copy, scale=HD ** -0.5).then_inc(qkv_copied, 1)
            for j in range(2):
                split_high(act, FIRST["k"] + 2 + j)
            for j in range(4):
                n = FIRST["k"] + j
                if j >= 2:
                    split_high(act, n + 2)
                act.wait_ge(slot_used, n + 1)
                copy(k_plain[:, j], bank[:, j], ACT.Copy).then_inc(qkv_copied, 1)
                copy(kc[:, j], bank[:, 4 + j, 0:CTX], ACT.Copy).then_inc(qkv_copied, 1)
            for j in range(4):
                split_high(act, FIRST["v"] + j + 2)
            act.wait_ge(slot_used, FIRST["v"] + 4)
            for t in range(TT):
                copy(v_tok[:, t], bank[:, t], ACT.Copy).then_inc(qkv_copied, 1)
            for t in range(CT):
                copy(vc[:, t], bank[:, 4 + t], ACT.Copy).then_inc(qkv_copied, 1)

            act.wait_ge(rope_done, 8)
            for i in range(LATE_RING - 1):
                act.dma_start(ada_late[i], a["stream"][ADA_FIRST + i]).then_inc(ada_late_loaded[i], 16)

            def load_late(i):
                if i < ADA_SLOTS - ADA_FIRST:
                    if i >= LATE_RING:
                        act.wait_ge(ada_late_used, i - LATE_RING + 1)
                    act.dma_start(ada_late[i % LATE_RING], a["stream"][ADA_FIRST + i]) \
                       .then_inc(ada_late_loaded[i % LATE_RING], 16)

            def next_loads(n):
                load_late(n + LATE_RING - 1)
                h = n // TT + 1
                if n % TT == 1 and 2 <= h < HEADS:
                    act.wait_ge(att_biased, TT * (h - 1))
                    act.dma_start(bias1[:, h % 2], a["bias"][h]).then_inc(bias_loaded[h % 2], 16)

            att_scalar(act, 0, ATT1, next_loads)

            act.wait_ge(y_split, 4)
            for dst, src in ((zt[0:EMB, 0], "hy_z"), (w12f[0:FW, 0, 0:2 * FW], "hy_w12"), (w3f[0:FW, :, :], "hy_w3")):
                act.dma_start(dst, a[src]).then_inc(filt_loaded, 16)
            act.dma_start(decay[:, :, :], a["decay"]).then_inc(decay_loaded, 16)
            act.dma_start(dft[:, :, :], a["dft1"]).then_inc(dft_loaded, 16)
            for i in range(2):
                act.wait_ge(arg_ready, i + 1)
                copy(hid[0:FW, i], arg[0:FW, 0], ACT.Sin).then_inc(hid_ready, 1)
            for n in range(2):
                for f in range(4):
                    act.wait_ge(k_made, 4 * n + f + 1)
                    b = 4 + 2 * (f % 2)
                    link(copy(spec[n][:, f], bank[:, b], ACT.Copy, scale=1.0 / T))
                    copy(spec[n][:, 4 + f], bank[:, b + 1], ACT.Copy, scale=1.0 / T).then_inc(k_copied, 1)
            act.dma_start(dft[:, :, :], a["dft2"]).then_inc(dft_loaded, 16)

            with act.Fori(0, 3) as part:
                for j in range(4):
                    n = FIRST["hyena_in"] + j
                    split_high(act, n + 2, part)
                    act.wait_ge(slot_used, part * 4 + (n + 1))
                    wc, bc = VECTOR_AT["hy_conv_w"][0] + 12 + j, VECTOR_AT["hy_conv_b"][0] + j
                    copy(hyu[:, bass.ds(part * 4 + j, 1)].rearrange("p a n -> p (a n)"), bank[:, j], ACT.Identity,
                         scale=vec[:, bass.ds(part * 4 + wc, 1)], bias=vec[:, bass.ds(part * 4 + bc, 1)]).then_inc(conv_centre, 1)
            for n in range(2):
                for t in range(TT):
                    act.wait_ge(z_turned, 4 * n + t + 1)
                    copy(z_tok[:, t], bank[:, t], ACT.Copy).then_inc(z_copied, 1)
            act.wait_ge(y_made, 8)
            act.dma_start(x[:, :, :], a["x"]).then_inc(x_loaded, 16)
            for c in range(4):
                act.wait_ge(z_done, 4 + c + 1)
                copy(y_high[:, 4 + c], hyz[:, c], ACT.Copy).then_inc(y_rounded, 1)

            def merge_scalar(stage, branches, tiles, bias):
                with act.Fori(0, branches) as b:
                    for p in range(4):
                        q = 4 * (p % 2)
                        for i in range(2):
                            n = FIRST[stage] + 3 * p + i
                            g = 2 * p + i
                            split_high(act, n + 2, b * 3)
                            act.wait_ge(slot_used, b * 12 + (n + 1))
                            act.wait_ge(merge_added, b * 8 + (tiles + g + 3))
                            shift = vec[:, bass.ds(b * 8 + (bias + g), 1)] if bias is not None else v_("zero")
                            copy(sig[:, i], bank[:, q + i], ACT.Sigmoid, bias=shift).then_inc(merge_sig, 1)
                        split_high(act, FIRST[stage] + 3 * p + 4, b * 3)
                        for i in range(2):
                            g = 2 * p + i
                            act.wait_ge(merge_added, b * 8 + (tiles + g + 5))
                            copy(m_high[:, g], merged[:, g], ACT.Copy).then_inc(merge_rounded, 1)

            def splits(stage):
                with act.Fori(0, 2) as i:
                    for j in range(4):
                        split_high(act, FIRST[stage] + j + 2, i)

            def down_splits(stage):
                for half in range(2):
                    n = FIRST[stage] + 11 * half
                    split_high(act, n + 2)
                    with act.Fori(0, 2) as i:
                        for j in range(4):
                            split_high(act, n + 1 + j + 2, i)
                    split_high(act, n + 11)
                    split_high(act, n + 12)

            merge_scalar("merge1", 2, 0, None)
            splits("out1")
            norm_scalar(act, "n_x2")

            with act.Fori(0, 11) as i:
                for q in range(2):
                    n = FIRST["up1"] + 2 * q
                    split_high(act, n + 2, i)
                    act.wait_ge(slot_used, i * 4 + (n + 1))
                    act.wait_ge(up_prod, i * 2 + (q + 1))
                    copy(ff_s[:, q], bank[:, 2 * q], ACT.Silu).then_inc(up_gate, 1)
                    split_high(act, n + 3, i)
                    act.wait_ge(up_prod, i * 2 + (q + 3))
                    copy(hid_high[:, bass.ds(i * 2 + q, 1)].rearrange("p a n -> p (a n)"), ff_p[:, q], ACT.Copy) \
                        .then_inc(up_rounded, 1)
            down_splits("down1")

            act.wait_ge(slot_used, FIRST["down1"] + 22)
            act.dma_start(mem_in[:, :, :], a["mem"]).then_inc(mem_loaded, 16)
            act.dma_start(cmask[:, 0], a["cmask"]).then_inc(mask_loaded, 16)
            act.dma_start(pos_i[64:96, 0], a["positions"].partition_broadcast(DROPE)).then_inc(pos_loaded, 16)
            act.wait_ge(mem_loaded, 16)
            norm_scalar(act, "n_final", "n_mem")
            split_high(act, FIRST["mem_k"] + 2)
            split_high(act, FIRST["mem_k"] + 3)

            def mem_v_slots():
                for j in range(4):
                    split_high(act, FIRST["mem_v"] + j)

            norm_scalar(act, "n_mix", before_rounding=mem_v_slots)
            for j in range(4):
                n = FIRST["mem_k"] + j
                act.wait_ge(slot_used, n + 1)
                copy(kx[:, j], bank[:, j, 0:CTX], ACT.Copy).then_inc(in_copied, 1)
            for j in range(2):
                split_high(act, FIRST["in2"] + j)
            act.wait_ge(slot_used, FIRST["mem_v"] + 4)
            for t in range(CT):
                copy(vx[:, t], bank[:, 4 + t], ACT.Copy).then_inc(in_copied, 1)
            dests = [cq[:, i] for i in range(3)] + [ckv[:, i] for i in range(2)] + [kr[64:96, 0]] \
                + [xq[:, i] for i in range(4)] + [u_ssm[:, i] for i in range(4)]
            act.wait_ge(norm_done, NORM["n_mem"]["done"])
            for j, dst in enumerate(dests):
                n = FIRST["in2"] + j
                if j != 7:
                    split_high(act, n + 2)
                act.wait_ge(slot_used, n + 1)
                src = bank[64:96, j % 4] if j == 5 else bank[:, j % 4]
                copy(dst, src, ACT.Copy).then_inc(in_copied, 1)
                if j == 6:
                    split_high(act, n + 3)
                    norm_scalar(act, "n_cq", "n_ckv")
                if j in (8, 9):
                    act.wait_ge(s5_arg, j - 7)
                    copy(s5[:, 16 * (j - 2):16 * (j - 1)], s5[:, 16 * 5:16 * 6], ACT.Sin).then_inc(s5_sin, 1)
                if j in (10, 11):
                    act.wait_ge(rope_arg, j - 9)
                    copy(rope2[64:96, 11 - j], rope_a[64:96, 0], ACT.Sin).then_inc(rope_sin, 1)
            for j in range(4):
                n = FIRST["q_b"] + j
                split_high(act, n + 2)
                act.wait_ge(slot_used, n + 1)
                for i in range(2):
                    copy(qh[0:DQK, 2 * j + i], bank[0:DQK, (2 * j + i) % 4], ACT.Copy).then_inc(in_copied, 1)
            heads_scalar(act, BATCHES[0])
            att_scalar(act, ATT1, ATT2)

            n = FIRST["kv_b"]
            split_high(act, n + 2)
            act.wait_ge(slot_used, n + 1)
            for h in range(HEADS):
                copy(k_head[h][0:DNOPE], bank[64 * (h % 2):64 * (h % 2) + 64, 4 + h // 2], ACT.Copy).then_inc(in_copied, 1)
            split_high(act, n + 3)
            act.wait_ge(slot_used, n + 2)
            act.wait_ge(kr_copied, HEADS)
            heads_scalar(act, BATCHES[1])
            for t in range(TT):
                copy(v_mla[:, t], bank[:, t], ACT.Copy).then_inc(in_copied, 1)

            def load_s5(n):
                if n == ATT2 + 20:
                    act.wait_ge(att_scored, ATT2 + 16)
                    act.dma_start(bmat[0][:, :, :], a["ssm_b"][0]).then_inc(s5_b[0], 16)
                if n == ATT3 - 1:
                    act.wait_ge(att_scored, ATT3)
                    act.dma_start(cmat[:, :, :], a["ssm_c"]).then_inc(s5_c, 16)

            att_scalar(act, ATT2, ATT3, load_s5)

            act.wait_ge(y_split, 16)
            act.dma_start(bmat[1][:, :, :], a["ssm_b"][1]).then_inc(s5_b[1], 16)
            for i in range(4):
                act.wait_ge(s5_y, i + 1)
                copy(gy[:, i], gy[:, i], ACT.Gelu_apprx_tanh).then_inc(s5_gelu, 1)
            act.wait_ge(s5_gelu, 4)
            for c in range(4):
                copy(gy_high[:, c], gy[:, c], ACT.Copy).then_inc(glu_rounded, 1)
            for c in range(4):
                n = FIRST["glu"] + c // 2
                if c % 2 == 0:
                    split_high(act, n + 2)
                    act.wait_ge(slot_used, n + 1)
                if c >= 2:
                    act.wait_ge(glu_prod, c - 1)
                copy(gsig[:, c % 2], bank[:, c], ACT.Sigmoid, bias=v_("b_glu", c)).then_inc(glu_sig, 1)
                act.wait_ge(glu_prod, c + 1)
                copy(y_high[:, 4 + c], gprod[:, c % 2], ACT.Copy).then_inc(y_rounded, 1)

            merge_scalar("merge2", 3, 16, VECTOR_AT["b_gate"][0])
            splits("out2")
            norm_scalar(act, "n_ffn")

            with act.Fori(0, 11) as i:
                for q in range(2):
                    n = FIRST["up2"] + 2 * q
                    for g, dst in ((0, ff_a), (1, ff_v)):
                        split_high(act, n + 2 + g, i)
                        act.wait_ge(slot_used, i * 4 + (n + 1 + g))
                        if g == 0:
                            act.wait_ge(up_prod, i * 2 + (22 + q + 1))
                        wc, bc = VECTOR_AT["conv_w"][0] + 88 + 22 * g + q, VECTOR_AT["conv_b"][0] + 22 * g + q
                        copy(dst[:, q], bank[:, 2 * q + g], ACT.Identity, scale=vec[:, bass.ds(i * 2 + wc, 1)],
                             bias=vec[:, bass.ds(i * 2 + bc, 1)]).then_inc(up_centre, 1)
                    act.wait_ge(up_conv, i * 4 + (4 + 2 * q + 1))
                    copy(ff_s[:, q], ff_a[:, q], ACT.Silu).then_inc(up_gate, 1)
                    act.wait_ge(up_prod, i * 2 + (22 + q + 3))
                    copy(hid_high[:, bass.ds(i * 2 + q, 1)].rearrange("p a n -> p (a n)"), ff_p[:, q], ACT.Copy) \
                        .then_inc(up_rounded, 1)
            down_splits("down2")
            for k in range(8):
                act.wait_ge(out_added, 4 + 24 + k + 1)
                act.dma_start(out[k], x[:, k]).then_inc(stored, 16)
            act.wait_ge(stored, 16 * 8)

        @block.tensor
        def _(pe):
            mm = nc.tensor.matmul
            pe.wait_ge(first_loaded, 64)
            norm_tensor(pe, NORM["n_x1"])

            def ready(n):
                pe.wait_ge(low_ready, n + 1)

            def normalised(name):
                n = NORM[name]
                return lambda k: pe.wait_ge(norm_done, n["done"] - len(n["tiles"]) + k + 1)

            for j in range(4):
                n = FIRST["q"] + j
                ready(n)
                tile_product(bank[:, j], n % RING, 0, H, None if j else normalised("n_x1")).then_inc(slot_used, 1)
                if j == 1:
                    norm_tensor(pe, NORM["n_ctx"])
            for j in range(4):
                ready(FIRST["k"] + j)
                pe.wait_ge(qkv_copied, j + 1)
                tile_product(bank[:, j], (FIRST["k"] + j) % RING, 0, H)
            pe.wait_ge(norm_done, NORM["n_ctx"]["done"])
            for j in range(4):
                tile_product(bank[:, 4 + j, 0:CTX], (FIRST["k"] + j) % RING, 0, HC).then_inc(slot_used, 1)
            pe.wait_ge(qkv_copied, 12)

            def token_major(stage, groups):
                for i in range(4):
                    n = FIRST[stage] + i
                    ready(n)
                    for kk in range(2):
                        k = 2 * i + kk
                        wh, wl = (r[:, n % RING, kk * 512:kk * 512 + 512] for r in (ring_high, ring_low))
                        for b, (ah, al), t in groups:
                            s = slice(t * P, (t + 1) * P)
                            last = product(bank[:, b], ah[:, k, s], al[:, k, s], wh, wl, k == 0, k == 7)
                    last.then_inc(slot_used, 1)

            token_major("v", [(t, (h_high, h_low), t) for t in range(TT)] + [(4 + t, (hc_high, hc_low), t) for t in range(CT)])
            pe.wait_ge(qkv_copied, 18)
            pe.wait_ge(rope_done, 8)
            att_tensor(pe, 0, ATT1)

            pe.wait_ge(filt_loaded, 16 * 3)
            pe.wait_ge(y_split, 4)
            mm(bank[0:FW, 0], w12f[0:EMB, 0, 0:FW], zt[0:EMB, 0], start=True, stop=True).then_inc(hid_made, 1)
            pe.wait_ge(hid_ready, 1)
            mm(bank[0:FW, 0], w12f[0:FW, 0, FW:2 * FW], hid[0:FW, 0], start=True, stop=True).then_inc(hid_made, 1)
            pe.wait_ge(hid_ready, 2)
            for n in range(2):
                for t in range(TT):
                    if 4 * n + t >= 2:
                        pe.wait_ge(filt_summed, 4 * n + t - 1)
                    for d in range(2):
                        last = mm(bank[:, 2 * (t % 2) + d], hid[0:FW, 1, t * P:(t + 1) * P], w3f[0:FW, 2 * d + n],
                                  start=True, stop=True)
                    last.then_inc(filt_made, 1)
                pe.wait_ge(dft_loaded, 16)
                for f in range(4):
                    if 4 * n + f >= 2:
                        pe.wait_ge(k_copied, 4 * n + f - 1)
                    for t in range(TT):
                        if f == 0:
                            pe.wait_ge(filt_summed, 4 * n + t + 1)
                        for d in range(2):
                            last = mm(bank[:, 4 + 2 * (f % 2) + d], dft[:, 4 * d + t, f * P:(f + 1) * P], filt[:, 4 * d + t],
                                      start=(t == 0), stop=(t == 3))
                    last.then_inc(k_made, 1)

            with pe.Fori(0, 3) as part:
                for j in range(4):
                    n = FIRST["hyena_in"] + j
                    pe.wait_ge(low_ready, part * 4 + (n + 1))
                    pe.wait_ge(conv_done, part * 4 + (j + 1))
                    tile_product(bank[:, j], n % RING, 0, H).then_inc(slot_used, 1)
            pe.wait_ge(conv_done, 4 + 12)
            pe.wait_ge(k_copied, 8)
            for n in range(2):
                for t in range(TT):
                    for c in range(4):
                        last = nc.tensor.transpose(bank[:, t, c * P:(c + 1) * P], hyu[:, c, t * P:(t + 1) * P], ident[:, :])
                    last.then_inc(z_turned, 1)
                pe.wait_ge(z_copied, 4 * n + 4)
                pe.wait_ge(dft_loaded, 32)
                for f in range(4):
                    if 4 * n + f >= 2:
                        pe.wait_ge(y_made, 4 * n + f - 1)
                    for d in range(2):
                        for t in range(TT):
                            last = mm(bank[:, 4 + 2 * (f % 2) + d], dft[:, 4 * d + t, f * P:(f + 1) * P], z_tok[:, t],
                                      start=(t == 0), stop=(t == 3))
                    last.then_inc(u_made, 1)
                for f in range(4):
                    pe.wait_ge(y_made, 4 * n + f + 1)
                    for c in range(4):
                        mm(bank[:, c], y_re[:, f, c * P:(c + 1) * P], dft[:, f], start=(f == 0), stop=False)
                        last = mm(bank[:, c], y_im[:, f, c * P:(c + 1) * P], dft[:, 4 + f], start=False, stop=(f == 3))
                        if f == 3:
                            last.then_inc(z_back, 1)
                pe.wait_ge(z_done, 4 * n + 4)

            def merge_tensor(stage, branches, tiles):
                with pe.Fori(0, branches) as b:
                    for p in range(4):
                        q = 4 * (p % 2)
                        for i in range(2):
                            n = FIRST[stage] + 3 * p + i
                            pe.wait_ge(low_ready, b * 12 + (n + 1))
                            pe.wait_ge(merge_added, b * 8 + (tiles + 2 * p + i + 1))
                            tile_product(bank[:, q + i], n % RING, 0, H).then_inc(slot_used, 1)
                        n = FIRST[stage] + 3 * p + 2
                        pe.wait_ge(low_ready, b * 12 + (n + 1))
                        ys = [(y_high[:, bass.ds(b * 4 + k, 1)].rearrange("p a n -> p (a n)"),
                               y_low[:, bass.ds(b * 4 + k, 1)].rearrange("p a n -> p (a n)")) for k in range(4)]
                        for i in range(2):
                            last = tile_product(bank[:, q + 2 + i], n % RING, 4 * i, ys)
                        last.then_inc(slot_used, 1)

            def out_tensor(stage, tiles, merges):
                def merged_tile(k):
                    pe.wait_ge(merge_low, merges - 8 + max(k + 1, 6))

                for j in range(8):
                    n = FIRST[stage] + j
                    pe.wait_ge(low_ready, n + 1)
                    pe.wait_ge(out_added, tiles + j + 1)
                    tile_product(bank[:, j % 4], n % RING, 0, M_, None if j else merged_tile).then_inc(slot_used, 1)

            def up_tensor(stage, name, freed, before, each):
                def four_slots(i, first):
                    for q in range(2):
                        for g in range(2):
                            n = FIRST[stage] + 2 * q + g
                            pe.wait_ge(low_ready, i * 4 + (n + 1))
                            if g == 0:
                                pe.wait_ge(freed, i * (2 * each) + (before + each * (q + 1)))
                            tile_product(bank[:, 2 * q + g], n % RING, 0, H, first if q == g == 0 else None) \
                                .then_inc(slot_used, 1)

                four_slots(0, normalised(name))
                with pe.Fori(1, 11) as i:
                    four_slots(i, None)

            def down_tensor(stage, before):
                pe.wait_ge(up_low, before + 18)
                for half in range(2):
                    def one(n, hidden, wait, start, stop):
                        pe.wait_ge(low_ready, wait)
                        for kk in range(2):
                            ah, al = hidden(kk)
                            for m in range(4):
                                wh, wl = block_of(n % RING, 4 * kk + m)
                                last = product(bank[:, 4 - 4 * half + m], wh, wl, ah, al, start and kk == 0, stop and kk == 1)
                        last.then_inc(slot_used, 1)

                    base = FIRST[stage] + 11 * half
                    one(base, lambda kk: (hid_high[:, kk], hid_low[:, kk]), base + 1, True, False)
                    with pe.Fori(0, 2) as i:
                        for j in range(4):
                            def tiles(kk, j=j):
                                k = bass.ds(i * 8 + (2 * (1 + j) + kk), 1)
                                return tuple(t[:, k].rearrange("p a n -> p (a n)") for t in (hid_high, hid_low))
                            one(base + 1 + j, tiles, i * 4 + (base + 1 + j + 1), False, False)
                    pe.wait_ge(up_low, before + 22)
                    for m in (9, 10):
                        one(base + m, lambda kk, m=m: (hid_high[:, 2 * m + kk], hid_low[:, 2 * m + kk]), base + m + 1,
                            False, m == 10)

            pe.wait_ge(y_split, 8)
            merge_tensor("merge1", 2, 0)
            out_tensor("out1", 0, 16)
            norm_tensor(pe, NORM["n_x2"])
            up_tensor("up1", "n_x2", up_prod, 0, 1)
            down_tensor("down1", 0)
            pe.wait_ge(out_added, 4 + 16)
            norm_tensor(pe, NORM["n_final"])
            norm_tensor(pe, NORM["n_mem"])
            for j in range(4):
                n = FIRST["mem_k"] + j
                ready(n)
                tile_product(bank[:, j, 0:CTX], n % RING, 0, HM, None if j else normalised("n_mem")).then_inc(slot_used, 1)
            norm_tensor(pe, NORM["n_mix"])
            token_major("mem_v", [(4 + t, (hm_high, hm_low), t) for t in range(CT)])
            for j in range(14):
                n = FIRST["in2"] + j
                ready(n)
                pe.wait_ge(in_copied, j + 1 if j < 4 else IN_MEM + j - 3)
                tile_product(bank[:, j % 4], n % RING, 0, H, None if j else normalised("n_mix")).then_inc(slot_used, 1)
                if j == 7:
                    norm_tensor(pe, NORM["n_cq"])
                    norm_tensor(pe, NORM["n_ckv"])
            pe.wait_ge(norm_done, NORM["n_ckv"]["done"])
            for j in range(4):
                n = FIRST["q_b"] + j
                ready(n)
                for i in range(2):
                    h = 2 * j + i
                    pe.wait_ge(in_copied, IN_IN2 + max(h - 3, 0))
                    for k, (ah, al) in enumerate(CQ):
                        wh, wl = block_of(n % RING, 3 * i + k, DQK)
                        last = product(bank[0:DQK, h % 4], wh, wl, ah, al, k == 0, k == 2)
                last.then_inc(slot_used, 1)
            pe.wait_ge(in_copied, IN_QB)
            heads_tensor(pe, BATCHES[0])
            for k in range(4):
                spread(pe, BATCHES[0], k)
            att_tensor(pe, ATT1, ATT2, lambda n: n - ATT1 < 12 and spread(pe, BATCHES[0], n - ATT1 + 4))
            pe.wait_ge(y_split, 12)

            n = FIRST["kv_b"]
            ready(n)
            for m in range(4):
                last = tile_product(bank[:, 4 + m], n % RING, 2 * m, CKV)
            last.then_inc(slot_used, 1)
            ready(n + 1)
            for t in range(TT):
                for k in range(2):
                    s = slice(t * P, (t + 1) * P)
                    wh, wl = (r[:, (n + 1) % RING, k * 512:k * 512 + 512] for r in (ring_high, ring_low))
                    last = product(bank[:, t], ckv_high[:, k, s], ckv_low[:, k, s], wh, wl, k == 0, k == 1)
            last.then_inc(slot_used, 1)
            heads_tensor(pe, BATCHES[1])
            for k in range(2):
                if k == 0:
                    pe.wait_ge(in_copied, IN_K + 4)
                spread(pe, BATCHES[1], k)
            att_tensor(pe, ATT2, ATT3, lambda n: ahead(n) and spread(pe, BATCHES[1], ahead(n)))

            pe.wait_ge(y_split, 16)

            def s5_output(s):
                pe.wait_ge(s5_states, s + 1)
                i = s // 4
                if s % 4 == 0 and i >= 2:
                    pe.wait_ge(s5_y, i - 1)
                q = s % 4 * 32
                mats = [m[:, s * 32:(s + 1) * 32] for m in (cmat[:, 0], cmat_minus[:, 0], cmat[:, 1], cmat[:, 1])]
                for r in range(4):
                    last = mm(bank[q:q + 32, 4 + i % 2], mats[r], s5s[:, r], start=(r == 0), stop=(r == 3))
                last.then_inc(s5_out, 1)

            for s in range(ST):
                if s % 8 == 0:
                    pe.wait_ge(s5_b[s // 8], 16)
                if s >= 2:
                    pe.wait_ge(s5_rotated, s - 1)
                for r in range(2):
                    last = mm(bank[:, 2 * (s % 2) + r], bmat[s // 8][:, 2 * r + s % 8 // 4, (s % 4) * P:(s % 4 + 1) * P],
                              u_ssm[:, s // 4], start=True, stop=True)
                last.then_inc(s5_in, 1)
                if s >= 1:
                    s5_output(s - 1)
            s5_output(ST - 1)
            pe.wait_ge(glu_low, 4)
            pe.wait_ge(s5_rotated, ST)
            for j in range(2):
                n = FIRST["glu"] + j
                ready(n)
                for i in range(2):
                    last = tile_product(bank[:, 2 * j + i], n % RING, 4 * i, GY)
                last.then_inc(slot_used, 1)
            pe.wait_ge(y_split, 20)
            merge_tensor("merge2", 3, 16)
            out_tensor("out2", 16, 16 + 24)
            norm_tensor(pe, NORM["n_ffn"])
            up_tensor("up2", "n_ffn", up_conv, 0, 2)
            down_tensor("down2", 22)

        @block.vector
        def _(dve):
            link = Chain(dve, dve_step)
            tt, ts, stt = nc.vector.tensor_tensor, nc.vector.tensor_scalar, nc.vector.scalar_tensor_tensor
            MAGIC = 12582912.0
            TAU = (6.28125, 0.0019350051879882812, 3.019915981956753e-07)

            def reduce_angle(value, whole, last):
                link(ts(whole, value, 1.0 / (2 * math.pi), MAGIC, ALU.mult, ALU.add))
                link(ts(whole, whole, -MAGIC, None, ALU.add))
                for part in TAU:
                    link(stt(out=value, in0=whole, scalar=-part, in1=value, op0=ALU.mult, op1=ALU.add))
                return ts(last, value, 3.1415925, -3.1415925, ALU.min, ALU.max)

            dve.sem_inc(conv_done, 4)
            dve.sem_inc(merge_added, 4)
            dve.sem_inc(out_added, 4)
            dve.sem_inc(up_prod, 2)
            dve.sem_inc(up_conv, 4)

            dve.wait_ge(first_loaded, 64)

            def modulation(weights, rows, m, target, used):
                nc.vector.tensor_tensor_reduce(ada_prod[:, 0], weights, rows[:, 0], 1.0, v_("b_ada", m), ALU.mult, ALU.add,
                                               target[:, m:m + 1]).then_inc(used, 1)

            for which, (rows, target) in enumerate(((silu_rows, mod), (silu_rows_c, mod_c))):
                dve.wait_ge(silu_ready, which + 1)
                for m in range(ADA_FIRST):
                    if which == 0 and m % 4 == 0:
                        dve.wait_ge(ada_first_loaded[m // 4], 16 * 4)
                    n = which * ADA_FIRST + m
                    if n:
                        dve.wait_ge(ada_first_used, n)
                    modulation(ada_first[m], rows, m, target, ada_first_used)
                dve.wait_ge(ada_first_used, (which + 1) * ADA_FIRST)
                gain = (gain1, gain1_c)[which]
                stt(out=gain[:, :], in0=target[:, 8:16], scalar=1.0, in1=v_("norm1", 0, 8), op0=ALU.add, op1=ALU.mult) \
                    .then_inc(mod_ready, 1)
                dve.wait_ge(mod_ready, which + 1)
                norm_vector(dve, link, NORM["n_ctx" if which else "n_x1"])

            dve.wait_ge(trig_loaded, 16)
            for src, dst, count in [(q_scaled, q_rot, lambda j: j + 1), (k_plain, k_rot, lambda j: 4 + 2 * j + 1)]:
                for j in range(4):
                    dve.wait_ge(qkv_copied, count(j))
                    link(nc.vector.stream_shuffle(rope_t[:, 0], src[:, j], mask=MASK_SWAP))
                    link(tt(rope_t[:, 0], rope_t[:, 0], trig1[:, 1], ALU.mult))
                    link(tt(rope_t[:, 1], src[:, j], trig1[:, 0], ALU.mult))
                    tt(dst[:, j], rope_t[:, 0], rope_t[:, 1], ALU.add).then_inc(rope_done, 1)
                    dve.wait_ge(rope_done, j + 1 if src is q_scaled else 5 + j)
            def late_modulation(n):
                dve.wait_ge(ada_late_loaded[n % LATE_RING], 16 * (n // LATE_RING + 1))
                if n:
                    dve.wait_ge(ada_late_used, n)
                modulation(ada_late[n % LATE_RING], silu_rows, ADA_FIRST + n, mod, ada_late_used)

            att_vector(dve, link, 0, ATT1, late_modulation)
            dve.wait_ge(ada_late_used, ADA_SLOTS - ADA_FIRST)
            link(stt(out=gain2[:, :], in0=mod[:, 32:40], scalar=1.0, in1=v_("norm2", 0, 8), op0=ALU.add, op1=ALU.mult))

            for i in range(2):
                dve.wait_ge(hid_made, i + 1)
                if i:
                    dve.wait_ge(hid_ready, 1)
                link(ts(arg[0:FW, 0], bank[0:FW, 0], v_(f"hy_b{i + 1}", 0, 1, 0, FW), v_("hy_freq", 0, 1, 0, FW), ALU.add, ALU.mult))
                reduce_angle(arg[0:FW, 0], arg[0:FW, 1], arg[0:FW, 0]).then_inc(arg_ready, 1)
            dve.wait_ge(hid_ready, 2)
            dve.wait_ge(decay_loaded, 16)
            for n in range(2):
                for t in range(TT):
                    dve.wait_ge(filt_made, 4 * n + t + 1)
                    if n and t == 0:
                        dve.wait_ge(k_made, 4)
                    b = 2 * (t % 2)
                    link(tt(arg[:, 0], bank[:, b], decay[:, t], ALU.mult))
                    link(tt(arg[:, 1], bank[:, b + 1], decay[:, t], ALU.mult))
                    if t == 0:
                        link(nc.vector.memset(arg[0:1, 1], 0.0))
                    link(tt(filt[:, t], arg[:, 0], arg[:, 1], ALU.add))
                    tt(filt[:, 4 + t], arg[:, 0], arg[:, 1], ALU.subtract).then_inc(filt_summed, 1)
                    dve.wait_ge(filt_summed, 4 * n + t + 1)

            with dve.Fori(0, 3) as part:
                start = link.count
                link.count = start + part * 4
                for j in range(4):
                    dve.wait_ge(conv_centre, part * 4 + (j + 1))
                    tile = bass.ds(part * 4 + j, 1)
                    later = hyu[:, tile, 1:T].rearrange("p a n -> p (a n)")
                    sooner = hyu[:, tile, 0:T - 1].rearrange("p a n -> p (a n)")
                    w0, w2 = (VECTOR_AT["hy_conv_w"][0] + tap * 12 + j for tap in (0, 2))
                    link(stt(out=later, in0=bank[:, j, 0:T - 1], scalar=vec[:, bass.ds(part * 4 + w0, 1)], in1=later,
                             op0=ALU.mult, op1=ALU.add))
                    stt(out=sooner, in0=bank[:, j, 1:T], scalar=vec[:, bass.ds(part * 4 + w2, 1)], in1=sooner,
                        op0=ALU.mult, op1=ALU.add).then_inc(conv_done, 1)
            link.count = start + 12
            dve.wait_ge(conv_done, 4 + 12)
            dve.wait_ge(k_copied, 8)
            for n in range(2):
                for f in range(4):
                    dve.wait_ge(u_made, 4 * n + f + 1)
                    b = 4 + 2 * (f % 2)
                    kre, kim = spec[n][:, f], spec[n][:, 4 + f]
                    link(tt(y_re[:, f], bank[:, b], kre, ALU.mult))
                    link(tt(hyt[:, 0], bank[:, b + 1], kim, ALU.mult))
                    link(tt(y_re[:, f], y_re[:, f], hyt[:, 0], ALU.subtract))
                    link(tt(y_im[:, f], bank[:, b], kim, ALU.mult))
                    link(tt(hyt[:, 1], bank[:, b + 1], kre, ALU.mult))
                    tt(y_im[:, f], y_im[:, f], hyt[:, 1], ALU.add).then_inc(y_made, 1)
                    dve.wait_ge(y_made, 4 * n + f + 1)
                for c in range(4):
                    dve.wait_ge(z_back, 4 * n + c + 1)
                    link(stt(out=hyz[:, c], in0=hyu[:, c], scalar=v_("hy_bias", 4 * n + c), in1=bank[:, c],
                             op0=ALU.mult, op1=ALU.add))
                    dst = hyu[:, c] if n == 0 else hyz[:, c]
                    tt(dst, hyz[:, c], hyu[:, 4 + 4 * n + c], ALU.mult).then_inc(z_done, 1)
                    dve.wait_ge(z_done, 4 * n + c + 1)
            for c in range(4):
                dve.wait_ge(y_rounded, 4 + c + 1)
                tt(y_low[:, 4 + c], hyz[:, c], y_high[:, 4 + c], ALU.subtract).then_inc(y_split, 1)
            dve.wait_ge(y_split, 8)

            def merge_vector(stage, branches, tiles):
                link(nc.vector.memset(merged[:, :, :].rearrange("p a n -> p (a n)"), 0.0))
                start = link.count
                with dve.Fori(0, branches) as b:
                    link.count = start + b * 8
                    for p in range(4):
                        q = 4 * (p % 2)
                        dve.wait_ge(slot_used, b * 12 + (FIRST[stage] + 3 * p + 3))
                        for i in range(2):
                            g = 2 * p + i
                            dve.wait_ge(merge_sig, b * 8 + (tiles + g + 1))
                            link(tt(mprod[:, i], sig[:, i], bank[:, q + 2 + i], ALU.mult))
                            tt(merged[:, g], merged[:, g], mprod[:, i], ALU.add).then_inc(merge_added, 1)
                        for i in range(2):
                            g = 2 * p + i
                            dve.wait_ge(merge_rounded, b * 8 + (tiles + g + 1))
                            tt(m_low[:, g], merged[:, g], m_high[:, g], ALU.subtract).then_inc(merge_low, 1)
                link.count = start + branches * 8
                dve.wait_ge(merge_low, tiles + branches * 8)

            def add_to_x(k, b, gate):
                xk = x[:, k] if isinstance(k, int) else x[:, bass.ds(k, 1)].rearrange("p a n -> p (a n)")
                if gate is None:
                    return tt(xk, xk, bank[:, b], ALU.add)
                g = mod[:, gate + k:gate + k + 1] if isinstance(k, int) else mod[:, bass.ds(k + gate, 1)]
                return stt(out=xk, in0=bank[:, b], scalar=g, in1=xk, op0=ALU.mult, op1=ALU.add)

            def out_vector(stage, gate):
                with dve.Fori(0, 2) as i:
                    for j in range(4):
                        dve.wait_ge(slot_used, i * 4 + (FIRST[stage] + j + 1))
                        add_to_x(i * 4 + j, j, gate).then_inc(out_added, 1)

            def down_vector(stage, gate):
                for half in range(2):
                    dve.wait_ge(slot_used, FIRST[stage] + 11 * (half + 1))
                    for m in range(4):
                        add_to_x(4 * half + m, 4 - 4 * half + m, gate).then_inc(out_added, 1)

            merge_vector("merge1", 2, 0)
            dve.wait_ge(x_loaded, 32)
            out_vector("out1", 16)
            norm_vector(dve, link, NORM["n_x2"])
            with dve.Fori(0, 11) as i:
                for q in range(2):
                    hidden = bass.ds(i * 2 + q, 1)
                    dve.wait_ge(up_gate, i * 2 + (q + 1))
                    dve.wait_ge(slot_used, i * 4 + (FIRST["up1"] + 2 * q + 2))
                    tt(ff_p[:, q], ff_s[:, q], bank[:, 2 * q + 1], ALU.mult).then_inc(up_prod, 1)
                    dve.wait_ge(up_rounded, i * 2 + (q + 1))
                    tt(hid_low[:, hidden].rearrange("p a n -> p (a n)"), ff_p[:, q],
                       hid_high[:, hidden].rearrange("p a n -> p (a n)"), ALU.subtract).then_inc(up_low, 1)
                    dve.wait_ge(up_low, i * 2 + (q + 1))
            down_vector("down1", 40)

            norm_vector(dve, link, NORM["n_final"])
            norm_vector(dve, link, NORM["n_mem"])
            norm_vector(dve, link, NORM["n_mix"])
            norm_vector(dve, link, NORM["n_cq"])
            norm_vector(dve, link, NORM["n_ckv"])
            LOG2E, LN2_HIGH, LN2_LOW = 1.4426950408889634, 0.693359375, -2.12194440e-4

            def exact_exp(dst, src, whole, rest, poly):
                bias = MAGIC + 127.0
                link(ts(rest, src, 88.0, -87.0, ALU.min, ALU.max))
                link(ts(whole, rest, LOG2E, bias, ALU.mult, ALU.add))
                link(ts(poly, whole, -bias, None, ALU.add))
                link(stt(out=rest, in0=poly, scalar=-LN2_HIGH, in1=rest, op0=ALU.mult, op1=ALU.add))
                link(stt(out=rest, in0=poly, scalar=-LN2_LOW, in1=rest, op0=ALU.mult, op1=ALU.add))
                link(ts(whole.bitcast(I32), whole.bitcast(I32), 23, None, ALU.logical_shift_left))
                link(ts(poly, rest, 1.0 / math.factorial(7), None, ALU.mult))
                for d in range(6, 0, -1):
                    link(stt(out=poly, in0=poly, scalar=1.0 / math.factorial(d), in1=rest, op0=ALU.add, op1=ALU.mult))
                link(stt(out=dst, in0=poly, scalar=1.0, in1=whole, op0=ALU.add, op1=ALU.mult))

            exact_exp(s5v(DT), v_("log_dt", 0, 16), s5v(WH), s5v(RE), s5v(PO))
            link(tt(s5v(TH), v_("lam_im", 0, 16), s5v(DT), ALU.mult))
            reduce_angle(s5v(TH), s5v(WH), s5v(AN)).then_inc(s5_arg, 1)
            dve.wait_ge(s5_sin, 1)
            link(ts(s5v(TH), s5v(AN), math.pi / 2, None, ALU.add))
            reduce_angle(s5v(TH), s5v(WH), s5v(AN)).then_inc(s5_arg, 1)
            link(tt(s5v(ARE), v_("lam_re", 0, 16), s5v(DT), ALU.mult))
            exact_exp(s5v(MAG), s5v(ARE), s5v(WH), s5v(RE), s5v(PO))
            dve.wait_ge(s5_sin, 2)
            lr, li = v_("lam_re", 0, 16), v_("lam_im", 0, 16)
            link(tt(s5v(ARE), s5v(MAG), s5v(CO), ALU.mult))
            link(ts(s5v(ARE), s5v(ARE), -1.0, None, ALU.add))
            link(tt(s5v(AIM), s5v(MAG), s5v(SI), ALU.mult))
            link(tt(s5v(DEN), lr, lr, ALU.mult))
            link(tt(s5v(WH), li, li, ALU.mult))
            link(tt(s5v(DEN), s5v(DEN), s5v(WH), ALU.add))
            link(nc.vector.reciprocal(s5v(DEN), s5v(DEN)))
            link(tt(s5v(FRE), s5v(ARE), lr, ALU.mult))
            link(tt(s5v(WH), s5v(AIM), li, ALU.mult))
            link(tt(s5v(FRE), s5v(FRE), s5v(WH), ALU.add))
            link(tt(s5v(FRE), s5v(FRE), s5v(DEN), ALU.mult))
            link(tt(s5v(FIM), s5v(AIM), lr, ALU.mult))
            link(tt(s5v(WH), s5v(ARE), li, ALU.mult))
            link(tt(s5v(FIM), s5v(FIM), s5v(WH), ALU.subtract))
            link(tt(s5v(FIM), s5v(FIM), s5v(DEN), ALU.mult))

            dve.wait_ge(pos_loaded, 16)
            value, whole = rope_w[64:96, 0], rope_w[64:96, 1]
            angle = rope_a[64:96, 0]
            link(nc.vector.tensor_copy(value, pos_i[64:96, 0]))
            link(ts(value, value, v_("inv_freq", 0, 1, 64, 96), None, ALU.mult))
            reduce_angle(value, whole, angle).then_inc(rope_arg, 1)
            dve.wait_ge(rope_sin, 1)
            link(ts(rope2[64:96, 1], rope2[64:96, 1], v_("rope_sign", 0, 1, 64, 96), None, ALU.mult))
            link(ts(value, angle, math.pi / 2, None, ALU.add))
            reduce_angle(value, whole, angle).then_inc(rope_arg, 1)
            dve.wait_ge(rope_sin, 2)

            def rotate(count, head):
                link(nc.vector.stream_shuffle(value, head, mask=MASK_SWAP))
                link(tt(value, value, rope2[64:96, 1], ALU.mult))
                link(tt(whole, head, rope2[64:96, 0], ALU.mult))
                tt(head, value, whole, ALU.add).then_inc(mla_roped, 1)
                dve.wait_ge(mla_roped, count + 1)

            def rotate_query(n):
                step = n - ATT1
                if 1 <= step < 13:
                    apply_roots(dve, BATCHES[0], step + 3)
                if 6 <= step < 6 + HEADS:
                    h = step - 6
                    dve.wait_ge(heads_done, 2 * XH + h + 1)
                    if h:
                        dve.wait_ge(mla_roped, h)
                    nc.vector.stream_shuffle(value, qh[64:96, h], mask=MASK_SWAP).then_inc(partner_shuffled, 1)

            for k in range(4):
                apply_roots(dve, BATCHES[0], k)
            dve.wait_ge(mask_loaded, 16)
            att_vector(dve, link, ATT1, ATT2, rotate_query)
            for h in range(HEADS):
                nc.vector.tensor_copy(k_head[h][64:96], kr[64:96, 0]).then_inc(kr_copied, 1)
            dve.wait_ge(mla_roped, HEADS)
            for h in range(2):
                apply_roots(dve, BATCHES[1], h)
                dve.wait_ge(heads_done, BATCHES[1]["first"] + h + 1)
                rotate(HEADS + h, k_head[h][64:96])

            def rotate_ahead(n):
                h, t = divmod(n - ATT2, TT)
                if t == 1 and ahead(n - 1):
                    apply_roots(dve, BATCHES[1], h + 2)
                if h + 2 < HEADS and t == 2:
                    dve.wait_ge(heads_done, BATCHES[1]["first"] + h + 3)
                    dve.wait_ge(mla_roped, HEADS + h + 2)
                    nc.vector.stream_shuffle(value, k_head[h + 2][64:96], mask=MASK_SWAP).then_inc(partner_shuffled, 1)

            att_vector(dve, link, ATT2, ATT3, rotate_ahead)

            for s in range(ST):
                e_re, e_im = tab[:, 2 * (s % 2)], tab[:, 2 * (s % 2) + 1]
                in_re, in_im = bank[:, 2 * (s % 2)], bank[:, 2 * (s % 2) + 1]
                r0, r1, t0, t1 = s5r[:, 0], s5r[:, 1], s5t[:, 0], s5t[:, 1]
                dve.wait_ge(s5_in, s + 1)
                dve.wait_ge(s5_table, s + 1)
                link.mark(tt(r0, in_re, e_re, ALU.mult))
                real = link.mark(tt(t0, in_im, e_im, ALU.mult))
                link.mark(tt(r1, in_im, e_re, ALU.mult))
                imag = link.mark(tt(t1, in_re, e_im, ALU.mult))
                link.wait(real)
                real = link.mark(tt(r0, r0, t0, ALU.add))
                link.wait(imag)
                tt(r1, r1, t1, ALU.subtract).then_inc(s5_rotated, 1)
                decay_b = s5[:, 16 * MAG + s:16 * MAG + s + 1].to_broadcast([P, T])
                link.wait(real)
                link.mark(nc.vector.tensor_tensor_scan(t0, decay_b, r0, 0.0, ALU.mult, ALU.add))
                dve.wait_ge(s5_rotated, s + 1)
                scanned = link.mark(nc.vector.tensor_tensor_scan(t1, decay_b, r1, 0.0, ALU.mult, ALU.add))
                if s == 0:
                    dve.wait_ge(s5_c, 16)
                    c_re, c_im, minus, p0, p1 = (v.rearrange("p (a n) -> p a n", n=32) for v in (
                        cmat[:, 0], cmat[:, 1], cmat_minus[:, 0], gy[:, 0], gy[:, 1]))
                    f_re, f_im = (s5v(i).rearrange("p (a n) -> p a n", n=1).to_broadcast([P, ST, 32]) for i in (FRE, FIM))
                    link(tt(p0, c_im, f_im, ALU.mult))
                    link(tt(p1, c_im, f_re, ALU.mult))
                    link(tt(minus, c_re, f_re, ALU.mult))
                    link(tt(c_im, c_re, f_im, ALU.mult))
                    link(tt(c_re, minus, p0, ALU.subtract))
                    link(tt(c_im, c_im, p1, ALU.add))
                    link(ts(c_im, c_im, -1.0, None, ALU.mult))
                    link(ts(minus, c_re, -1.0, None, ALU.mult))
                if s:
                    dve.wait_ge(s5_out, s)
                link.wait(scanned)
                link.mark(tt(s5s[:, 0], t0, e_re, ALU.mult))
                link.mark(tt(s5s[:, 1], t1, e_im, ALU.mult))
                link.mark(tt(s5s[:, 2], t0, e_im, ALU.mult))
                tt(s5s[:, 3], t1, e_re, ALU.mult).then_inc(s5_states, 1)
                dve.wait_ge(s5_states, s + 1)
                if s % 4 == 3:
                    i = s // 4
                    dve.wait_ge(s5_out, s + 1)
                    stt(out=gy[:, i], in0=u_ssm[:, i], scalar=v_("ssm_d", i), in1=bank[:, 4 + i % 2],
                        op0=ALU.mult, op1=ALU.add).then_inc(s5_y, 1)
            for c in range(4):
                dve.wait_ge(glu_rounded, c + 1)
                tt(gy_low[:, c], gy[:, c], gy_high[:, c], ALU.subtract).then_inc(glu_low, 1)
            for c in range(4):
                dve.wait_ge(glu_sig, c + 1)
                tt(gprod[:, c % 2], gsig[:, c % 2], gy[:, c], ALU.mult).then_inc(glu_prod, 1)
                dve.wait_ge(y_rounded, 16 + c + 1)
                tt(y_low[:, 4 + c], gprod[:, c % 2], y_high[:, 4 + c], ALU.subtract).then_inc(y_split, 1)
            dve.wait_ge(y_split, 20)

            merge_vector("merge2", 3, 16)
            out_vector("out2", None)
            norm_vector(dve, link, NORM["n_ffn"])
            start = link.count
            with dve.Fori(0, 11) as i:
                link.count = start + i * 4
                for q in range(2):
                    hidden = bass.ds(i * 2 + q, 1)
                    for g, dst in ((0, ff_a), (1, ff_v)):
                        dve.wait_ge(up_centre, i * 4 + (2 * q + g + 1))
                        w0, w1 = (VECTOR_AT["conv_w"][0] + 44 * tap + 22 * g + q for tap in (0, 1))
                        link(stt(out=dst[:, q, 1:T], in0=bank[:, 2 * q + g, 0:T - 1], scalar=vec[:, bass.ds(i * 2 + w1, 1)],
                                 in1=dst[:, q, 1:T], op0=ALU.mult, op1=ALU.add))
                        stt(out=dst[:, q, 2:T], in0=bank[:, 2 * q + g, 0:T - 2], scalar=vec[:, bass.ds(i * 2 + w0, 1)],
                            in1=dst[:, q, 2:T], op0=ALU.mult, op1=ALU.add).then_inc(up_conv, 1)
                    dve.wait_ge(up_conv, i * 4 + (4 + 2 * q + 2))
                    dve.wait_ge(up_gate, i * 2 + (22 + q + 1))
                    tt(ff_p[:, q], ff_s[:, q], ff_v[:, q], ALU.mult).then_inc(up_prod, 1)
                    dve.wait_ge(up_rounded, i * 2 + (22 + q + 1))
                    tt(hid_low[:, hidden].rearrange("p a n -> p (a n)"), ff_p[:, q],
                       hid_high[:, hidden].rearrange("p a n -> p (a n)"), ALU.subtract).then_inc(up_low, 1)
            link.count = start + 44
            down_vector("down2", None)


INS = ["x", "c", "c_ctx", "ctx", "mem", "stream", "vectors", "ones", "identity", "one_column", "trig1", "bias", "hy_w3", "hy_z", "hy_w12", "decay",
       "dft1", "dft2", "cmask", "positions", "ssm_b", "ssm_c"]


def constants():
    out = {"ones": np.ones((P, P), np.float32), "identity": np.eye(P, dtype=np.float32)}
    out["one_column"] = np.tile((np.arange(31) == 15).astype(np.float32), (P, 1))
    t = np.arange(T)
    nf = HD // 4
    inv = 10000.0 ** (-np.arange(nf, dtype=np.float32) / nf)
    trig = np.zeros((P, 2, T), np.float32)
    for p in range(P):
        d = p % HD
        pos = (t // GRID_W if d < HD // 2 else t % GRID_W).astype(np.float32)
        ang = (pos * np.float32(inv[d % nf])).astype(np.float32).astype(np.float64)
        trig[p, 0] = np.cos(ang)
        trig[p, 1] = np.sin(ang) * (-1 if d % 32 < nf else 1)
    out["trig1"] = trig
    f32 = np.float32
    tl = np.linspace(0.0, 1.0, T, dtype=f32)
    w = (2.0 * math.pi * np.arange(T, dtype=f32) / T).astype(f32)
    bands = np.linspace(1e-4, (EMB - 1) // 2 - 1, (EMB - 1) // 2, dtype=f32)
    arg = (bands[:, None] * w[None, :]).astype(f32)
    out["hy_z"] = np.concatenate([tl[None], np.cos(arg), np.sin(-arg)], 0).astype(f32)
    deltas = np.abs(np.linspace(math.log(1e-2) / 1.5, math.log(1e-2) / 0.3, HYW, dtype=f32))
    out["decay"] = np.exp(-tl[:, None] * deltas[None, :]).astype(f32).reshape(TT, P, HYW).transpose(1, 0, 2).copy()
    n = np.arange(T, dtype=np.float64)
    for name, shift in (("dft1", 0.0), ("dft2", 0.5)):
        ang = 2 * math.pi * np.outer(n + shift, n + 0.5) / (2 * T)
        both = np.stack([np.cos(ang), np.sin(ang)]).astype(f32)
        out[name] = both.reshape(2, TT, P, T).transpose(2, 0, 1, 3).reshape(P, 8, T).copy()
    mask = np.zeros((P, T), f32)
    mask[:, T - P:] = np.where(np.arange(P)[None, :] <= np.arange(P)[:, None], 0.0, NEG)
    out["cmask"] = mask
    return out


def k_tiles(w, columns=P):
    k, n = w.shape
    return w.reshape(k // P, P, n).transpose(1, 0, 2)


def slots_by_tile(w):
    k, n = w.shape
    return w.reshape(k // P, P, n // P, P).transpose(2, 1, 0, 3).reshape(n // P, P, -1)


def slots_of(w, k_each, n_all):
    k, n = w.shape
    return w.reshape(k // P // k_each, k_each, P, n).transpose(0, 2, 1, 3).reshape(-1, P, k_each * n)


def slots_down(w):
    return np.concatenate([slots_of(np.ascontiguousarray(w[:, h * 512:h * 512 + 512]), 2, 512) for h in range(2)])


def slots_pairs(w1, w2):
    s1, s2 = slots_by_tile(w1), slots_by_tile(w2)
    return np.stack([s1, s2], 1).reshape(-1, P, SLOT)


def slots_merge(gates, outs):
    parts = []
    for g, o in zip(gates, outs):
        gs = slots_by_tile(g)
        os_ = slots_by_tile(o).reshape(4, 2, P, 512).transpose(0, 2, 1, 3).reshape(4, P, SLOT)
        for p in range(4):
            parts += [gs[2 * p:2 * p + 1], gs[2 * p + 1:2 * p + 2], os_[p:p + 1]]
    return np.concatenate(parts)


def padded(blocks, n=SLOT):
    out = np.zeros((1, P, n), blocks.dtype)
    out[0, :, :blocks.shape[1]] = blocks
    return out


def feature_columns(v):
    v = np.asarray(v).reshape(-1)
    if v.size % P:
        out = np.zeros((P, 1), np.float32)
        out[:v.size, 0] = v
        return out
    return v.reshape(-1, P).T


def lay_out(i):
    i = {k: np.asarray(v) for k, v in i.items()}
    d = constants()

    def tokens(v):
        return v[0].T.reshape(KD, P, -1).transpose(1, 0, 2).copy()

    d["x"], d["ctx"], d["mem"] = tokens(i["x"]), tokens(i["ctx"]), tokens(i["mem_2"])
    d["c"], d["c_ctx"] = i["c"].reshape(D), i["c_ctx"].reshape(D)
    d["positions"] = i["positions_2"].astype(np.int32).reshape(T)

    w_in = i["w_in"][0]
    part = lambda w, lo, n: np.ascontiguousarray(w[:, lo:lo + n])
    st = [np.ascontiguousarray(i["w_ada"][0].T).reshape(ADA_SLOTS, P, D), slots_by_tile(part(w_in, 0, 512)), slots_by_tile(part(w_in, 512, 512)),
          slots_of(part(w_in, 1024, 512), 2, 512), slots_by_tile(part(w_in, 1536, 1536)),
          slots_merge([part(w_in, 3072, 1024), part(w_in, 4096, 1024)], [i["w_na_o"][0], i["w_hy_o"][0]]),
          slots_by_tile(i["w_out"][0]), slots_pairs(i["ffn_w1"][0], i["ffn_w3"][0]), slots_down(i["ffn_w2"][0])]
    w_mem = i["w_mem_kv_2"][0]
    st += [slots_by_tile(part(w_mem, 0, 512)), slots_of(part(w_mem, 512, 512), 2, 512)]
    w2 = i["w_in_2"][0]
    kr = np.zeros((D, P), np.float32)
    kr[:, 64:96] = w2[:, QL + KVL:QL + KVL + DROPE]
    o = QL + KVL + DROPE
    st += [slots_by_tile(part(w2, 0, QL + KVL)), slots_by_tile(kr), slots_by_tile(part(w2, o + 512, 512)),
           slots_by_tile(part(w2, o, 512))]
    qb = k_tiles(i["w_q_b_2"][0]).reshape(P, 3, HEADS, DQK)
    for j in range(4):
        blocks = np.zeros((P, 2, 3, P), np.float32)
        blocks[:, :, :, :DQK] = qb[:, :, 2 * j:2 * j + 2].transpose(0, 2, 1, 3)
        st.append(padded(blocks.reshape(P, -1)))
    kvb = k_tiles(i["w_kv_b_2"][0]).reshape(P, 2, HEADS, 2, 64)
    st.append(kvb[:, :, :, 0].reshape(P, 2, 4, P).transpose(0, 2, 1, 3).reshape(1, P, SLOT))
    st.append(kvb[:, :, :, 1].reshape(1, P, SLOT))
    st.append(slots_by_tile(i["w_glu_2"][0]).reshape(2, 2, P, 512).transpose(0, 2, 1, 3).reshape(2, P, SLOT))
    gates = o + 1024
    st += [slots_merge([part(w2, gates + 1024 * b, 1024) for b in range(3)],
                       [i["w_o_mla_2"][0], i["w_o_ssm_2"][0], i["w_o_cross_2"][0]]),
           slots_by_tile(i["w_out_2"][0]), slots_pairs(part(i["w_up_2"][0], 0, FF), part(i["w_up_2"][0], FF, FF)),
           slots_down(i["w_down_2"][0])]
    d["stream"] = np.concatenate(st)
    assert d["stream"].shape == (ADA_SLOTS + NS, P, SLOT), d["stream"].shape

    rpb = i["na_rpb"][0]
    cq_ = np.arange(GRID_W)
    start = np.clip(cq_ - WIN_W // 2, 0, GRID_W - WIN_W)
    bias = np.full((HEADS, 2, GRID_W, TAPS, GRID_W), NEG, np.float32)
    for c in range(GRID_W):
        lo = start[c]
        for rr in range(2):
            rows = np.arange(TAPS) + 1 - rr
            bias[:, rr, c, :, lo:lo + WIN_W] = rpb[:, rows][:, :, lo - c + WIN_W - 1:lo - c + WIN_W - 1 + WIN_W]
    d["bias"] = bias.reshape(HEADS, P, TAPS * GRID_W)

    w3 = i["hy_ffn_w3"][0]
    d["hy_w3"] = w3.reshape(FW, 4, HYW).copy()
    w12 = np.zeros((FW, 2 * FW), np.float32)
    w12[:EMB, :FW] = i["hy_ffn_w1"][0]
    w12[:, FW:] = i["hy_ffn_w2"][0]
    d["hy_w12"] = w12

    b_all = np.zeros((2, ST, P, P), np.float32)
    c_all = np.zeros((P, 2, ST, 32), np.float32)
    for r, (bn, cn) in enumerate((("ssm_b_re_2", "ssm_c_re_2"), ("ssm_b_im_2", "ssm_c_im_2"))):
        bm, cm = i[bn][0], i[cn][0]
        for g in range(32):
            s, half, ch = g // 2, g % 2, (g % 8) * 16
            b_all[r, s, ch:ch + 16, half * 64:half * 64 + 64] = bm[g].T
            c_all[half * 64:half * 64 + 64, r, s, half * 16:half * 16 + 16] = cm[g].T
    d["ssm_b"] = b_all.reshape(2, 2, 8, P, P).transpose(1, 3, 0, 2, 4).reshape(2, P, 4, 512).copy()
    d["ssm_c"] = c_all.reshape(P, 2, ST * 32)

    sign = np.zeros(P, np.float32)
    sign[64:80], sign[80:96] = -1.0, 1.0
    freq = np.zeros(P, np.float32)
    inv = (np.float32(10000.0) ** (-np.arange(0, DROPE, 2, dtype=np.float32) / np.float32(DROPE))).astype(np.float32)
    freq[64:96] = np.tile(inv, 2)
    named = {
        "b_ada": i["b_ada"], "norm1": i["norm1_g"], "norm2": i["norm2_g"],
        "final": i["final_g"], "norm_mix": i["norm_mix_g_2"], "mem_norm": i["mem_norm_g_2"], "norm_ffn": i["norm_ffn_g_2"],
        "hy_conv_w": i["hy_conv_w"], "hy_conv_b": i["hy_conv_b"], "hy_bias": i["hy_bias"], "hy_b1": i["hy_ffn_b1"],
        "hy_b2": i["hy_ffn_b2"], "hy_freq": i["hy_sin_freq"], "conv_w": i["conv_w_2"], "conv_b": i["conv_b_2"],
        "b_gate": i["b_gate_2"], "b_glu": i["b_glu_2"], "q_a": i["q_a_norm_g_2"], "kv_a": i["kv_a_norm_g_2"],
        "q_norm": i["q_norm_g_2"], "k_norm": i["k_norm_g_2"], "xq": i["xq_norm_g_2"], "xk": i["xk_norm_g_2"],
        "lam_re": i["ssm_lambda_re_2"], "lam_im": i["ssm_lambda_im_2"],
        "log_dt": np.repeat(i["ssm_log_dt_2"].reshape(32, 1), NSTATE, 1), "ssm_d": i["ssm_d_2"],
        "inv_freq": freq, "rope_sign": sign, "zero": np.zeros(8 * P, np.float32), "eps": np.full(P, EPS, np.float32),
    }
    columns = [feature_columns(named[name]) for name, _ in VECTORS]
    assert [c.shape[1] for c in columns] == [n for _, n in VECTORS]
    d["vectors"] = np.concatenate(columns, 1).astype(np.float32, copy=False)
    return {k: np.ascontiguousarray(d[k]) for k in INS}


def kernel(**inputs):
    import concourse.bacc as bacc
    from concourse.bass_utils import run_bass_kernel_spmd

    arrays = lay_out(inputs)
    nc = bacc.Bacc("TRN2", target_bir_lowering=False, num_devices=1)
    aps = {k: nc.dram_tensor(f"in_{k}", v.shape, mybir.dt.from_np(v.dtype), kind="ExternalInput").ap()
           for k, v in arrays.items()}
    out = nc.dram_tensor("out_0", (KD, P, T), F32, kind="ExternalOutput").ap()
    build(nc, aps, out)
    r = run_bass_kernel_spmd(nc, [{f"in_{k}": v for k, v in arrays.items()}], core_ids=[0])
    y = r.results[0]["out_0"]
    return np.ascontiguousarray(y.reshape(D, T).T)[None]
```
